# Optimizing a Trainium2 kernel written in Bass

```python
import jax
import jax.numpy as jnp
from jax import lax
import numpy as np

D_MODEL = 1024
BATCH = 1
SEQ = 256
DEPTH = 2

GRID_W = 64
CTX_LEN = 256
CHUNK = 128
Q_BLOCK = 128
EPS = 1e-6
N_MOD = 6

SGU_HEADS = 4
SGU_HEAD_DIM = 64
SGU_WIDTH = SGU_HEADS * SGU_HEAD_DIM

SSD_HEADS = 6
SSD_HEAD_DIM = 64
SSD_WIDTH = SSD_HEADS * SSD_HEAD_DIM
SSD_GROUPS = 2
SSD_HPG = SSD_HEADS // SSD_GROUPS
SSD_STATE = 128
SSD_CONV = 5
SSD_BC = SSD_GROUPS * SSD_STATE
SSD_CONV_CH = SSD_WIDTH + 2 * SSD_BC

MLA_HEADS = 6
MLA_NOPE = 64
MLA_ROPE = 32
MLA_V = 64
MLA_WIDTH = MLA_HEADS * MLA_V
Q_LORA = 384
KV_LORA = 256
ROPE_THETA = 10000.0
MLA_SCALE = (MLA_NOPE + MLA_ROPE) ** -0.5

MIX_WIDTH = SGU_WIDTH + SSD_WIDTH + MLA_WIDTH
IN_SGU = 2 * SGU_WIDTH
IN_SSD = SSD_WIDTH + SSD_CONV_CH + 2 * SSD_HEADS
IN_MLA = Q_LORA + KV_LORA + MLA_ROPE
IN_WIDTH = IN_SGU + IN_SSD + IN_MLA

D_FF = 2816
N_EXPERTS = 8
TOP_K = 2
D_FF_EXPERT = 1408

kernel_name = "hybrid_sgu_ssd_mla_moe_dit"

def rmsnorm(x, g):
    xf = x.astype(jnp.float32)
    y = xf * lax.rsqrt(jnp.mean(xf * xf, axis=-1, keepdims=True) + EPS)
    return y.astype(x.dtype) * g

def layernorm(x, g, b):
    xf = x.astype(jnp.float32)
    mu = jnp.mean(xf, axis=-1, keepdims=True)
    xc = xf - mu
    y = xc * lax.rsqrt(jnp.mean(xc * xc, axis=-1, keepdims=True) + EPS)
    return y.astype(x.dtype) * g + b

def modulate(x, g, shift, scale):
    return rmsnorm(x, g) * (1 + scale) + shift

def axial_rope_tables(n_tokens):
    grid_rows = n_tokens // GRID_W
    row = jnp.repeat(jnp.arange(grid_rows, dtype=jnp.float32), GRID_W)
    col = jnp.tile(jnp.arange(GRID_W, dtype=jnp.float32), grid_rows)
    n_freq = MLA_ROPE // 4
    inv_freq = ROPE_THETA ** (-jnp.arange(n_freq, dtype=jnp.float32) / n_freq)
    ang = jnp.stack([row[:, None] * inv_freq, col[:, None] * inv_freq], axis=1)
    return jnp.cos(ang), jnp.sin(ang)

def apply_axial_rope(t, cos, sin):
    shp = t.shape
    t = t.reshape(shp[:-1] + (2, 2, MLA_ROPE // 4))
    t1, t2 = t[..., 0, :], t[..., 1, :]
    cos = cos.astype(t.dtype)
    sin = sin.astype(t.dtype)
    out = jnp.stack([t1 * cos - t2 * sin, t1 * sin + t2 * cos], axis=-2)
    return out.reshape(shp)

def sgu_mixer(p, w_s, b_s, g_n, beta_n):
    bsz, n, _ = p.shape
    u, v = jnp.split(jax.nn.gelu(p), 2, axis=-1)
    v = layernorm(v, g_n, beta_n).reshape(bsz, n // CHUNK, CHUNK, SGU_HEADS, SGU_HEAD_DIM)
    mixed = jnp.einsum('hts,bcshd->bcthd', w_s, v) + b_s.T[:, :, None]
    return u * mixed.reshape(bsz, n, SGU_WIDTH)

def depthwise_conv(x, w, b):
    pad = SSD_CONV // 2
    y = lax.conv_general_dilated(x, w[:, None, :], window_strides=(1,), padding=[(pad, pad)],
                                 dimension_numbers=('NWC', 'WIO', 'NWC'), feature_group_count=x.shape[-1])
    return y + b

def ssd_streams(p, conv_w, conv_b, dt_bias):
    bsz, n, _ = p.shape
    z = p[..., :SSD_WIDTH]
    xbc = jax.nn.silu(depthwise_conv(p[..., SSD_WIDTH:SSD_WIDTH + SSD_CONV_CH], conv_w, conv_b))
    dt = jax.nn.softplus(p[..., SSD_WIDTH + SSD_CONV_CH:] + dt_bias.reshape(-1))
    xs = xbc[..., :SSD_WIDTH].reshape(bsz, n, SSD_GROUPS, SSD_HPG, SSD_HEAD_DIM)
    bm = xbc[..., SSD_WIDTH:SSD_WIDTH + SSD_BC].reshape(bsz, n, SSD_GROUPS, SSD_STATE)
    cm = xbc[..., SSD_WIDTH + SSD_BC:].reshape(bsz, n, SSD_GROUPS, SSD_STATE)
    dt = dt.reshape(bsz, n, 2, SSD_GROUPS, SSD_HPG)
    return z, xs, bm, cm, dt

def ssd_final_state(x, dt, a, bm):
    acs = jnp.cumsum(dt.astype(jnp.float32) * a, axis=1)
    w = jnp.exp(acs[:, -1:] - acs).astype(x.dtype) * dt
    return jnp.einsum('blgn,blgj,blgjp->bgjpn', bm, w, x)

def ssd_chunked(x, dt, a, bm, cm, h0):
    bsz, n, g, j, p = x.shape
    nc = n // CHUNK
    xc = x.reshape(bsz, nc, CHUNK, g, j, p)
    dtc = dt.reshape(bsz, nc, CHUNK, g, j)
    bc = bm.reshape(bsz, nc, CHUNK, g, SSD_STATE)
    cc = cm.reshape(bsz, nc, CHUNK, g, SSD_STATE)
    acs = jnp.cumsum(dtc.astype(jnp.float32) * a, axis=2)
    xdt = xc * dtc[..., None]
    seg = acs[:, :, :, None] - acs[:, :, None, :]
    lower = jnp.tril(jnp.ones((CHUNK, CHUNK), dtype=bool))[:, :, None, None]
    decay = jnp.exp(jnp.where(lower, seg, -jnp.inf)).astype(x.dtype)
    cb = jnp.einsum('bclgn,bcsgn->bclsg', cc, bc)
    y_diag = jnp.einsum('bclsgj,bcsgjp->bclgjp', cb[..., None] * decay, xdt)
    to_end = jnp.exp(acs[:, :, -1:] - acs).astype(x.dtype)
    states = jnp.einsum('bcsgn,bcsgj,bcsgjp->bcgjpn', bc, to_end, xdt)
    chunk_decay = jnp.exp(acs[:, :, -1]).astype(x.dtype)

    def carry_step(h, inp):
        dec, st = inp
        return dec[..., None, None] * h + st, h

    _, h_in = lax.scan(carry_step, h0, (jnp.moveaxis(chunk_decay, 1, 0), jnp.moveaxis(states, 1, 0)))
    h_in = jnp.moveaxis(h_in, 0, 1)
    y_off = jnp.einsum('bclgn,bcgjpn,bclgj->bclgjp', cc, h_in, jnp.exp(acs).astype(x.dtype))
    return (y_diag + y_off).reshape(bsz, n, g, j, p)

def ssd_mixer(p, pc, conv_w, conv_b, dt_bias, a_log, d_skip, g_ssd, need_ctx):
    z, xs, bm, cm, dt = ssd_streams(p, conv_w, conv_b, dt_bias)
    zc, xsc, bmc, cmc, dtc = ssd_streams(pc, conv_w, conv_b, dt_bias)
    a = -jnp.exp(a_log.astype(jnp.float32)).reshape(2, SSD_GROUPS, SSD_HPG)
    skip = d_skip.reshape(SSD_GROUPS, SSD_HPG, 1)
    bsz, n = xs.shape[:2]
    y = skip * xs
    yc = skip * xsc
    for direction in range(2):
        order = (lambda t: t) if direction == 0 else (lambda t: jnp.flip(t, axis=1))
        h_ctx = ssd_final_state(order(xsc), order(dtc[:, :, direction]), a[direction], order(bmc))
        y = y + order(ssd_chunked(order(xs), order(dt[:, :, direction]), a[direction],
                                  order(bm), order(cm), h_ctx))
        if need_ctx:
            yc = yc + order(ssd_chunked(order(xsc), order(dtc[:, :, direction]), a[direction],
                                        order(bmc), order(cmc), jnp.zeros_like(h_ctx)))
    out = rmsnorm(y.reshape(bsz, n, SSD_WIDTH) * jax.nn.silu(z), g_ssd)
    if not need_ctx:
        return out, None
    outc = rmsnorm(yc.reshape(bsz, pc.shape[1], SSD_WIDTH) * jax.nn.silu(zc), g_ssd)
    return out, outc

def mla_queries(p, g_q, w_uq):
    bsz, n, _ = p.shape
    q = (rmsnorm(p[..., :Q_LORA], g_q) @ w_uq).reshape(bsz, n, MLA_HEADS, MLA_NOPE + MLA_ROPE)
    return q[..., :MLA_NOPE], q[..., MLA_NOPE:]

def mla_keys_values(p, g_kv, w_ukv):
    bsz, n, _ = p.shape
    kv = (rmsnorm(p[..., Q_LORA:Q_LORA + KV_LORA], g_kv) @ w_ukv).reshape(bsz, n, MLA_HEADS, MLA_NOPE + MLA_V)
    k_rope = p[..., Q_LORA + KV_LORA:]
    return kv[..., :MLA_NOPE], k_rope, kv[..., MLA_NOPE:]

def mla_attend(qn, qr, kn, kr, v):
    s = jnp.einsum('bqhd,bkhd->bhqk', qn, kn) + jnp.einsum('bqhr,bkr->bhqk', qr, kr)
    prob = jax.nn.softmax(s.astype(jnp.float32) * MLA_SCALE, axis=-1).astype(v.dtype)
    return jnp.einsum('bhqk,bkhd->bqhd', prob, v)

def mla_mixer(p, pc, g_q, w_uq, g_kv, w_ukv, cos, sin, need_ctx):
    bsz, n, _ = p.shape
    qn, qr = mla_queries(p, g_q, w_uq)
    qr = apply_axial_rope(qr, cos[:, None], sin[:, None])
    kn, kr, v = mla_keys_values(p, g_kv, w_ukv)
    kr = apply_axial_rope(kr, cos, sin)
    knc, krc, vc = mla_keys_values(pc, g_kv, w_ukv)
    kn_all = jnp.concatenate([knc, kn], axis=1)
    kr_all = jnp.concatenate([krc, kr], axis=1)
    v_all = jnp.concatenate([vc, v], axis=1)
    n_blk = n // Q_BLOCK

    def to_blocks(t):
        return jnp.moveaxis(t.reshape((bsz, n_blk, Q_BLOCK) + t.shape[2:]), 1, 0)

    o = lax.map(lambda qb: mla_attend(qb[0], qb[1], kn_all, kr_all, v_all), (to_blocks(qn), to_blocks(qr)))
    o = jnp.moveaxis(o, 0, 1).reshape(bsz, n, MLA_WIDTH)
    if not need_ctx:
        return o, None
    qnc, qrc = mla_queries(pc, g_q, w_uq)
    oc = mla_attend(qnc, qrc, knc, krc, vc).reshape(bsz, pc.shape[1], MLA_WIDTH)
    return o, oc

def swiglu(h, wg, wu, wd):
    return (jax.nn.silu(h @ wg) * (h @ wu)) @ wd

def moe_ffn(h, w_router, wg, wu, wd):
    logits = (h @ w_router).astype(jnp.float32)
    top_logit, top_idx = lax.top_k(logits, TOP_K)
    top_w = jax.nn.softmax(top_logit, axis=-1).astype(h.dtype)
    out = jnp.zeros_like(h)
    for e in range(N_EXPERTS):
        gate_e = jnp.sum(jnp.where(top_idx == e, top_w, 0), axis=-1, keepdims=True)
        out = out + gate_e * swiglu(h, wg[e], wu[e], wd[e])
    return out

def setup_inputs(seed: int = 0) -> dict:
    key = jax.random.key(seed)
    ks = iter(jax.random.split(key, 40))
    L = DEPTH
    n_dense = (DEPTH + 1) // 2
    n_moe = DEPTH // 2

    def nrm(shape, scale):
        return jax.random.normal(next(ks), shape, jnp.float32) * scale

    def gain(shape):
        return 1.0 + nrm(shape, 0.02)

    x = nrm((BATCH, SEQ, D_MODEL), 1.0)
    c = nrm((BATCH, D_MODEL), 1.0)
    ctx = nrm((BATCH, CTX_LEN, D_MODEL), 1.0)
    c_ctx = nrm((D_MODEL,), 1.0)
    w_mod = nrm((L, D_MODEL, N_MOD * D_MODEL), 0.5 * D_MODEL ** -0.5)
    b_mod = nrm((L, N_MOD * D_MODEL), 0.02)
    g_mix = gain((L, D_MODEL))
    w_in = nrm((L, D_MODEL, IN_WIDTH), D_MODEL ** -0.5)
    w_sgu = nrm((L, SGU_HEADS, CHUNK, CHUNK), CHUNK ** -0.5)
    b_sgu = nrm((L, SGU_HEADS, CHUNK), 0.02)
    g_sgu = gain((L, SGU_WIDTH))
    beta_sgu = nrm((L, SGU_WIDTH), 0.02)
    conv_w = nrm((L, SSD_CONV, SSD_CONV_CH), SSD_CONV ** -0.5)
    conv_b = nrm((L, SSD_CONV_CH), 0.02)
    dt0 = jnp.exp(jax.random.uniform(next(ks), (L, 2, SSD_HEADS), jnp.float32, np.log(1e-3), np.log(1e-1)))
    dt_bias = dt0 + jnp.log(-jnp.expm1(-dt0))
    a_log = jnp.log(jax.random.uniform(next(ks), (L, 2, SSD_HEADS), jnp.float32, 1.0, 16.0))
    d_skip = gain((L, SSD_HEADS))
    g_ssd = gain((L, SSD_WIDTH))
    g_q = gain((L, Q_LORA))
    w_uq = nrm((L, Q_LORA, MLA_HEADS * (MLA_NOPE + MLA_ROPE)), Q_LORA ** -0.5)
    g_kv = gain((L, KV_LORA))
    w_ukv = nrm((L, KV_LORA, MLA_HEADS * (MLA_NOPE + MLA_V)), KV_LORA ** -0.5)
    w_out = nrm((L, MIX_WIDTH, D_MODEL), MIX_WIDTH ** -0.5)
    g_ffn = gain((L, D_MODEL))
    w_gate = nrm((n_dense, D_MODEL, D_FF), D_MODEL ** -0.5)
    w_up = nrm((n_dense, D_MODEL, D_FF), D_MODEL ** -0.5)
    w_down = nrm((n_dense, D_FF, D_MODEL), D_FF ** -0.5)
    w_router = nrm((n_moe, D_MODEL, N_EXPERTS), D_MODEL ** -0.5)
    w_gate_e = nrm((n_moe, N_EXPERTS, D_MODEL, D_FF_EXPERT), D_MODEL ** -0.5)
    w_up_e = nrm((n_moe, N_EXPERTS, D_MODEL, D_FF_EXPERT), D_MODEL ** -0.5)
    w_down_e = nrm((n_moe, N_EXPERTS, D_FF_EXPERT, D_MODEL), D_FF_EXPERT ** -0.5)
    g_final = gain((D_MODEL,))
    return {"x": x, "c": c, "ctx": ctx, "c_ctx": c_ctx, "w_mod": w_mod, "b_mod": b_mod, "g_mix": g_mix,
            "w_in": w_in, "w_sgu": w_sgu, "b_sgu": b_sgu, "g_sgu": g_sgu, "beta_sgu": beta_sgu,
            "conv_w": conv_w, "conv_b": conv_b, "dt_bias": dt_bias, "a_log": a_log, "d_skip": d_skip,
            "g_ssd": g_ssd, "g_q": g_q, "w_uq": w_uq, "g_kv": g_kv, "w_ukv": w_ukv, "w_out": w_out,
            "g_ffn": g_ffn, "w_gate": w_gate, "w_up": w_up, "w_down": w_down, "w_router": w_router,
            "w_gate_e": w_gate_e, "w_up_e": w_up_e, "w_down_e": w_down_e, "g_final": g_final}

def reference(x, c, ctx, c_ctx, w_mod, b_mod, g_mix, w_in, w_sgu, b_sgu, g_sgu, beta_sgu, conv_w, conv_b,
              dt_bias, a_log, d_skip, g_ssd, g_q, w_uq, g_kv, w_ukv, w_out, g_ffn, w_gate, w_up, w_down,
              w_router, w_gate_e, w_up_e, w_down_e, g_final):
    bsz, n, d = x.shape
    cos, sin = axial_rope_tables(n)
    cond = jax.nn.silu(c)
    cond_ctx = jax.nn.silu(c_ctx)
    xc = ctx
    for layer in range(DEPTH):
        need_ctx = layer < DEPTH - 1
        mod = (cond @ w_mod[layer] + b_mod[layer]).reshape(bsz, 1, N_MOD, d)
        modc = (cond_ctx @ w_mod[layer] + b_mod[layer]).reshape(N_MOD, d)
        h = modulate(x, g_mix[layer], mod[:, :, 0], mod[:, :, 1])
        hc = modulate(xc, g_mix[layer], modc[0], modc[1])
        p = h @ w_in[layer]
        pc = hc @ w_in[layer]
        s0, s1 = IN_SGU, IN_SGU + IN_SSD
        o_sgu = sgu_mixer(p[..., :s0], w_sgu[layer], b_sgu[layer], g_sgu[layer], beta_sgu[layer])
        o_ssd, oc_ssd = ssd_mixer(p[..., s0:s1], pc[..., s0:s1], conv_w[layer], conv_b[layer], dt_bias[layer],
                                  a_log[layer], d_skip[layer], g_ssd[layer], need_ctx)
        o_mla, oc_mla = mla_mixer(p[..., s1:], pc[..., s1:], g_q[layer], w_uq[layer], g_kv[layer],
                                  w_ukv[layer], cos, sin, need_ctx)
        x = x + mod[:, :, 2] * (jnp.concatenate([o_sgu, o_ssd, o_mla], axis=-1) @ w_out[layer])
        if need_ctx:
            oc_sgu = sgu_mixer(pc[..., :s0], w_sgu[layer], b_sgu[layer], g_sgu[layer], beta_sgu[layer])
            xc = xc + modc[2] * (jnp.concatenate([oc_sgu, oc_ssd, oc_mla], axis=-1) @ w_out[layer])
        if layer % 2 == 0:
            i = layer // 2
            ffn = lambda t: swiglu(t, w_gate[i], w_up[i], w_down[i])
        else:
            i = layer // 2
            ffn = lambda t: moe_ffn(t, w_router[i], w_gate_e[i], w_up_e[i], w_down_e[i])
        x = x + mod[:, :, 5] * ffn(modulate(x, g_ffn[layer], mod[:, :, 3], mod[:, :, 4]))
        if need_ctx:
            xc = xc + modc[5] * ffn(modulate(xc, g_ffn[layer], modc[3], modc[4]))
    return rmsnorm(x, g_final)


_drawn_inputs = setup_inputs


def setup_inputs(seed=0):
    import zlib

    import numpy as np

    out = dict(_drawn_inputs(seed))
    spreads = {}
    factors = {'g_mix': 5.993,
     'b_sgu': 8.0,
     'g_sgu': 8.0,
     'beta_sgu': 8.0,
     'conv_b': 7.666,
     'd_skip': 64.0,
     'g_ssd': 25.966,
     'g_q': 8.0,
     'g_kv': 8.0,
     'g_ffn': 3.601,
     'g_final': 8.197}
    for name, (base, spread) in spreads.items():
        noise = np.random.default_rng([zlib.crc32(name.encode()), seed]).standard_normal(out[name].shape)
        drawn = base * np.exp(spread * noise) if base else spread * noise
        out[name] = jnp.asarray(drawn.astype(out[name].dtype))
    for name, factor in factors.items():
        out[name] = (out[name] * factor).astype(out[name].dtype)
    return out
```

```python
from contextlib import ExitStack

import numpy as np

import concourse.bass as bass
from concourse import mybir

F32 = mybir.dt.float32
F32R = mybir.dt.float32r
ALU = mybir.AluOpType
ACT = mybir.ActivationFunctionType
AX = mybir.AxisListType

P = 128
L = 2
D = 1024
KD = D // P
CTX, SEQ = 256, 256
NT = (CTX + SEQ) // P
TOK = NT * P
EPS = 1e-6

SGU_H, SGU_W = 4, 256
SSD_H, SSD_HD, SSD_W, HPG = 6, 64, 384, 3
STATE = 128
TAPS = 5
XBC = SSD_W + 4 * STATE
KX = XBC // P
MLA_H, NOPE, ROPE, MLA_V = 6, 64, 32, 64
QK = NOPE + ROPE
Q_LORA, KV_LORA = 384, 256
SCALE = QK ** -0.5
IN_SGU = 2 * SGU_W
GRID_W = 64
THETA = 10000.0

D_FF = 2816
KF = D_FF // P
NE = 8
D_FFE = 1408
KE = D_FFE // P

C_DT, C_KR, C_KV, C_Q, C_Z, C_U, C_V, C_END = 0, 12, 44, 300, 684, 1068, 1324, 1580
CHUNKS = [(0, 150), (150, 300), (300, 556), (556, 684), (684, 876), (876, 1068), (1068, 1324), (1324, 1580)]
CTX_CHUNKS = 2

R = 3
SLOT = 2048
W_SPLIT = 3
MODS = 6
MOD_TILES = MODS * KD
MOD_LOADS = MOD_TILES // 2
GU_LOADS = KF
DN_LOADS = 2 * KD
ME_GU, ME_DN = KE, 7
ME_LOADS = ME_GU + ME_DN
DN_PARTS = [(2 * i, 2, 0, KD) for i in range(5)] + [(10, 1, 0, KD // 2), (10, 1, KD // 2, KD // 2)]

T0 = [0, CTX // P]
CHAIN = [[0, 1, 2, 3], [1, 0, 3, 2]]


def const_array():
    i = np.arange(P)
    ident = np.eye(P)
    ones = np.ones((P, P))
    upto = (i[:, None] <= i[None, :]).astype(np.float64)
    sel = np.zeros((P, SSD_H, P))
    for h in range(SSD_H):
        sel[h, h, :] = 1.0
    n_freq = ROPE // 4
    inv = THETA ** (-np.arange(n_freq, dtype=np.float32) / np.float32(n_freq))
    tok = np.arange(SEQ)
    ang = np.stack([(tok // GRID_W)[:, None] * inv, (tok % GRID_W)[:, None] * inv], axis=1).astype(np.float32)
    rope = np.stack([np.cos(ang), np.sin(ang)], axis=1).reshape(SEQ // P, P, 2 * 2 * n_freq)
    rope = rope.transpose(1, 0, 2).reshape(P, -1)
    first = np.broadcast_to(NE - np.arange(NE), (P, NE))
    fold = np.stack([(i % 32 == k) for k in range(2)], axis=1)
    parts = [ident, ones, upto, upto.T, sel.reshape(P, -1), rope, first, fold]
    return np.concatenate([np.asarray(a, np.float32) for a in parts], axis=1)


N_CONST = 4 * P + SSD_H * P + 64 + NE + 2

COLS = {}
_at = 0
for _name, _n in (("conv_w", KX * TAPS), ("conv_b", KX), ("b_mod", MOD_TILES), ("g_mix", KD), ("g_ffn", KD), ("b_sgu", SGU_H),
                  ("g_ssd", 3), ("g_q", 3), ("g_kv", 2)):
    COLS[_name] = (_at, _n)
    _at += _n
N_COL = _at
ROWS = {"dt_bias": (0, 12), "a_log": (12, 12), "d_skip": (24, 6), "g_sgu": (30, 256), "beta_sgu": (286, 256)}
N_ROW = 542


class Bank:

    def __init__(self, tile, full, free):
        self.tile, self.full, self.free = tile, full, free
        self.order, self.fulls, self.reads = {}, [0], [0]

    def add(self, name, reads=1, fulls=1):
        assert name not in self.order, name
        self.order[name] = len(self.reads)
        self.reads.append(self.reads[-1] + reads)
        self.fulls.append(self.fulls[-1] + fulls)

    def filled(self, name):
        return self.fulls[self.order[name]]

    def taken(self, name):
        return self.reads[self.order[name]]

    def before(self, name):
        return self.reads[self.order[name] - 1]


def program(nc, t):
    ctx = ExitStack()
    with ctx:
        def sb(name, n, p=P, dt=F32):
            return ctx.enter_context(nc.sbuf_tensor(name, [p, n], dt))

        def sem(name):
            return ctx.enter_context(nc.semaphore(name))

        const = sb("const", N_CONST)
        colp = sb("colp", L * N_COL)
        rowp = sb("rowp", L * N_ROW)
        wsT = sb("wsT", L * SGU_H * P)
        gfin = sb("gfin", KD)
        rtr = sb("rtr", KD * NE)
        acs_s = sb("acs_s", 96)
        condr = sb("condr", KD * 2)
        condp = sb("condp", KD * 32)
        ea = sb("ea", L * 12)
        mods = sb("mods", L * MOD_TILES * 2)
        amod = sb("amod", L * 2 * KD * 2)
        X = sb("X", KD * TOK)
        ring = sb("ring", R * SLOT)
        nv = sb("nv", TOK)
        ns = sb("ns", TOK)
        rstd = sb("rstd", TOK)
        mrow = [nv[:, 0:2 * P], nv[:, 2 * P:4 * P], ns[:, 0:2 * P]]
        pair = sb("pair", 2 * TOK)
        pair2 = sb("pair2", 2 * TOK)
        stats = sb("stats", 12)
        sv = sb("sv", 12)
        ssq = sb("ssq", 12)
        rs = sb("rs", 12)
        bn = sb("bn", 4 * 8)
        small = sb("small", 12 * 48)
        sst = sb("sst", 16)
        mx = sb("mx", 4)
        rsum = sb("rsum", NT * MLA_H)
        rinv = sb("rinv", NT * MLA_H)
        WORK = 23600
        with ExitStack() as mixer:
            H = mixer.enter_context(nc.sbuf_tensor("H", [P, KD * TOK], F32))
            ptok = mixer.enter_context(nc.sbuf_tensor("ptok", [P, NT * C_END], F32))
            work = mixer.enter_context(nc.sbuf_tensor("work", [P, WORK], F32))

        def view(at, n):
            assert at[0] + n <= WORK, (at[0], n)
            v = work[:, at[0]:at[0] + n]
            at[0] += n
            return v

        at = [0]
        xp = [view(at, 2 * (CTX + 4)).rearrange("p (s n) -> p s n", s=2) for _ in range(2)]
        cacc = [view(at, TOK) for _ in range(2)]
        xbcT = view(at, KX * TOK).rearrange("p (c n) -> p c n", c=KX)
        xsB = view(at, NT * 640).rearrange("p (t n) -> p t n", t=NT)
        acsT = view(at, 2 * TOK).rearrange("p (r n) -> p r n", r=2)
        cbm = view(at, 4 * TOK).rearrange("p (r g n) -> p r g n", r=2, g=2)
        seg = [view(at, TOK) for _ in range(2)]
        Ex = [view(at, TOK) for _ in range(2)]
        Mt = [view(at, TOK) for _ in range(2)]
        xdt = view(at, 2 * NT * SSD_W).rearrange("p (r t n) -> p r t n", r=2, t=NT)
        wx = view(at, 2 * NT * SSD_W).rearrange("p (r t n) -> p r t n", r=2, t=NT)
        hin = view(at, 2 * 3 * SSD_W).rearrange("p (r i n) -> p r i n", r=2, i=3)
        ytmp = view(at, SSD_W)
        ysum = view(at, SSD_W)
        at = [0]
        qlT = view(at, 3 * TOK).rearrange("p (c n) -> p c n", c=3)
        kvT = view(at, 2 * TOK).rearrange("p (c n) -> p c n", c=2)
        qtk = [view(at, MLA_H * QK) for _ in range(2)]
        krp = view(at, NT * QK).rearrange("p (t n) -> p t n", t=NT)
        rtmp = view(at, 4 * MLA_H * ROPE // 2)
        qT = view(at, MLA_H * TOK).rearrange("p (h n) -> p h n", h=MLA_H)
        kT = view(at, MLA_H * TOK).rearrange("p (h n) -> p h n", h=MLA_H)
        vt = view(at, NT * SSD_W).rearrange("p (t n) -> p t n", t=NT)
        pr = [view(at, TOK) for _ in range(2)]
        pT = [view(at, TOK) for _ in range(2)]
        at = [0]
        act = view(at, KF * TOK)
        sg = [view(at, TOK) for _ in range(3)]

        me_h = [sb(f"me_h_{part}", KD * SEQ, dt=F32R)[:, :].rearrange("p (c n) -> p c n", c=KD) for part in ("hi", "lo")]
        me_raw = sb("me_raw", KD * SEQ)[:, :].rearrange("p (c n) -> p c n", c=KD)
        me_act = [sb(f"me_act_{part}", KE * SEQ, dt=F32R) for part in ("hi", "lo")]
        me_w = [sb(f"me_w_{part}", W_SPLIT * SLOT, dt=F32R) for part in ("hi", "lo")]
        me_sg = [sb(f"me_sg{b}", SEQ) for b in range(3)]
        me_up = [sb(f"me_up{b}", SEQ) for b in range(3)]
        me_prod = [sb(f"me_prod{b}", SEQ) for b in range(3)]
        zeros = sb("zeros", TOK)
        gateb = sb("gateb", NE * SEQ)
        grep = sb("grep", 2 * P)
        lg = sb("lg", 256)

        Xv = X[:, :].rearrange("p (c n) -> p c n", c=KD)
        Hv = H[:, :].rearrange("p (c n) -> p c n", c=KD)
        pt = ptok[:, :].rearrange("p (t n) -> p t n", t=NT)
        ident = const[:, 0:P]
        ones = const[:, P:2 * P]
        upto = const[:, 2 * P:3 * P]
        down = const[:, 3 * P:4 * P]
        sel = const[:, 4 * P:4 * P + SSD_H * P]
        rope0 = 4 * P + SSD_H * P
        first = const[:, rope0 + 64:rope0 + 64 + NE]
        fold = const[:, rope0 + 64 + NE:rope0 + 66 + NE]
        modv = mods[:, :].rearrange("p (l m c k) -> p l m c k", l=L, m=MODS, c=KD)
        amv = amod[:, :].rearrange("p (l w c k) -> p l w c k", l=L, w=2, c=KD)

        def col(l, name):
            a, n = COLS[name]
            return colp[:, l * N_COL + a:l * N_COL + a + n]

        def row(l, name):
            a, n = ROWS[name]
            return rowp[:, l * N_ROW + a:l * N_ROW + a + n]

        def wslot(n):
            return ring[:, (n % R) * SLOT:(n % R + 1) * SLOT]

        load_of = {}

        def plan(name):
            load_of[name] = len(load_of)

        for n in range(MOD_LOADS):
            plan(f"mod0.{n}")
        for l in range(L):
            for n in range(4):
                plan(f"xbc{l}.{n}")
            for n in range(len(CHUNKS)):
                plan(f"tok{l}.{n}")
            plan(f"ukv{l}")
            plan(f"uq{l}")
            for n in range(4):
                plan(f"wo{l}.{n}")
            if l == 0:
                for n in range(MOD_LOADS):
                    if n < GU_LOADS:
                        plan(f"gu.{n}")
                    plan(f"mod1.{n}")
                for n in range(DN_LOADS):
                    plan(f"dn.{n}")
            else:
                for n in range(NE * ME_LOADS):
                    plan(f"me.{n}")
        XL = [(0, 1), (2, 3), (4, 5), (6,)]

        def load_size(k):
            k %= ME_LOADS
            if k < ME_GU:
                return SLOT
            _, nf, _, nj = DN_PARTS[k - ME_GU]
            return nf * nj * P

        w_full = [sem(f"w_full{s}") for s in range(R)]
        w_begun = sem("w_begun")

        def w_wait(pe, n):
            pe.wait_ge(w_full[n % R], 16 * (n // R + 1))

        B = []
        for b in range(8):
            tile = ctx.enter_context(nc.psum_tensor(f"bank{b}", [P, 512], F32))
            B.append(Bank(tile, sem(f"bank{b}_full"), sem(f"bank{b}_free")))
        use = {}

        def uses(b, name, reads=1, fulls=1):
            B[b].add(name, reads, fulls)
            use[name] = B[b]

        for n in range(MOD_LOADS):
            uses(n % R, f"mrow0.{n}")
        uses(7, "mod0", fulls=MOD_LOADS // R)
        tiles = [range(T0[l], NT) for l in range(L)]
        for l in range(L):
            T = tiles[l]
            both = 2 if l == 0 else 1
            uses(0, f"norm{2 * l}", fulls=0)
            for c in range(KX):
                uses(1 + c % 2, f"xbc{l}.{c}")
            for q in range(len(CHUNKS)):
                for i in (range(NT) if q < CTX_CHUNKS else T):
                    uses(3 + i, f"tok{l}.{q}.{i}")
            for i in range(NT):
                uses(1, f"xsT{l}.{i}")
                uses(2, f"BT{l}.{i}")
            uses(7, f"acs{l}")
            uses(3, f"rows{l}.0")
            uses(4, f"rows{l}.1")
            uses(5, f"cb{l}.0", 2)
            uses(6, f"cb{l}.1", 2)
            for r in range(2):
                for i in range(3):
                    uses(7 if r == 0 else 0, f"st{l}.{r}.{i}")
            for k in range(12):
                uses(1 + k % 2, f"bc{l}.{k}")
            for i in T:
                uses(3 + i, f"y{l}.{i}")
            for i in T:
                for r in range(2):
                    if CHAIN[r].index(i):
                        uses(1 + r, f"off{l}.{i}.{r}")
            for c in range(3):
                uses(c, f"qlT{l}.{c}")
            for c in range(2):
                uses(3 + c, f"kvT{l}.{c}")
            for h in range(MLA_H):
                uses(5 + h % 2, f"kn{l}.{h}")
            for i in range(NT):
                uses(1 + i % 2, f"v{l}.{i}")
            uses(3, f"kr{l}")
            for i in T:
                for hh in range(2):
                    uses(4 + hh, f"q{l}.{i}.{hh}")
                for hh in range(2):
                    uses(6 + hh, f"qT{l}.{i}.{hh}")
            for i in T:
                for h in range(MLA_H):
                    uses(h % 2, f"s{l}.{i}.{h}")
                    uses(2 + h % 2, f"pT{l}.{i}.{h}")
                uses(4 + i % 2, f"o{l}.{i}")
            for i in T:
                uses(6 + i % 2, f"sgu{l}.{i}", SGU_H)
            for i in T:
                uses(0, f"oT{l}.{i}.0", 2)
                uses(1, f"oT{l}.{i}.1", 3)
            for j in range(KD):
                uses(2 + j % 2, f"wo{l}.{j}", both)
            uses(0, f"norm{2 * l + 1}", fulls=0)
            if l == 0:
                for i in range(KF):
                    uses(i % 3, f"gate.{i}")
                    uses(3 + i % 3, f"up.{i}", 0)
                for n in range(MOD_LOADS):
                    uses(6, f"mrow1.{n}")
                uses(7, "mod1")
                for j in range(KD):
                    uses(6 + j % 2, f"dn.{j}", both)
            else:
                uses(0, "logits")
                for e in range(NE):
                    uses(1 + e % 2, f"gb.{e}")
                for b in range(4, 8):
                    uses(b, f"moe.{b}", 2, fulls=0 if b == 4 else 1)
                for e in range(NE):
                    for i in range(KE):
                        uses(i % 3, f"meg.{e}.{i}")
        uses(0, "norm4", fulls=0)

        def claim(pe, name):
            if use[name].before(name):
                pe.wait_ge(use[name].free, use[name].before(name))

        def full(eng, name):
            eng.wait_ge(use[name].full, use[name].filled(name))

        def taken(eng, name):
            eng.wait_ge(use[name].free, use[name].taken(name))

        s_par = sem("s_par")
        s_x = sem("s_x")
        s_out = sem("s_out")
        cond_ready = sem("cond_ready")
        ea_ready = sem("ea_ready")
        amod_ready = sem("amod_ready")
        sq_ready = sem("sq_ready")
        sq_used = sem("sq_used")
        ns_ready = sem("ns_ready")
        rstd_ready = sem("rstd_ready")
        tmp_ready = sem("tmp_ready")
        h_ready = sem("h_ready")
        pads_ready = sem("pads_ready")
        conv_done = sem("conv_done")
        xbc_ready = sem("xbc_ready")
        dt_a = sem("dt_a")
        dt_v = sem("dt_v")
        da_ready = sem("da_ready")
        dec_in = sem("dec_in")
        dec_ready = sem("dec_ready")
        xdt_ready = sem("xdt_ready")
        wx_ready = sem("wx_ready")
        seg_ready = sem("seg_ready")
        ex_ready = sem("ex_ready")
        m_ready = sem("m_ready")
        diag_done = sem("diag_done")
        yg_ready = sem("yg_ready")
        yss_ready = sem("yss_ready")
        gn_v = sem("gn_v")
        gn_s = sem("gn_s")
        ossd_ready = sem("ossd_ready")
        st_ready = sem("st_ready")
        sv_ready = sem("sv_ready")
        ss_ready = sem("ss_ready")
        qkn_ready = sem("qkn_ready")
        krp_ready = sem("krp_ready")
        qrope_ready = sem("qrope_ready")
        mx_ready = sem("mx_ready")
        pr_ready = sem("pr_ready")
        pv_done = sem("pv_done")
        vn_ready = sem("vn_ready")
        sg_ready = sem("sg_ready")
        act_ready = sem("act_ready")
        act_read = sem("act_read")
        top_v = sem("top_v")
        top_a = sem("top_a")
        grep_ready = sem("grep_ready")
        zero_ready = sem("zero_ready")
        out_ready = sem("out_ready")
        hl_ready = sem("hl_ready")
        w_hi = sem("w_hi")
        w_lo = sem("w_lo")
        act_hi = sem("act_hi")
        dve_chain = sem("dve_chain")

        block = ctx.enter_context(nc.Block())

        @block.sync
        def _(sp):
            def load(name, src, n):
                i = load_of[name]
                if i >= R:
                    sp.wait_ge(w_begun, i - R + 2)
                sp.dma_start(wslot(i)[:, 0:n], src).then_inc(w_full[i % R], 16)

            sp.dma_start(condr[:, :], t["cond"]).then_inc(s_par, 16)
            sp.dma_start(const[:, :], t["const"]).then_inc(s_par, 16)
            sp.dma_start(colp[:, :], t["colp"]).then_inc(s_par, 16)
            sp.dma_start(rowp[:, :], t["rowp"].to_broadcast([P, L * N_ROW])).then_inc(s_par, 16)
            sp.dma_start(wsT[:, :], t["wsT"]).then_inc(s_par, 16)
            sp.dma_start(gfin[:, :], t["gfin"]).then_inc(s_par, 16)
            sp.dma_start(rtr[:, :], t["w_router"]).then_inc(s_par, 16)
            for n in range(R):
                load(f"mod0.{n}", t["w_mod"][n], SLOT)
            sp.dma_start(X[:, :], t["x"]).then_inc(s_x, 16)
            with sp.Fori(1, MOD_LOADS // R) as i:
                for k in range(R):
                    sp.wait_ge(w_begun, i * R + (k - R + 2))
                    sp.dma_start(wslot(k), t["w_mod"][bass.ds(i * R + k, 1), :, :].rearrange("a p n -> p (a n)"))\
                      .then_inc(w_full[k], 16)
            for l in range(L):
                for n, cs in enumerate(XL):
                    load(f"xbc{l}.{n}", t["w_xbc"][l, n, :, 0:len(cs) * KD * P], len(cs) * KD * P)
                for q, (a, b) in enumerate(CHUNKS):
                    load(f"tok{l}.{q}", t["w_tok"][l, :, KD * a:KD * b], KD * (b - a))
                load(f"ukv{l}", t["w_ukv"][l], 2 * 768)
                load(f"uq{l}", t["w_uq"][l], 3 * 576)
                for n in range(4):
                    load(f"wo{l}.{n}", t["w_out"][l, n], SLOT)
                if l == 0:
                    n0 = load_of["gu.0"]
                    with sp.Fori(0, GU_LOADS // R) as i:
                        for k in range(R):
                            for src, first_row, m in ((t["w_gu"], 0, 2 * k), (t["w_mod"], MOD_LOADS, 2 * k + 1)):
                                sp.wait_ge(w_begun, i * (2 * R) + (n0 + m - R + 2))
                                sp.dma_start(wslot(n0 + m), src[bass.ds(i * R + (first_row + k), 1), :, :].rearrange("a p n -> p (a n)"))\
                                  .then_inc(w_full[(n0 + m) % R], 16)
                    for n in range(GU_LOADS - GU_LOADS % R, MOD_LOADS):
                        if n < GU_LOADS:
                            load(f"gu.{n}", t["w_gu"][n], SLOT)
                        load(f"mod1.{n}", t["w_mod"][MOD_LOADS + n], SLOT)
                    for n in range(DN_LOADS):
                        load(f"dn.{n}", t["w_dn"][n], KF // 2 * P)
                else:
                    n0 = load_of["me.0"]

                    def w_free(e, k):
                        if isinstance(e, int):
                            if k < R:
                                sp.wait_ge(w_begun, n0 + k - R + 2)
                            else:
                                sp.wait_ge(w_lo, k - R + 1)
                        else:
                            sp.wait_ge(w_lo, e * ME_LOADS + (k - R + 1))

                    def expert(e):
                        for k in range(ME_GU):
                            w_free(e, k)
                            sp.dma_start(wslot(n0 + k), t["w_egu"][bass.ds(e * KE + k, 1), :, :].rearrange("a p n -> p (a n)"))\
                              .then_inc(w_full[(n0 + k) % R], 16)
                        at = 0
                        for k, (f, nf, j, nj) in enumerate(DN_PARTS):
                            n = nf * nj * P
                            w_free(e, ME_GU + k)
                            sp.dma_start(wslot(n0 + ME_GU + k)[:, 0:n],
                                         t["w_edn"][bass.ds(e, 1), :, at:at + n].rearrange("a p n -> p (a n)"))\
                              .then_inc(w_full[(n0 + ME_GU + k) % R], 16)
                            at += n

                    expert(0)
                    with sp.Fori(1, NE) as e:
                        expert(e)
            sp.wait_ge(out_ready, KD)
            sp.dma_start(t["out"], Xv[:, :, CTX:TOK]).then_inc(s_out, 16)
            sp.wait_ge(s_out, 16)

        @block.tensor
        def _(pe):
            def done(ins, name):
                ins.then_inc(use[name].full, 1)

            def mod_rows(bank, slot, w_value):
                pe.wait_ge(w_full[slot % R], w_value)
                for kk in range(KD):
                    g = 32 * (kk % 4)
                    ins = pe.matmul(bank.tile[g:g + 32, 0:2 * P], condp[:, kk * 32:(kk + 1) * 32],
                                    wslot(slot)[:, kk * 2 * P:(kk + 1) * 2 * P], start=(kk < 4), stop=(kk >= 4))
                    if kk == 0:
                        ins.then_inc(w_begun, 1)
                ins.then_inc(bank.full, 1)

            def mod_cols(bank, row_ready, row, out, at):
                pe.wait_ge(bank.free, row_ready)
                for c in range(2):
                    ins = pe.matmul(out[:, at + 2 * c:at + 2 * c + 2] if isinstance(at, int) else out[:, bass.ds(at + 2 * c, 2)],
                                    row[:, c * P:(c + 1) * P], fold, start=True, stop=True)
                return ins

            def modulation0():
                done0 = use["mod0"]
                with pe.Fori(0, MOD_LOADS // R) as i:
                    for k in range(R):
                        mod_rows(B[k], k, (i + 1) * 16)
                        ins = mod_cols(B[k], i + B[k].taken(f"mrow0.{k}"), mrow[k], done0.tile, i * (4 * R) + 4 * k)
                    ins.then_inc(done0.full, 1)

            def norm_sum(q, n):
                claim(pe, f"norm{q}")
                for c in range(KD):
                    pe.wait_ge(sq_ready, KD * q + c + 1)
                    pe.matmul(use[f"norm{q}"].tile[:, 0:n], ones, pair[:, (c % 2) * TOK:(c % 2) * TOK + n],
                              start=(c == 0), stop=(c == KD - 1)).then_inc(sq_used, 1)

            def in_proj(l):
                for n, cs in enumerate(XL):
                    w = load_of[f"xbc{l}.{n}"]
                    w_wait(pe, w)
                    for ci, c in enumerate(cs):
                        name = f"xbc{l}.{c}"
                        claim(pe, name)
                        for kk in range(KD):
                            if n == 0 and ci == 0:
                                pe.wait_ge(h_ready, KD * 2 * l + kk + 1)
                            ins = pe.matmul(use[name].tile[:, :], wslot(w)[:, (ci * KD + kk) * P:(ci * KD + kk + 1) * P],
                                            Hv[:, kk, :], start=(kk == 0), stop=(kk == KD - 1))
                            if ci == 0 and kk == 0:
                                ins.then_inc(w_begun, 1)
                        done(ins, name)
                for q, (a, b) in enumerate(CHUNKS):
                    w = load_of[f"tok{l}.{q}"]
                    w_wait(pe, w)
                    wv = wslot(w)[:, 0:KD * (b - a)].rearrange("p (k n) -> p k n", k=KD)
                    for i in (range(NT) if q < CTX_CHUNKS else tiles[l]):
                        name = f"tok{l}.{q}.{i}"
                        claim(pe, name)
                        for kk in range(KD):
                            ins = pe.matmul(use[name].tile[:, 0:b - a], Hv[:, kk, i * P:(i + 1) * P], wv[:, kk, :],
                                            start=(kk == 0), stop=(kk == KD - 1))
                            if kk == 0 and i == (0 if q < CTX_CHUNKS else T0[l]):
                                ins.then_inc(w_begun, 1)
                        done(ins, name)

            def ssd(l):
                T = tiles[l]
                t0 = T0[l]
                for i in range(NT):
                    claim(pe, f"xsT{l}.{i}")
                    if i == 0:
                        pe.wait_ge(xbc_ready, KX * (l + 1))
                    for c in range(3):
                        ins = pe.transpose(use[f"xsT{l}.{i}"].tile[:, c * P:(c + 1) * P], xbcT[:, c, i * P:(i + 1) * P], ident)
                    done(ins, f"xsT{l}.{i}")
                    claim(pe, f"BT{l}.{i}")
                    for c in range(2):
                        ins = pe.transpose(use[f"BT{l}.{i}"].tile[:, c * P:(c + 1) * P], xbcT[:, 3 + c, i * P:(i + 1) * P], ident)
                    done(ins, f"BT{l}.{i}")
                da = small[:, 0:48]
                claim(pe, f"acs{l}")
                pe.wait_ge(da_ready, l + 1)
                acs = use[f"acs{l}"].tile
                pe.matmul(acs[:, 0:24], upto, da[:, 0:24], start=True, stop=True)
                pe.matmul(acs[:, 24:48], down, da[:, 24:48], start=True, stop=True)
                done(pe.matmul(acs[:, 48:96], ones, da, start=True, stop=True), f"acs{l}")
                for r in range(2):
                    claim(pe, f"rows{l}.{r}")
                    for i in range(NT):
                        ins = pe.matmul(use[f"rows{l}.{r}"].tile[0:6, i * P:(i + 1) * P], da[:, r * 24 + i * 6:r * 24 + i * 6 + 6],
                                        upto if r == 0 else down, start=True, stop=True)
                    done(ins, f"rows{l}.{r}")
                for g in range(2):
                    claim(pe, f"cb{l}.{g}")
                    for i in T:
                        ins = pe.matmul(use[f"cb{l}.{g}"].tile[:, i * P:(i + 1) * P], xbcT[:, 3 + g, i * P:(i + 1) * P],
                                        xbcT[:, 5 + g, i * P:(i + 1) * P], start=True, stop=True)
                    done(ins, f"cb{l}.{g}")
                def state(i3):
                    for r in range(2):
                        i = CHAIN[r][i3]
                        name = f"st{l}.{r}.{i3}"
                        claim(pe, name)
                        if i3 == 0:
                            pe.wait_ge(wx_ready, 2 * l + r + 1)
                            taken(pe, f"BT{l}.{NT - 1}")
                        for g in range(2):
                            ins = pe.matmul(use[name].tile[:, g * 192:(g + 1) * 192], xsB[:, i, 384 + g * P:384 + (g + 1) * P],
                                            wx[:, r, i, g * 192:(g + 1) * 192], start=True, stop=True)
                        done(ins, name)

                def diag(k):
                    h, r = k // 2, k % 2
                    pe.wait_ge(m_ready, 12 * l + k + 1)
                    if k < 2:
                        pe.wait_ge(xdt_ready, 2 * l + r + 1)
                    for i in T:
                        if k == 0:
                            claim(pe, f"y{l}.{i}")
                        ins = pe.matmul(use[f"y{l}.{i}"].tile[:, h * 64:(h + 1) * 64], Mt[k % 2][:, i * P:(i + 1) * P],
                                        xdt[:, r, i, h * 64:(h + 1) * 64], start=(r == 0), stop=(r == 1))
                        if k == 11:
                            done(ins, f"y{l}.{i}")
                    if k < 11:
                        ins.then_inc(diag_done, 1)

                for k in range(12):
                    h, r = k // 2, k % 2
                    name = f"bc{l}.{k}"
                    claim(pe, name)
                    if k < 2:
                        taken(pe, f"rows{l}.{r}")
                    done(pe.matmul(use[name].tile[:, t0 * P:TOK], sel[0:6, h * P:(h + 1) * P], acsT[0:6, r, t0 * P:TOK],
                                   start=True, stop=True), name)
                    if k >= 1:
                        diag(k - 1)
                    if k in (1, 4, 7):
                        state(k // 3)
                diag(11)
                for i in T:
                    for r in range(2):
                        pos = CHAIN[r].index(i)
                        if pos == 0:
                            continue
                        name = f"off{l}.{i}.{r}"
                        claim(pe, name)
                        taken(pe, f"st{l}.{r}.2")
                        for g in range(2):
                            ins = pe.matmul(use[name].tile[:, g * 192:(g + 1) * 192], xbcT[:, 5 + g, i * P:(i + 1) * P],
                                            hin[:, r, pos - 1, g * 192:(g + 1) * 192], start=True, stop=True)
                        done(ins, name)

            def mla(l):
                T = tiles[l]
                pe.wait_ge(qkn_ready, l + 1)
                for c in range(3):
                    name = f"qlT{l}.{c}"
                    claim(pe, name)
                    for i in T:
                        ins = pe.transpose(use[name].tile[:, i * P:(i + 1) * P], pt[:, i, C_Q + c * P:C_Q + (c + 1) * P], ident)
                    done(ins, name)
                for c in range(2):
                    name = f"kvT{l}.{c}"
                    claim(pe, name)
                    for i in range(NT):
                        ins = pe.transpose(use[name].tile[:, i * P:(i + 1) * P], pt[:, i, C_KV + c * P:C_KV + (c + 1) * P], ident)
                    done(ins, name)
                w = load_of[f"ukv{l}"]
                w_wait(pe, w)
                ukv = wslot(w)[:, 0:2 * 768].rearrange("p (k n) -> p k n", k=2)
                for h in range(MLA_H):
                    name = f"kn{l}.{h}"
                    claim(pe, name)
                    for kk in range(2):
                        if h == 0:
                            taken(pe, f"kvT{l}.{kk}")
                        ins = pe.matmul(use[name].tile[0:NOPE, :], ukv[:, kk, h * NOPE:(h + 1) * NOPE], kvT[:, kk, :],
                                        start=(kk == 0), stop=(kk == 1))
                        if h == 0 and kk == 0:
                            ins.then_inc(w_begun, 1)
                    done(ins, name)
                for i in range(NT):
                    name = f"v{l}.{i}"
                    claim(pe, name)
                    for kk in range(2):
                        ins = pe.matmul(use[name].tile[:, 0:384], kvT[:, kk, i * P:(i + 1) * P], ukv[:, kk, 384:768],
                                        start=(kk == 0), stop=(kk == 1))
                    done(ins, name)
                name = f"kr{l}"
                claim(pe, name)
                pe.wait_ge(krp_ready, l + 1)
                for i in range(NT):
                    ins = pe.transpose(use[name].tile[0:QK, i * P:(i + 1) * P], krp[:, i, :], ident)
                done(ins, name)
                w = load_of[f"uq{l}"]
                w_wait(pe, w)
                uq = wslot(w)[:, 0:3 * 576].rearrange("p (k n) -> p k n", k=3)
                for c in range(3):
                    taken(pe, f"qlT{l}.{c}")

                def q_rows(i):
                    for hh in range(2):
                        name = f"q{l}.{i}.{hh}"
                        claim(pe, name)
                        for kk in range(3):
                            ins = pe.matmul(use[name].tile[:, 0:288], qlT[:, kk, i * P:(i + 1) * P],
                                            uq[:, kk, hh * 288:(hh + 1) * 288], start=(kk == 0), stop=(kk == 2))
                            if i == T0[l] and hh == 0 and kk == 0:
                                ins.then_inc(w_begun, 1)
                        done(ins, name)

                def q_cols(i):
                    taken(pe, f"q{l}.{i}.0")
                    taken(pe, f"q{l}.{i}.1")
                    if i >= 2:
                        pe.wait_ge(qrope_ready, 2 * l + i - 1)
                    for hh in range(2):
                        name = f"qT{l}.{i}.{hh}"
                        claim(pe, name)
                        for h in (range(0, 4) if hh == 0 else range(4, 6)):
                            ins = pe.transpose(use[name].tile[0:QK, (h % 4) * P:(h % 4 + 1) * P],
                                               qtk[i % 2][:, h * QK:(h + 1) * QK], ident)
                        done(ins, name)

                for i in T:
                    q_rows(i)
                    if i > T0[l]:
                        q_cols(i - 1)
                q_cols(NT - 1)
                units = [(i, h) for i in T for h in range(MLA_H)]

                def scores(i, h):
                    name = f"s{l}.{i}.{h}"
                    nk = 2 if i < 2 else NT
                    claim(pe, name)
                    if (i, h) == units[0]:
                        taken(pe, f"kr{l}")
                        for hh in range(MLA_H):
                            taken(pe, f"kn{l}.{hh}")
                        for ii in range(NT):
                            taken(pe, f"v{l}.{ii}")
                        for ii in T:
                            taken(pe, f"qT{l}.{ii}.0")
                            taken(pe, f"qT{l}.{ii}.1")
                    done(pe.matmul(use[name].tile[:, 0:nk * P], qT[0:QK, h, i * P:(i + 1) * P], kT[0:QK, h, 0:nk * P],
                                   start=True, stop=True), name)

                scores(*units[0])
                for u, (i, h) in enumerate(units):
                    if u + 1 < len(units):
                        scores(*units[u + 1])
                    nk = 2 if i < 2 else NT
                    name = f"pT{l}.{i}.{h}"
                    claim(pe, name)
                    pe.wait_ge(pr_ready, 24 * l + u + 1)
                    for k in range(nk):
                        ins = pe.transpose(use[name].tile[:, k * P:(k + 1) * P], pr[u % 2][:, k * P:(k + 1) * P], ident)
                    done(ins, name)
                    taken(pe, name)
                    oname = f"o{l}.{i}"
                    if h == 0:
                        claim(pe, oname)
                    for k in range(nk):
                        ins = pe.matmul(use[oname].tile[:, h * 64:(h + 1) * 64], pT[u % 2][:, k * P:(k + 1) * P],
                                        vt[:, k, h * 64:(h + 1) * 64], start=(k == 0), stop=(k == nk - 1))
                    if h == MLA_H - 1:
                        done(ins, oname)
                    else:
                        ins.then_inc(pv_done, 1)

            def sgu(l):
                pe.wait_ge(vn_ready, [4, 6][l])
                for i in tiles[l]:
                    name = f"sgu{l}.{i}"
                    claim(pe, name)
                    for h in range(SGU_H):
                        ins = pe.matmul(use[name].tile[:, h * 64:(h + 1) * 64], wsT[:, (l * SGU_H + h) * P:(l * SGU_H + h + 1) * P],
                                        pt[:, i, C_V + h * 64:C_V + (h + 1) * 64], start=True, stop=True)
                    done(ins, name)

            def out_proj(l):
                T = tiles[l]
                t0 = T0[l]
                pe.wait_ge(ossd_ready, l + 1)
                for i in T:
                    taken(pe, f"o{l}.{i}")
                    taken(pe, f"sgu{l}.{i}")
                    for b in range(2):
                        name = f"oT{l}.{i}.{b}"
                        claim(pe, name)
                        for c in range(4):
                            a = C_Q + (4 * b + c) * P
                            ins = pe.transpose(use[name].tile[:, c * P:(c + 1) * P], pt[:, i, a:a + P], ident)
                        done(ins, name)
                for i in T:
                    for b in range(2):
                        taken(pe, f"oT{l}.{i}.{b}")
                for n in range(4):
                    w = load_of[f"wo{l}.{n}"]
                    w_wait(pe, w)
                    for c in range(2):
                        name = f"wo{l}.{2 * n + c}"
                        claim(pe, name)
                        for kk in range(KD):
                            ins = pe.matmul(use[name].tile[:, t0 * P:TOK], wslot(w)[:, (c * KD + kk) * P:(c * KD + kk + 1) * P],
                                            Hv[:, kk, t0 * P:TOK], start=(kk == 0), stop=(kk == KD - 1))
                            if c == 0 and kk == 0:
                                ins.then_inc(w_begun, 1)
                        done(ins, name)

            def ffn():
                n0 = load_of["gu.0"]
                for kk in range(KD):
                    pe.wait_ge(h_ready, KD + kk + 1)
                gb = [B[b].before(f"gate.{b}") for b in range(3)]

                def hidden(k, slot, w_value, gate_free, up_read):
                    pe.wait_ge(w_full[slot % R], w_value)
                    for half in range(2):
                        if half == 0:
                            pe.wait_ge(B[k].free, gate_free)
                        elif up_read is None:
                            claim(pe, f"up.{k}")
                        else:
                            pe.wait_ge(act_ready, up_read)
                        for kk in range(KD):
                            ins = pe.matmul(B[3 * half + k].tile[:, :], wslot(slot)[:, (half * KD + kk) * P:(half * KD + kk + 1) * P],
                                            Hv[:, kk, :], start=(kk == 0), stop=(kk == KD - 1))
                            if half == 0 and kk == 0:
                                ins.then_inc(w_begun, 1)
                        ins.then_inc(B[3 * half + k].full, 1)

                mrow_taken = B[6].taken("mrow1.0")
                out = use["mod1"].tile
                claim(pe, "mrow1.0")
                claim(pe, "mod1")

                def value(m):
                    return 16 * ((n0 + m) // R + 1)

                for k in range(R):
                    hidden(k, n0 + 2 * k, value(2 * k), gb[k], None)
                    if k:
                        mod_cols(B[6], mrow_taken + k - 1, mrow[k - 1], out, 4 * (k - 1))
                    mod_rows(B[6], n0 + 2 * k + 1, value(2 * k + 1))
                with pe.Fori(1, KF // R) as i:
                    for k in range(R):
                        hidden(k, n0 + 2 * k, (i * 2 + ((n0 + 2 * k) // R + 1)) * 16, i + gb[k], i * R + (k - 2))
                        mod_cols(B[6], i * R + (mrow_taken + k - 1), mrow[(k - 1) % R], out, i * (4 * R) + 4 * (k - 1))
                        mod_rows(B[6], n0 + 2 * k + 1, (i * 2 + ((n0 + 2 * k + 1) // R + 1)) * 16)
                for n in range(KF - KF % R, MOD_LOADS):
                    if n < KF:
                        m = load_of[f"gu.{n}"]
                        hidden(n % R, m, 16 * (m // R + 1), gb[n % R] + n // R, n - 2)
                    mod_cols(B[6], mrow_taken + n - 1, mrow[(n - 1) % R], out, 4 * (n - 1))
                    m = load_of[f"mod1.{n}"]
                    mod_rows(B[6], m, 16 * (m // R + 1))
                n = MOD_LOADS - 1
                done(mod_cols(B[6], mrow_taken + n, mrow[n % R], out, 4 * n), "mod1")
                pe.wait_ge(act_ready, KF)
                for j in range(KD):
                    name = f"dn.{j}"
                    claim(pe, name)
                    for half in range(2):
                        w = load_of[f"dn.{2 * j + half}"]
                        w_wait(pe, w)
                        for f in range(KF // 2):
                            ff = half * (KF // 2) + f
                            ins = pe.matmul(use[name].tile[:, :], wslot(w)[:, f * P:(f + 1) * P], act[:, ff * TOK:(ff + 1) * TOK],
                                            start=(ff == 0), stop=(ff == KF - 1))
                            if f == 0:
                                ins.then_inc(w_begun, 1)
                        if half == 1:
                            done(ins, name)

            def moe():
                for kk in range(KD):
                    pe.wait_ge(hl_ready, kk + 1)
                claim(pe, "logits")
                for i in range(2):
                    for kk in range(KD):
                        for part in range(2):
                            ins = pe.matmul(use["logits"].tile[:, i * NE:(i + 1) * NE], me_h[part][:, kk, i * P:(i + 1) * P].bitcast(F32),
                                            rtr[:, kk * NE:(kk + 1) * NE], start=(kk == 0 and part == 0),
                                            stop=(kk == KD - 1 and part == 1))
                done(ins, "logits")
                for e in range(NE):
                    name = f"gb.{e}"
                    claim(pe, name)
                    for i in range(2):
                        pe.wait_ge(grep_ready, 2 * e + i + 1)
                        ins = pe.matmul(use[name].tile[:, i * P:(i + 1) * P], grep[:, i * P:(i + 1) * P], ident,
                                        start=True, stop=True)
                    done(ins, name)
                pe.wait_ge(zero_ready, 2)
                for b in range(4, 8):
                    claim(pe, f"moe.{b}")
                    ins = pe.matmul(B[b].tile[:, :], zeros[:, 0:P], zeros[:, :], start=True, stop=False, skip_group_check=True)
                    if b == 4:
                        ins.then_inc(act_read, 1)
                    else:
                        done(ins, f"moe.{b}")
                n0 = load_of["me.0"]
                gb = [B[b].before(f"meg.0.{b}") for b in range(3)]
                per = [len(range(b, KE, 3)) for b in range(3)]

                def split_product(out, n, tile, right, first, last):
                    a = (n % W_SPLIT) * SLOT + tile * P
                    hi, lo = (w[:, a:a + P] for w in me_w)
                    ins0 = pe.matmul(out, hi, right[0], start=first, stop=False, skip_group_check=True)
                    pe.matmul(out, lo, right[0], start=False, stop=False, skip_group_check=True)
                    return ins0, pe.matmul(out, hi, right[1], start=False, stop=last, skip_group_check=True)

                with pe.Fori(0, NE) as e:
                    for i in range(KE):
                        b = i % 3
                        pe.wait_ge(w_lo, e * ME_LOADS + (i + 1))
                        pe.wait_ge(B[b].free, e * per[b] + (gb[b] + i // 3))
                        for half in range(2):
                            for kk in range(KD):
                                ins0, ins = split_product(B[b].tile[:, half * SEQ:(half + 1) * SEQ], i, half * KD + kk,
                                                          [h[:, kk, :] for h in me_h], kk == 0, kk == KD - 1)
                                if half == 0 and kk == 0:
                                    ins0.then_inc(w_begun, 1)
                        ins.then_inc(B[b].full, 1)
                    for k, (f0, nf, j0, nj) in enumerate(DN_PARTS):
                        pe.wait_ge(w_lo, e * ME_LOADS + (ME_GU + k + 1))
                        pe.wait_ge(act_ready, e * KE + (KF + f0 + nf))
                        for f in range(nf):
                            for j in range(nj):
                                jj = j0 + j
                                ins0, ins = split_product(B[4 + jj // 2].tile[:, (jj % 2) * SEQ:(jj % 2 + 1) * SEQ], ME_GU + k, f * nj + j,
                                                          [h[:, (f0 + f) * SEQ:(f0 + f + 1) * SEQ] for h in me_act], False, False)
                                if f == 0 and j == 0:
                                    ins0.then_inc(w_begun, 1)
                    ins.then_inc(act_read, 1)

            pe.wait_ge(cond_ready, 1)
            modulation0()
            for l in range(L):
                norm_sum(2 * l, TOK)
                in_proj(l)
                ssd(l)
                mla(l)
                sgu(l)
                out_proj(l)
                norm_sum(2 * l + 1, TOK - T0[l] * P)
                if l == 0:
                    ffn()
                else:
                    moe()
            norm_sum(4, SEQ)

        @block.scalar
        def _(ac):
            def take(name, out, in_, func=ACT.Copy, scale=1.0):
                ac.activation(out, in_, func, scale=scale).then_inc(use[name].free, 1)

            def norm(q, l, w, t0, x_ready, parts=None):
                n = TOK - t0 * P
                for c in range(KD):
                    x_ready(c)
                    if q or c >= 2:
                        ac.wait_ge(sq_used, KD * q + c - 1)
                    ac.activation(pair[:, (c % 2) * TOK:(c % 2) * TOK + n], Xv[:, c, t0 * P:TOK], ACT.Square).then_inc(sq_ready, 1)
                taken(ac, f"norm{q}")
                ac.activation(ns[:, 0:n], nv[:, 0:n], ACT.Sqrt).then_inc(ns_ready, 1)
                if w is None:
                    return
                ac.wait_ge(amod_ready, 2 * l + w + 1)
                for c in range(KD):
                    ac.wait_ge(tmp_ready, KD * q + c + 1)
                    for k in range(2):
                        a, b = k * CTX, (k + 1) * CTX
                        if a < t0 * P:
                            continue
                        for out in ([Hv[:, c, a:b]] if parts is None else [p[:, c, a - t0 * P:b - t0 * P] for p in parts]):
                            ins = ac.activation(out, pair2[:, (c % 2) * TOK + a - t0 * P:(c % 2) * TOK + b - t0 * P],
                                                ACT.Identity, bias=modv[:, l, 3 * w, c, k:k + 1], scale=amv[:, l, w, c, k:k + 1])
                    ins.then_inc(h_ready, 1)

            def in_proj(l):
                def silu(c):
                    ac.wait_ge(conv_done, KX * l + c + 1)
                    ac.activation(xbcT[:, c, :], cacc[c % 2], ACT.Silu, bias=col(l, "conv_b")[:, c:c + 1]).then_inc(xbc_ready, 1)

                for c in range(KX):
                    name = f"xbc{l}.{c}"
                    full(ac, name)
                    if c == 0:
                        ac.wait_ge(pads_ready, 2 * l + 2)
                    if c >= 2:
                        ac.wait_ge(conv_done, KX * l + c - 1)
                    take(name, xp[c % 2][:, :, 2:2 + CTX], use[name].tile[:, :].rearrange("p (s n) -> p s n", s=2))
                    if c >= 1:
                        silu(c - 1)
                silu(KX - 1)
                for q, (a, b) in enumerate(CHUNKS):
                    func = ACT.Gelu_apprx_tanh if a >= C_U else ACT.Silu if a >= C_Z else ACT.Copy
                    for i in (range(NT) if q < CTX_CHUNKS else tiles[l]):
                        name = f"tok{l}.{q}.{i}"
                        full(ac, name)
                        take(name, pt[:, i, a:b], use[name].tile[:, 0:b - a], func)

            def ssd(l):
                T = tiles[l]
                t0 = T0[l]
                for i in range(NT):
                    full(ac, f"xsT{l}.{i}")
                    take(f"xsT{l}.{i}", xsB[:, i, 0:384], use[f"xsT{l}.{i}"].tile[:, 0:384])
                    full(ac, f"BT{l}.{i}")
                    take(f"BT{l}.{i}", xsB[:, i, 384:640], use[f"BT{l}.{i}"].tile[:, 0:256])
                ac.wait_ge(dt_v, l + 1)
                ac.activation(small[:, 96:144], small[:, 144:192], ACT.Exp).then_inc(dt_a, 1)
                for r in range(2):
                    full(ac, f"rows{l}.{r}")
                    take(f"rows{l}.{r}", acsT[0:6, r, :], use[f"rows{l}.{r}"].tile[0:6, :])
                ac.wait_ge(dec_in, l + 1)
                ac.activation(small[:, 432:576], small[:, 288:432], ACT.Exp).then_inc(dec_ready, 1)
                for k in range(12):
                    ac.wait_ge(seg_ready, 12 * l + k + 1)
                    if k >= 2:
                        ac.wait_ge(m_ready, 12 * l + k - 1)
                    ac.activation(Ex[k % 2][:, t0 * P:TOK], seg[k % 2][:, t0 * P:TOK], ACT.Exp).then_inc(ex_ready, 1)
                for n, i in enumerate(T):
                    ac.wait_ge(yg_ready, 4 * l + n + 1)
                    ac.activation(Mt[0][:, 0:384], pt[:, i, C_Z:C_Z + 384], ACT.Square, accum_out=sst[:, i:i + 1]).then_inc(yss_ready, 1)
                    if n + 1 < len(T):
                        ac.wait_ge(yss_ready, 4 * l + n + 1)
                ac.wait_ge(gn_v, l + 1)
                ac.activation(sst[:, 8 + t0:12], sst[:, 4 + t0:8], ACT.Sqrt).then_inc(gn_s, 1)

            def mla(l):
                T = tiles[l]
                ac.wait_ge(ossd_ready, l + 1)
                for i in T:
                    if i > T[0]:
                        ac.wait_ge(st_ready, 8 * l + i - T[0])
                    ac.activation(pr[0][:, 0:384], pt[:, i, C_Q:C_Q + 384], ACT.Square, accum_out=stats[:, i:i + 1]).then_inc(st_ready, 1)
                for i in range(NT):
                    ac.wait_ge(st_ready, 8 * l + len(T) + i)
                    ac.activation(pr[0][:, 0:256], pt[:, i, C_KV:C_KV + 256], ACT.Square, accum_out=stats[:, 4 + i:5 + i])\
                      .then_inc(st_ready, 1)
                ac.wait_ge(sv_ready, l + 1)
                ac.activation(ssq[:, :], sv[:, :], ACT.Sqrt).then_inc(ss_ready, 1)
                a = T0[l] * P
                for c in range(3):
                    name = f"qlT{l}.{c}"
                    full(ac, name)
                    take(name, qlT[:, c, a:TOK], use[name].tile[:, a:TOK], scale=col(l, "g_q")[:, c:c + 1])
                for c in range(2):
                    name = f"kvT{l}.{c}"
                    full(ac, name)
                    take(name, kvT[:, c, :], use[name].tile[:, :], scale=col(l, "g_kv")[:, c:c + 1])
                for i in range(NT):
                    name = f"v{l}.{i}"
                    full(ac, name)
                    take(name, vt[:, i, :], use[name].tile[:, 0:384])
                name = f"kr{l}"
                full(ac, name)
                take(name, kT[NOPE:QK, :, :], use[name].tile[NOPE:QK, :].unsqueeze(1).to_broadcast([ROPE, MLA_H, TOK]))

                def q_cols(i):
                    for hh in range(2):
                        name = f"qT{l}.{i}.{hh}"
                        full(ac, name)
                        hs = slice(0, 4) if hh == 0 else slice(4, 6)
                        nh = 4 if hh == 0 else 2
                        take(name, qT[0:QK, hs, i * P:(i + 1) * P],
                             use[name].tile[0:QK, 0:nh * P].rearrange("p (h n) -> p h n", h=nh))

                for i in T:
                    for hh in range(2):
                        name = f"q{l}.{i}.{hh}"
                        full(ac, name)
                        if hh == 0 and i >= T0[l] + 2:
                            full(ac, f"qT{l}.{i - 2}.1")
                        take(name, qtk[i % 2][:, hh * 288:(hh + 1) * 288], use[name].tile[:, 0:288])
                    if i > T0[l]:
                        q_cols(i - 1)
                q_cols(NT - 1)
                units = [(i, h) for i in T for h in range(MLA_H)]
                for u, (i, h) in enumerate(units):
                    nk = 2 if i < 2 else NT
                    ac.wait_ge(mx_ready, 24 * l + u + 1)
                    if u >= 2:
                        full(ac, f"pT{l}.{units[u - 2][0]}.{units[u - 2][1]}")
                    name = f"s{l}.{i}.{h}"
                    ac.activation(pr[u % 2][:, 0:nk * P], use[name].tile[:, 0:nk * P], ACT.Exp, bias=mx[:, u % 2:u % 2 + 1],
                                  scale=SCALE, accum_out=rsum[:, i * MLA_H + h:i * MLA_H + h + 1]).then_inc(pr_ready, 1)

            def out_proj(l):
                g = col(l, "g_ssd")
                for i in tiles[l]:
                    a, b = i * P, (i + 1) * P
                    name = f"oT{l}.{i}.0"
                    full(ac, name)
                    tl = use[name].tile
                    take(name, Hv[:, 0:3, a:b], tl[:, 0:384].rearrange("p (c n) -> p c n", c=3))
                    take(name, Hv[:, 3, a:b], tl[:, 384:512], scale=g[:, 0:1])
                    name = f"oT{l}.{i}.1"
                    full(ac, name)
                    tl = use[name].tile
                    take(name, Hv[:, 4, a:b], tl[:, 0:128], scale=g[:, 1:2])
                    take(name, Hv[:, 5, a:b], tl[:, 128:256], scale=g[:, 2:3])
                    take(name, Hv[:, 6:8, a:b], tl[:, 256:512].rearrange("p (c n) -> p c n", c=2))

            def ffn():
                gb = [B[b].filled(f"gate.{b}") for b in range(3)]

                def one(k, gfull, used):
                    ac.wait_ge(B[k].full, gfull)
                    if used is not None:
                        ac.wait_ge(act_ready, used)
                    ac.activation(sg[k], B[k].tile[:, :], ACT.Silu).then_inc(B[k].free, 1)

                for k in range(3):
                    one(k, gb[k], None)
                with ac.Fori(1, KF // R) as i:
                    for k in range(3):
                        one(k, i + gb[k], i * 3 + (k - 2))
                for f in range(KF - KF % R, KF):
                    one(f % R, gb[f % R] + f // R, f - 2)

            def high(e, k):
                n = load_of["me.0"] + k
                ac.wait_ge(w_full[n % R], (e * (ME_LOADS // R) + (n // R + 1)) * 16)
                ac.wait_ge(w_begun, e * ME_LOADS + (n - W_SPLIT + 2))
                size = load_size(k)
                a = (k % W_SPLIT) * SLOT
                ac.activation(me_w[0][:, a:a + size], wslot(n)[:, 0:size], ACT.Copy).then_inc(w_hi, 1)

            def moe():
                ac.wait_ge(top_v, 1)
                ac.activation(lg[:, 32:34], lg[:, 24:26], ACT.Exp).then_inc(top_a, 1)
                gb = [B[b].filled(f"meg.0.{b}") for b in range(3)]
                per = [len(range(b, KE, 3)) for b in range(3)]

                def expert(e, last):
                    for k in range(ME_LOADS):
                        if k + 2 < ME_LOADS or not last:
                            high(e, k + 2)
                        if k < KE:
                            b = k % 3
                            ac.wait_ge(B[b].full, e * per[b] + (gb[b] + k // 3))
                            ac.wait_ge(act_ready, e * KE + (KF + k - 2))
                            ac.activation(me_sg[b][:, :], B[b].tile[:, 0:SEQ], ACT.Silu).then_inc(sg_ready, 1)

                with ac.Fori(0, NE - 1) as e:
                    expert(e, False)
                expert(NE - 1, True)

            ac.wait_ge(s_par, 112)
            ac.wait_ge(zero_ready, 1)
            ac.activation(condp[:, :].rearrange("p (c k) -> p c k", c=KD)[:, :, 0:2], condr[:, :].rearrange("p (c k) -> p c k", c=KD),
                          ACT.Silu).then_inc(cond_ready, 1)
            for l in range(L):
                ac.activation(ea[:, l * 12:(l + 1) * 12], row(l, "a_log"), ACT.Exp).then_inc(ea_ready, 1)
            for l in range(L):
                def x_in(c):
                    if l == 0:
                        ac.wait_ge(s_x, 16)
                    else:
                        taken(ac, f"dn.{c}")

                norm(2 * l, l, 0, 0, x_in)
                in_proj(l)
                ssd(l)
                mla(l)
                out_proj(l)
                if l == 1:
                    taken(ac, f"wo{l}.{KD - 1}")
                    for k in range(2):
                        high(0, k)
                norm(2 * l + 1, l, 1, T0[l], lambda c: taken(ac, f"wo{l}.{c}"), (me_raw, me_h[0]) if l else None)
                if l == 0:
                    ffn()
                else:
                    moe()
            norm(4, 1, None, 2, lambda c: taken(ac, f"moe.{4 + c // 2}"))

        @block.vector
        def _(ve):
            links = [0]

            def link(ins):
                links[0] += 1
                ins.then_inc(dve_chain, 1)
                ve.wait_ge(dve_chain, links[0])

            def norm(q, t0, tail=None, parts=None):
                n = TOK - t0 * P
                ve.wait_ge(sq_used, KD * (q + 1))
                ve.tensor_scalar(nv[:, 0:n], use[f"norm{q}"].tile[:, 0:n], 1.0 / D, EPS, ALU.mult, ALU.add)\
                  .then_inc(use[f"norm{q}"].free, 1)
                ve.wait_ge(ns_ready, q + 1)
                link(ve.reciprocal(rstd[:, 0:n], ns[:, 0:n]))
                if tail:
                    tail()
                    return
                for c in range(KD):
                    if q or c >= 2:
                        ve.wait_ge(h_ready, KD * q + c - 1)
                    ve.tensor_tensor(pair2[:, (c % 2) * TOK:(c % 2) * TOK + n], Xv[:, c, t0 * P:TOK], rstd[:, 0:n], ALU.mult)\
                      .then_inc(tmp_ready, 1)
                    if parts and c >= 2:
                        low_h(q, c - 2, parts)
                if parts:
                    low_h(q, KD - 2, parts)
                    low_h(q, KD - 1, parts)

            def low_h(q, c, parts):
                raw, hi, lo = parts
                ve.wait_ge(h_ready, KD * q + c + 1)
                ve.tensor_tensor(lo[:, c, :], raw[:, c, :], hi[:, c, :].bitcast(F32), ALU.subtract).then_inc(hl_ready, 1)

            def mod_row(bank, filled, k):
                ve.wait_ge(bank.full, filled)
                ve.tensor_copy(mrow[k], bank.tile[:, 0:2 * P]).then_inc(bank.free, 1)

            def modulation(l):
                name = f"mod{l}"
                full(ve, name)
                ve.tensor_tensor(modv[:, l].rearrange("p m c k -> p (m c) k"),
                                 use[name].tile[:, 0:2 * MOD_TILES].rearrange("p (j k) -> p j k", k=2),
                                 col(l, "b_mod").unsqueeze(2).to_broadcast([P, MOD_TILES, 2]), ALU.add).then_inc(use[name].free, 1)
                taken(ve, name)
                for w, g in enumerate(("g_mix", "g_ffn")):
                    ve.scalar_tensor_tensor(amv[:, l, w], modv[:, l, 3 * w + 1], 1.0,
                                            col(l, g).unsqueeze(2).to_broadcast([P, KD, 2]), ALU.add, ALU.mult)\
                      .then_inc(amod_ready, 1)

            def conv(l):
                w = col(l, "conv_w")
                for c in range(KX):
                    taken(ve, f"xbc{l}.{c}")
                    if l or c >= 2:
                        ve.wait_ge(xbc_ready, KX * l + c - 1)
                    x = xp[c % 2]
                    y = cacc[c % 2].rearrange("p (s n) -> p s n", s=2)
                    link(ve.tensor_scalar(y, x[:, :, 0:CTX], w[:, c * TAPS:c * TAPS + 1], None, ALU.mult))
                    for k in range(1, TAPS):
                        ins = ve.scalar_tensor_tensor(y, x[:, :, k:k + CTX], w[:, c * TAPS + k:c * TAPS + k + 1], y, ALU.mult, ALU.add)
                        if k < TAPS - 1:
                            link(ins)
                    ins.then_inc(conv_done, 1)

            def bc6(ap):
                return ap.unsqueeze(2).to_broadcast([P, SSD_H, SSD_HD])

            def ssd(l):
                T = tiles[l]
                t0 = T0[l]
                s = small
                da, dt = s[:, 0:48], s[:, 48:96]
                for i in range(NT):
                    taken(ve, f"tok{l}.0.{i}")
                y = s[:, 192:240]
                link(ve.tensor_tensor(y.rearrange("p (r t j) -> p r t j", r=2, t=NT),
                                      pt[:, :, C_DT:C_DT + 12].rearrange("p t (r j) -> p r t j", r=2),
                                      row(l, "dt_bias").rearrange("p (r j) -> p r j", r=2).unsqueeze(2)
                                      .to_broadcast([P, 2, NT, SSD_H]), ALU.add))
                ve.scalar_tensor_tensor(s[:, 144:192], y, -1.0, y, ALU.mult, ALU.min).then_inc(dt_v, 1)
                ve.wait_ge(dt_v, l + 1)
                link(ve.tensor_scalar(dt, y, 0.0, None, ALU.max))
                ve.wait_ge(dt_a, l + 1)
                e, w2, ww, sr = s[:, 96:144], s[:, 240:288], s[:, 288:336], s[:, 336:384]
                link(ve.tensor_scalar(w2, e, 2.0, None, ALU.add))
                link(ve.reciprocal(w2, w2))
                link(ve.tensor_tensor(w2, w2, e, ALU.mult))
                link(ve.tensor_tensor(ww, w2, w2, ALU.mult))
                link(ve.tensor_scalar(sr, ww, 1.0 / 15, None, ALU.mult))
                for n in (13, 11, 9, 7, 5, 3):
                    link(ve.scalar_tensor_tensor(sr, sr, 1.0 / n, ww, ALU.add, ALU.mult))
                link(ve.scalar_tensor_tensor(sr, sr, 1.0, w2, ALU.add, ALU.mult))
                link(ve.scalar_tensor_tensor(dt, sr, 2.0, dt, ALU.mult, ALU.add))
                ve.wait_ge(ea_ready, l + 1)
                for r in range(2):
                    ins = ve.scalar_tensor_tensor(da[:, r * 24:(r + 1) * 24].rearrange("p (t j) -> p t j", t=NT),
                                                  dt[:, r * 24:(r + 1) * 24].rearrange("p (t j) -> p t j", t=NT), -1.0,
                                                  ea[:, l * 12 + r * 6:l * 12 + r * 6 + 6].unsqueeze(1).to_broadcast([P, NT, SSD_H]),
                                                  ALU.mult, ALU.mult)
                    if r == 0:
                        link(ins)
                ins.then_inc(da_ready, 1)
                taken(ve, f"xsT{l}.{NT - 1}")
                for r in range(2):
                    ve.tensor_tensor(xdt[:, r].rearrange("p t (j n) -> p t j n", j=SSD_H),
                                     xsB[:, :, 0:384].rearrange("p t (j n) -> p t j n", j=SSD_H),
                                     dt[:, r * 24:(r + 1) * 24].rearrange("p (t j) -> p t j", t=NT).unsqueeze(3)
                                     .to_broadcast([P, NT, SSD_H, SSD_HD]), ALU.mult).then_inc(xdt_ready, 1)
                name = f"acs{l}"
                full(ve, name)
                acs = acs_s[:, :]
                ve.tensor_copy(acs, use[name].tile[:, 0:96]).then_inc(use[name].free, 1)
                taken(ve, name)
                ve.tensor_tensor(s[:, 288:336], acs[:, 48:96], acs[:, 0:48], ALU.subtract)
                ve.tensor_copy(s[:, 336:432], acs[:, 0:96]).then_inc(dec_in, 1)
                for g in range(2):
                    name = f"cb{l}.{g}"
                    full(ve, name)
                    for r in range(2):
                        m = upto if r == 0 else down
                        n = NT - t0
                        ve.tensor_tensor(cbm[:, r, g, t0 * P:TOK].rearrange("p (t n) -> p t n", t=n),
                                         use[name].tile[:, t0 * P:TOK].rearrange("p (t n) -> p t n", t=n),
                                         m.unsqueeze(1).to_broadcast([P, n, P]), ALU.mult).then_inc(use[name].free, 1)

                def segs(k):
                    h, r = k // 2, k % 2
                    name = f"bc{l}.{k}"
                    full(ve, name)
                    if k >= 2:
                        ve.wait_ge(ex_ready, 12 * l + k - 1)
                    n = NT - t0
                    a = acs[:, r * 24 + h:r * 24 + 24:6][:, t0:NT].unsqueeze(2).to_broadcast([P, n, P])
                    sv_ = seg[k % 2][:, t0 * P:TOK].rearrange("p (t n) -> p t n", t=n)
                    ve.tensor_tensor(sv_, use[name].tile[:, t0 * P:TOK].rearrange("p (t n) -> p t n", t=n), a, ALU.min)\
                      .then_inc(use[name].free, 1)
                    taken(ve, name)
                    ve.tensor_tensor(sv_, sv_, a, ALU.subtract).then_inc(seg_ready, 1)

                def mm(k):
                    h, r = k // 2, k % 2
                    ve.wait_ge(ex_ready, 12 * l + k + 1)
                    if k == 0:
                        taken(ve, f"cb{l}.1")
                    if k >= 2:
                        ve.wait_ge(diag_done, 11 * l + k - 1)
                    ve.tensor_tensor(Mt[k % 2][:, t0 * P:TOK], Ex[k % 2][:, t0 * P:TOK], cbm[:, r, h // HPG, t0 * P:TOK], ALU.mult)\
                      .then_inc(m_ready, 1)

                dec = s[:, 432:576]

                def state(i3):
                    if i3 == 0:
                        ve.wait_ge(dec_ready, l + 1)
                    for r in range(2):
                        name = f"st{l}.{r}.{i3}"
                        full(ve, name)
                        if i3 == 0:
                            ve.tensor_copy(hin[:, r, 0], use[name].tile[:, 0:384]).then_inc(use[name].free, 1)
                        else:
                            i = CHAIN[r][i3]
                            cd = dec[:, 96 + r * 24 + i * 6:96 + r * 24 + i * 6 + 6]
                            link(ve.tensor_tensor(hin[:, r, i3].rearrange("p (j n) -> p j n", j=SSD_H),
                                                  hin[:, r, i3 - 1].rearrange("p (j n) -> p j n", j=SSD_H), bc6(cd), ALU.mult))
                            ve.tensor_tensor(hin[:, r, i3], hin[:, r, i3], use[name].tile[:, 0:384], ALU.add)\
                              .then_inc(use[name].free, 1)
                        taken(ve, name)

                for k in range(12):
                    segs(k)
                    if k >= 1:
                        mm(k - 1)
                    if k in (3, 6, 9):
                        state(k // 3 - 1)
                mm(11)
                for n, i in enumerate(T):
                    skip = row(l, "d_skip")
                    v6 = ysum.rearrange("p (j n) -> p j n", j=SSD_H)
                    t6 = ytmp.rearrange("p (j n) -> p j n", j=SSD_H)
                    link(ve.tensor_tensor(v6, xsB[:, i, 0:384].rearrange("p (j n) -> p j n", j=SSD_H), bc6(skip), ALU.mult))
                    name = f"y{l}.{i}"
                    full(ve, name)
                    ve.tensor_tensor(ysum, ysum, use[name].tile[:, 0:384], ALU.add).then_inc(use[name].free, 1)
                    taken(ve, name)
                    for r in range(2):
                        if CHAIN[r].index(i) == 0:
                            continue
                        name = f"off{l}.{i}.{r}"
                        full(ve, name)
                        ex = dec[:, 48 + r * 24 + i * 6:48 + r * 24 + i * 6 + 6]
                        ve.tensor_tensor(t6, use[name].tile[:, 0:384].rearrange("p (j n) -> p j n", j=SSD_H), bc6(ex), ALU.mult)\
                          .then_inc(use[name].free, 1)
                        taken(ve, name)
                        link(ve.tensor_tensor(ysum, ysum, ytmp, ALU.add))
                    taken(ve, f"tok{l}.5.{i}")
                    ve.tensor_tensor(pt[:, i, C_Z:C_Z + 384], ysum, pt[:, i, C_Z:C_Z + 384], ALU.mult).then_inc(yg_ready, 1)
                    ve.wait_ge(yg_ready, 4 * l + n + 1)
                ve.wait_ge(yss_ready, 4 * l + len(T))
                ve.tensor_scalar(sst[:, 4 + t0:8], sst[:, t0:4], 1.0 / SSD_W, EPS, ALU.mult, ALU.add).then_inc(gn_v, 1)
                ve.wait_ge(gn_s, l + 1)
                link(ve.reciprocal(sst[:, 12 + t0:16], sst[:, 8 + t0:12]))
                for n, i in enumerate(T):
                    ins = ve.tensor_scalar(pt[:, i, C_Z:C_Z + 384], pt[:, i, C_Z:C_Z + 384], sst[:, 12 + i:13 + i], None, ALU.mult)
                ins.then_inc(ossd_ready, 1)

            def mla(l):
                T = tiles[l]
                t0 = T0[l]
                taken(ve, f"tok{l}.7.{NT - 1}")
                for i in T:
                    link(ve.bn_stats(bn[:, i * 8:i * 8 + 6], pt[:, i, C_V:C_V + 256]))
                    link(ve.bn_aggr(bn[:, i * 8 + 6:i * 8 + 8], bn[:, i * 8:i * 8 + 6]))
                bv = bn[:, :].rearrange("p (t n) -> p t n", t=NT)
                ve.tensor_scalar(sv[:, 8 + t0:12], bv[:, t0:NT, 7], EPS, None, ALU.add)
                ve.wait_ge(st_ready, [8, 14][l])
                ve.tensor_scalar(sv[:, t0:4], stats[:, t0:4], 1.0 / Q_LORA, EPS, ALU.mult, ALU.add)
                ve.tensor_scalar(sv[:, 4:8], stats[:, 4:8], 1.0 / KV_LORA, EPS, ALU.mult, ALU.add).then_inc(sv_ready, 1)
                ve.wait_ge(ss_ready, l + 1)
                link(ve.reciprocal(rs[:, :], ssq[:, :]))
                for i in T:
                    ins = ve.tensor_scalar(pt[:, i, C_Q:C_Q + 384], pt[:, i, C_Q:C_Q + 384], rs[:, i:i + 1], None, ALU.mult)
                for i in range(NT):
                    ins = ve.tensor_scalar(pt[:, i, C_KV:C_KV + 256], pt[:, i, C_KV:C_KV + 256], rs[:, 4 + i:5 + i], None, ALU.mult)
                ins.then_inc(qkn_ready, 1)

                def rotate(src, dst, i, nh, width):
                    cs = const[:, rope0 + (i - 2) * 32:rope0 + (i - 1) * 32].rearrange("p (s a f) -> p s a f", s=2, a=2)
                    c = cs[:, 0].unsqueeze(1).to_broadcast([P, nh, 2, 8])
                    s = cs[:, 1].unsqueeze(1).to_broadcast([P, nh, 2, 8])
                    tm = [rtmp[:, k * 96:k * 96 + nh * 16].rearrange("p (h a f) -> p h a f", h=nh, a=2) for k in range(4)]
                    t1 = src.rearrange("p h (a m f) -> p h a m f", a=2, m=2)[:, :, :, 0, :]
                    t2 = src.rearrange("p h (a m f) -> p h a m f", a=2, m=2)[:, :, :, 1, :]
                    d1 = dst.rearrange("p h (a m f) -> p h a m f", a=2, m=2)[:, :, :, 0, :]
                    d2 = dst.rearrange("p h (a m f) -> p h a m f", a=2, m=2)[:, :, :, 1, :]
                    ve.tensor_tensor(tm[0], t1, c, ALU.mult)
                    ve.tensor_tensor(tm[1], t2, s, ALU.mult)
                    ve.tensor_tensor(tm[2], t1, s, ALU.mult)
                    link(ve.tensor_tensor(tm[3], t2, c, ALU.mult))
                    link(ve.tensor_tensor(d1, tm[0], tm[1], ALU.subtract))
                    return ve.tensor_tensor(d2, tm[2], tm[3], ALU.add)

                link(ve.memset(krp[:, :, 0:NOPE], 0.0))
                for i in range(2):
                    link(ve.tensor_copy(krp[:, i, NOPE:QK], pt[:, i, C_KR:C_KR + ROPE]))
                link(rotate(pt[:, 2, C_KR:C_KR + ROPE].unsqueeze(1), krp[:, 2, NOPE:QK].unsqueeze(1), 2, 1, ROPE))
                rotate(pt[:, 3, C_KR:C_KR + ROPE].unsqueeze(1), krp[:, 3, NOPE:QK].unsqueeze(1), 3, 1, ROPE).then_inc(krp_ready, 1)
                for h in range(MLA_H):
                    name = f"kn{l}.{h}"
                    full(ve, name)
                    ve.tensor_copy(kT[0:NOPE, h, :], use[name].tile[0:NOPE, :]).then_inc(use[name].free, 1)
                for i in T:
                    taken(ve, f"q{l}.{i}.0")
                    taken(ve, f"q{l}.{i}.1")
                    if i >= 2:
                        if i == 2:
                            ve.wait_ge(krp_ready, l + 1)
                        else:
                            ve.wait_ge(qrope_ready, 2 * l + 1)
                        q = qtk[i % 2].rearrange("p (h n) -> p h n", h=MLA_H)[:, :, NOPE:QK]
                        rotate(q, q, i, MLA_H, QK).then_inc(qrope_ready, 1)
                bn2 = bn[:, :].rearrange("p (t n) -> p t n", t=NT)
                for i in T:
                    v = pt[:, i, C_V:C_V + 256]
                    link(ve.tensor_scalar(v, v, bn2[:, i, 6:7], rs[:, 8 + i:9 + i], ALU.subtract, ALU.mult))
                    link(ve.tensor_tensor(v, v, row(l, "g_sgu"), ALU.mult))
                    ve.tensor_tensor(v, v, row(l, "beta_sgu"), ALU.add).then_inc(vn_ready, 1)
                units = [(i, h) for i in T for h in range(MLA_H)]

                def top(u):
                    i, h = units[u]
                    nk = 2 if i < 2 else NT
                    name = f"s{l}.{i}.{h}"
                    full(ve, name)
                    if u >= 2:
                        ve.wait_ge(pr_ready, 24 * l + u - 1)
                    ve.tensor_reduce(mx[:, 2 + u % 2:3 + u % 2], use[name].tile[:, 0:nk * P], AX.X, ALU.max)\
                      .then_inc(use[name].free, 1)
                    taken(ve, name)
                    ve.tensor_scalar(mx[:, u % 2:u % 2 + 1], mx[:, 2 + u % 2:3 + u % 2], -SCALE, None, ALU.mult).then_inc(mx_ready, 1)

                top(0)
                for u, (i, h) in enumerate(units):
                    if u + 1 < len(units):
                        top(u + 1)
                    nk = 2 if i < 2 else NT
                    name = f"pT{l}.{i}.{h}"
                    full(ve, name)
                    if u >= 2:
                        if units[u - 2][1] == MLA_H - 1:
                            full(ve, f"o{l}.{units[u - 2][0]}")
                        else:
                            ve.wait_ge(pv_done, 20 * l + (u - 2) - (u - 2) // MLA_H + 1)
                    ve.tensor_copy(pT[u % 2][:, 0:nk * P], use[name].tile[:, 0:nk * P]).then_inc(use[name].free, 1)
                    if h == MLA_H - 1:
                        name = f"o{l}.{i}"
                        a = i * MLA_H
                        link(ve.reciprocal(rinv[:, a:a + MLA_H], rsum[:, a:a + MLA_H]))
                        full(ve, name)
                        ve.tensor_tensor(pt[:, i, C_Q:C_Q + 384].rearrange("p (j n) -> p j n", j=MLA_H),
                                         use[name].tile[:, 0:384].rearrange("p (j n) -> p j n", j=MLA_H),
                                         bc6(rinv[:, a:a + MLA_H]), ALU.mult).then_inc(use[name].free, 1)

            def sgu(l):
                for i in tiles[l]:
                    name = f"sgu{l}.{i}"
                    full(ve, name)
                    for h in range(SGU_H):
                        u = pt[:, i, C_U + h * 64:C_U + (h + 1) * 64]
                        ve.scalar_tensor_tensor(u, use[name].tile[:, h * 64:(h + 1) * 64], col(l, "b_sgu")[:, h:h + 1], u,
                                                ALU.add, ALU.mult).then_inc(use[name].free, 1)

            def residual(l, m, name, j, t0=None):
                full(ve, name)
                for k in range(2):
                    if k * CTX < T0[l] * P:
                        continue
                    ve.scalar_tensor_tensor(Xv[:, j, k * CTX:(k + 1) * CTX], use[name].tile[:, k * CTX:(k + 1) * CTX],
                                            modv[:, l, m, j, k:k + 1], Xv[:, j, k * CTX:(k + 1) * CTX], ALU.mult, ALU.add)\
                      .then_inc(use[name].free, 1)

            def ffn():
                gb = [B[b].taken(f"gate.{b}") for b in range(3)]
                ub = [B[3 + b].filled(f"up.{b}") for b in range(3)]

                def one(k, out, gtaken, ufull):
                    ve.wait_ge(B[k].free, gtaken)
                    ve.wait_ge(B[3 + k].full, ufull)
                    ve.tensor_tensor(out, sg[k], B[3 + k].tile[:, :], ALU.mult).then_inc(act_ready, 1)

                mb = B[6].filled("mrow1.0")
                with ve.Fori(0, KF // R) as i:
                    for k in range(R):
                        one(k, act[:, bass.ds(i * (R * TOK) + k * TOK, TOK)], i + gb[k], i + ub[k])
                        mod_row(B[6], i * R + (mb + k), k)
                for f in range(KF - KF % R, MOD_LOADS):
                    if f < KF:
                        one(f % R, act[:, f * TOK:(f + 1) * TOK], gb[f % R] + f // R, ub[f % R] + f // R)
                    mod_row(B[6], mb + f, f % R)
                modulation(1)
                for j in range(KD):
                    residual(0, 5, f"dn.{j}", j)

            def route():
                full(ve, "logits")
                v = [lg[:, 40 + 16 * k:56 + 16 * k].rearrange("p (t e) -> p t e", t=2) for k in range(9)]
                lo, eq, key, oh1, l2, oh2, ga, gb_, tm = v
                m1, m2, dd = lg[:, 0:2], lg[:, 8:10], lg[:, 24:26]
                kx = lg[:, 16:18]
                fb = first.unsqueeze(1).to_broadcast([P, 2, NE])

                def b8(a):
                    return a.unsqueeze(2).to_broadcast([P, 2, NE])

                ve.tensor_copy(lo, use["logits"].tile[:, 0:16].rearrange("p (t e) -> p t e", t=2)).then_inc(use["logits"].free, 1)
                taken(ve, "logits")

                def best(src, m, oh):
                    link(ve.tensor_reduce(m, src, AX.X, ALU.max))
                    link(ve.tensor_tensor(eq, src, b8(m), ALU.is_equal))
                    link(ve.tensor_tensor(key, eq, fb, ALU.mult))
                    link(ve.tensor_reduce(kx, key, AX.X, ALU.max))
                    link(ve.tensor_tensor(oh, key, b8(kx), ALU.is_equal))

                best(lo, m1, oh1)
                link(ve.scalar_tensor_tensor(l2, oh1, -3.0e38, lo, ALU.mult, ALU.add))
                best(l2, m2, oh2)
                ve.tensor_tensor(dd, m2, m1, ALU.subtract).then_inc(top_v, 1)
                ve.wait_ge(top_a, 1)
                ex, w1, w2 = lg[:, 32:34], lg[:, 4:6], lg[:, 12:14]
                link(ve.tensor_scalar(w2, ex, 1.0, None, ALU.add))
                link(ve.reciprocal(w1, w2))
                link(ve.tensor_tensor(w2, ex, w1, ALU.mult))
                link(ve.tensor_tensor(ga, oh1, b8(w1), ALU.mult))
                link(ve.tensor_tensor(gb_, oh2, b8(w2), ALU.mult))
                link(ve.tensor_tensor(ga, ga, gb_, ALU.add))
                for e in range(NE):
                    for i in range(2):
                        if e:
                            full(ve, f"gb.{e - 1}")
                        ve.tensor_scalar(grep[:, i * P:(i + 1) * P], ones, ga[:, i, e:e + 1], None, ALU.mult).then_inc(grep_ready, 1)
                    name = f"gb.{e}"
                    full(ve, name)
                    ve.tensor_copy(gateb[:, e * SEQ:(e + 1) * SEQ], use[name].tile[:, 0:SEQ]).then_inc(use[name].free, 1)
                taken(ve, f"gb.{NE - 1}")

            def low(e, k):
                ve.wait_ge(w_hi, e * ME_LOADS + (k + 1))
                size = load_size(k)
                a = (k % W_SPLIT) * SLOT
                ve.tensor_tensor(me_w[1][:, a:a + size], wslot(load_of["me.0"] + k)[:, 0:size], me_w[0][:, a:a + size].bitcast(F32),
                                 ALU.subtract).then_inc(w_lo, 1)

            def moe():
                ve.memset(zeros[:, :], 0.0).then_inc(zero_ready, 1)
                route()
                per = [len(range(b, KE, 3)) for b in range(3)]
                tb = [B[b].taken(f"meg.0.{b}") for b in range(3)]

                def expert(e, last):
                    for k in range(ME_LOADS):
                        if k + 2 < ME_LOADS or not last:
                            low(e, k + 2)
                        if k >= KE:
                            continue
                        b = k % 3
                        ve.wait_ge(sg_ready, e * KE + (k + 1))
                        if k == 0:
                            ve.wait_ge(act_read, e + 1)
                        ve.tensor_tensor(me_up[b][:, :], B[b].tile[:, SEQ:2 * SEQ], gateb[:, bass.ds(e * SEQ, SEQ)], ALU.mult)\
                          .then_inc(B[b].free, 1)
                        ve.wait_ge(B[b].free, e * per[b] + (tb[b] + k // 3))
                        ve.tensor_tensor(me_prod[b][:, :], me_sg[b][:, :], me_up[b][:, :], ALU.mult)
                        hi, lo = (a[:, k * SEQ:(k + 1) * SEQ] for a in me_act)
                        ve.tensor_tensor(hi, me_sg[b][:, :], me_up[b][:, :], ALU.mult).then_inc(act_hi, 1)
                        ve.wait_ge(act_hi, e * KE + (k + 1))
                        ve.tensor_tensor(lo, me_prod[b][:, :], hi.bitcast(F32), ALU.subtract).then_inc(act_ready, 1)

                with ve.Fori(0, NE - 1) as e:
                    expert(e, False)
                expert(NE - 1, True)
                ve.wait_ge(act_read, NE + 1)
                for j in range(KD):
                    name = f"moe.{4 + j // 2}"
                    ve.scalar_tensor_tensor(Xv[:, j, CTX:TOK], use[name].tile[:, (j % 2) * SEQ:(j % 2 + 1) * SEQ],
                                            modv[:, 1, 5, j, 1:2], Xv[:, j, CTX:TOK], ALU.mult, ALU.add).then_inc(use[name].free, 1)

            def final():
                for c in range(KD):
                    ve.scalar_tensor_tensor(Xv[:, c, CTX:TOK], Xv[:, c, CTX:TOK], gfin[:, c:c + 1], rstd[:, 0:SEQ],
                                            ALU.mult, ALU.mult).then_inc(out_ready, 1)

            ve.memset(condp[:, :], 0.0).then_inc(zero_ready, 1)
            ve.wait_ge(s_par, 112)
            ve.memset(sv[:, :], 1.0)
            ve.memset(sst[:, :], 1.0)
            ve.memset(stats[:, :], 1.0)
            for l in range(L):
                if l == 0:
                    with ve.Fori(0, MOD_LOADS // R) as i:
                        for k in range(R):
                            mod_row(B[k], i + B[k].filled(f"mrow0.{k}"), k)
                    modulation(0)
                    ve.wait_ge(s_x, 16)
                else:
                    for c in range(KD):
                        taken(ve, f"dn.{c}")
                norm(2 * l, 0)
                for x in xp:
                    ve.memset(x[:, :, 0:2], 0.0)
                    ve.memset(x[:, :, CTX + 2:CTX + 4], 0.0).then_inc(pads_ready, 1)
                conv(l)
                ssd(l)
                mla(l)
                sgu(l)
                for j in range(KD):
                    residual(l, 2, f"wo{l}.{j}", j)
                taken(ve, f"wo{l}.{KD - 1}")
                if l == 1:
                    for k in range(2):
                        low(0, k)
                norm(2 * l + 1, T0[l], parts=(me_raw, me_h[0], me_h[1]) if l else None)
                if l == 0:
                    ffn()
                else:
                    moe()
            taken(ve, "moe.7")
            norm(4, 2, final)

        @block.gpsimd
        def _(po):
            for l in range(L):
                po.wait_ge(dec_ready, l + 1)
                for r in range(2):
                    po.wait_ge(xdt_ready, 2 * l + r + 1)
                    te = small[:, 432 + r * 24:432 + (r + 1) * 24].rearrange("p (t j) -> p t j", t=NT)
                    po.tensor_tensor(wx[:, r].rearrange("p t (j n) -> p t j n", j=SSD_H),
                                     xdt[:, r].rearrange("p t (j n) -> p t j n", j=SSD_H),
                                     te.unsqueeze(3).to_broadcast([P, NT, SSD_H, SSD_HD]), ALU.mult).then_inc(wx_ready, 1)


def small_params(v):
    def cols(a, n):
        return np.asarray(a).reshape(L, n, P).transpose(2, 0, 1)

    conv_w = np.asarray(v["conv_w"]).reshape(L, TAPS, KX, P).transpose(3, 0, 2, 1).reshape(P, L, KX * TAPS)
    b_sgu = np.asarray(v["b_sgu"]).transpose(2, 0, 1)
    col = np.concatenate([conv_w, cols(v["conv_b"], KX), cols(v["b_mod"], MOD_TILES), cols(v["g_mix"], KD), cols(v["g_ffn"], KD), b_sgu,
                          cols(v["g_ssd"], 3), cols(v["g_q"], 3), cols(v["g_kv"], 2)], axis=2)
    rows = np.concatenate([np.asarray(v[n]).reshape(L, -1) for n in ("dt_bias", "a_log", "d_skip", "g_sgu", "beta_sgu")], axis=1)
    return col.reshape(P, -1), rows.reshape(1, -1)


def tiles_of(w, k, per):
    lead = w.shape[:-2]
    n = w.shape[-1] // (per * P)
    a = w.reshape(*lead, k, P, n, per, P)
    m = len(lead)
    return a.transpose(*range(m), m + 2, m + 1, m + 3, m, m + 4).reshape(*lead, n, P, per * k * P)


def kernel(**inputs):
    import concourse.bacc as bacc
    from concourse.bass_utils import run_bass_kernel_spmd

    v = {k: np.asarray(a) for k, a in inputs.items()}
    s = IN_SGU
    z0, x0 = s, s + SSD_W
    dt0 = x0 + XBC
    q0 = dt0 + 12
    kv0 = q0 + Q_LORA
    kr0 = kv0 + KV_LORA
    w_in = v["w_in"]
    xbc = np.concatenate([w_in[:, :, x0:dt0], np.zeros((L, D, P), np.float32)], axis=2)
    tok = np.concatenate([w_in[:, :, dt0:q0], w_in[:, :, kr0:], w_in[:, :, kv0:kr0], w_in[:, :, q0:kv0], w_in[:, :, z0:x0],
                          w_in[:, :, 0:s]], axis=2).reshape(L, KD, P, C_END).transpose(0, 2, 1, 3)
    tok = np.concatenate([tok[..., a:b].reshape(L, P, -1) for a, b in CHUNKS], axis=2)
    ukv = v["w_ukv"].reshape(L, 2, P, MLA_H, 2, 64).transpose(0, 2, 1, 4, 3, 5).reshape(L, P, 2 * 768)
    uq = v["w_uq"].reshape(L, 3, P, 576).transpose(0, 2, 1, 3).reshape(L, P, 3 * 576)
    wo = v["w_out"]
    wo = np.concatenate([wo[:, SGU_W + SSD_W:], wo[:, SGU_W:SGU_W + SSD_W], wo[:, :SGU_W]], axis=1)
    gu = np.concatenate([tiles_of(v["w_gate"][0], KD, 1), tiles_of(v["w_up"][0], KD, 1)], axis=2)
    dn = v["w_down"][0].reshape(2, KF // 2, P, KD, P).transpose(3, 0, 2, 1, 4).reshape(DN_LOADS, P, -1)
    egu = np.concatenate([tiles_of(v["w_gate_e"][0], KD, 1), tiles_of(v["w_up_e"][0], KD, 1)], axis=3).reshape(NE * KE, P, SLOT)
    edn = v["w_down_e"][0].reshape(NE, KE, P, D).transpose(0, 2, 1, 3).reshape(NE, P, KE * D)
    x = np.concatenate([v["ctx"][0], v["x"][0]], axis=0).reshape(TOK, KD, P).transpose(2, 1, 0).reshape(P, -1)
    cond = np.stack([v["c_ctx"].reshape(KD, P), v["c"].reshape(KD, P)], axis=2).transpose(1, 0, 2).reshape(P, -1)
    colp, rowp = small_params(v)
    arrays = {
        "x": x, "cond": cond, "const": const_array(), "colp": colp, "rowp": rowp,
        "wsT": v["w_sgu"].transpose(3, 0, 1, 2).reshape(P, -1),
        "gfin": v["g_final"].reshape(KD, P).T,
        "w_router": v["w_router"][0].reshape(KD, P, NE).transpose(1, 0, 2).reshape(P, -1),
        "w_mod": v["w_mod"].reshape(L, KD, P, MOD_LOADS, 2 * P).transpose(0, 3, 2, 1, 4).reshape(L * MOD_LOADS, P, SLOT),
        "w_xbc": tiles_of(xbc, KD, 2), "w_tok": tok, "w_ukv": ukv, "w_uq": uq, "w_out": tiles_of(wo, KD, 2),
        "w_gu": gu, "w_dn": dn, "w_egu": egu, "w_edn": edn,
    }
    nc = bacc.Bacc("TRN2", target_bir_lowering=False, num_devices=1)
    t, feed = {}, {}
    for name, a in arrays.items():
        feed[f"in_{name}"] = np.ascontiguousarray(a)
        t[name] = nc.dram_tensor(f"in_{name}", a.shape, F32, kind="ExternalInput").ap()
    t["out"] = nc.dram_tensor("out", (P, KD, SEQ), F32, kind="ExternalOutput").ap()
    program(nc, t)
    r = run_bass_kernel_spmd(nc, [feed], core_ids=[0])
    return r.results[0]["out"].transpose(2, 1, 0).reshape(1, SEQ, D)
```

```python
from contextlib import ExitStack

import numpy as np

import concourse.bass as bass
from concourse import mybir

F32 = mybir.dt.float32
F32R = mybir.dt.float32r
ALU = mybir.AluOpType
ACT = mybir.ActivationFunctionType
AX = mybir.AxisListType

P = 128
L = 2
D = 1024
KD = D // P
CTX, SEQ = 256, 256
NT = (CTX + SEQ) // P
TOK = NT * P
EPS = 1e-6

SGU_H, SGU_W = 4, 256
SSD_H, SSD_HD, SSD_W, HPG = 6, 64, 384, 3
STATE = 128
TAPS = 5
XBC = SSD_W + 4 * STATE
KX = XBC // P
MLA_H, NOPE, ROPE, MLA_V = 6, 64, 32, 64
QK = NOPE + ROPE
Q_LORA, KV_LORA = 384, 256
SCALE = QK ** -0.5
IN_SGU = 2 * SGU_W
GRID_W = 64
THETA = 10000.0

D_FF = 2816
KF = D_FF // P
NE = 8
D_FFE = 1408
KE = D_FFE // P

C_DT, C_KR, C_KV, C_Q, C_Z, C_U, C_V, C_END = 0, 12, 44, 300, 684, 1068, 1324, 1580
CHUNKS = [(0, 150), (150, 300), (300, 556), (556, 684), (684, 876), (876, 1068), (1068, 1324), (1324, 1580)]
CTX_CHUNKS = 2

R = 3
SLOT = 2048
ME_R = 6
W_SPLIT = 3
PART, W_PARTS = 512, 3
MODS = 6
MOD_TILES = MODS * KD
MOD_LOADS = MOD_TILES // 2
MOD_EARLY = 4
GU_LOADS = KF
DN_LOADS = 2 * KD
GU_PARTS = KF * SLOT // PART
DN_TILES = [(0, 4), (4, 4), (8, 3)]
DN_PART_N = len(DN_TILES) * DN_LOADS
ME_GU, ME_DN = KE, 7
ME_LOADS = ME_GU + ME_DN
DN_PARTS = [(0, 1, 0, KD // 2)] + [(2 * i + 1, 2, 0, KD) for i in range(5)] + [(0, 1, KD // 2, KD // 2)]
DN_FIRST, DN_LAST = [0, 1], [KE - 1, 0]

T0 = [0, CTX // P]
CHAIN = [[0, 1, 2, 3], [1, 0, 3, 2]]


def const_array():
    i = np.arange(P)
    ident = np.eye(P)
    ones = np.ones((P, P))
    upto = (i[:, None] <= i[None, :]).astype(np.float64)
    sel = np.zeros((P, SSD_H, P))
    for h in range(SSD_H):
        sel[h, h, :] = 1.0
    n_freq = ROPE // 4
    inv = THETA ** (-np.arange(n_freq, dtype=np.float32) / np.float32(n_freq))
    tok = np.arange(SEQ)
    ang = np.stack([(tok // GRID_W)[:, None] * inv, (tok % GRID_W)[:, None] * inv], axis=1).astype(np.float32)
    rope = np.stack([np.cos(ang), np.sin(ang)], axis=1).reshape(SEQ // P, P, 2 * 2 * n_freq)
    rope = rope.transpose(1, 0, 2).reshape(P, -1)
    first = np.broadcast_to(NE - np.arange(NE), (P, NE))
    fold = np.stack([(i % 32 == k) for k in range(2)], axis=1)
    parts = [ident, ones, upto, upto.T, sel.reshape(P, -1), rope, first, fold]
    return np.concatenate([np.asarray(a, np.float32) for a in parts], axis=1)


N_CONST = 4 * P + SSD_H * P + 64 + NE + 2

COLS = {}
_at = 0
for _name, _n in (("conv_w", KX * TAPS), ("conv_b", KX), ("b_mod", MOD_TILES), ("g_mix", KD), ("g_ffn", KD), ("b_sgu", SGU_H),
                  ("g_ssd", 3), ("g_q", 3), ("g_kv", 2)):
    COLS[_name] = (_at, _n)
    _at += _n
N_COL = _at
ROWS = {"dt_bias": (0, 12), "a_log": (12, 12), "d_skip": (24, 6), "g_sgu": (30, 256), "beta_sgu": (286, 256)}
N_ROW = 542


class Bank:

    def __init__(self, tile, full, free):
        self.tile, self.full, self.free = tile, full, free
        self.order, self.fulls, self.reads = {}, [0], [0]

    def add(self, name, reads=1, fulls=1):
        assert name not in self.order, name
        self.order[name] = len(self.reads)
        self.reads.append(self.reads[-1] + reads)
        self.fulls.append(self.fulls[-1] + fulls)

    def filled(self, name):
        return self.fulls[self.order[name]]

    def taken(self, name):
        return self.reads[self.order[name]]

    def before(self, name):
        return self.reads[self.order[name] - 1]


def program(nc, t):
    ctx = ExitStack()
    with ctx:
        def sb(name, n, p=P, dt=F32):
            return ctx.enter_context(nc.sbuf_tensor(name, [p, n], dt))

        def sem(name):
            return ctx.enter_context(nc.semaphore(name))

        const = sb("const", N_CONST)
        colp = sb("colp", L * N_COL)
        rowp = sb("rowp", L * N_ROW)
        wsT = sb("wsT", L * SGU_H * P)
        gfin = sb("gfin", KD)
        rtr = sb("rtr", KD * NE)
        acs_s = sb("acs_s", 96)
        condr = sb("condr", KD * 2)
        condp = sb("condp", KD * 32)
        ea = sb("ea", L * 12)
        mods = sb("mods", L * MOD_TILES * 2)
        amod = sb("amod", L * 2 * KD * 2)
        X = sb("X", KD * TOK)
        ring = sb("ring", R * SLOT)
        nv = sb("nv", TOK)
        ns = sb("ns", TOK)
        rstd = sb("rstd", TOK)
        mrow = [nv[:, 0:2 * P], nv[:, 2 * P:4 * P], ns[:, 0:2 * P]]
        pair = sb("pair", 2 * TOK)
        pair2 = sb("pair2", 2 * TOK)
        mrow0 = [pair2[:, 2 * P * k:2 * P * (k + 1)] for k in range(3)]
        stats = sb("stats", 12)
        sv = sb("sv", 12)
        ssq = sb("ssq", 12)
        rs = sb("rs", 12)
        bn = sb("bn", 4 * 8)
        small = sb("small", 12 * 48)
        sst = sb("sst", 16)
        mx = sb("mx", 4)
        rsum = sb("rsum", NT * MLA_H)
        rinv = sb("rinv", NT * MLA_H)
        WORK = 23600
        with ExitStack() as mixer:
            H = mixer.enter_context(nc.sbuf_tensor("H", [P, KD * TOK], F32))
            ptok = mixer.enter_context(nc.sbuf_tensor("ptok", [P, NT * C_END], F32))
            work = mixer.enter_context(nc.sbuf_tensor("work", [P, WORK], F32))

        def view(at, n):
            assert at[0] + n <= WORK, (at[0], n)
            v = work[:, at[0]:at[0] + n]
            at[0] += n
            return v

        at = [0]
        xp = [view(at, 2 * (CTX + 4)).rearrange("p (s n) -> p s n", s=2) for _ in range(2)]
        cacc = [view(at, TOK) for _ in range(2)]
        xbcT = view(at, KX * TOK).rearrange("p (c n) -> p c n", c=KX)
        xsB = view(at, NT * 640).rearrange("p (t n) -> p t n", t=NT)
        acsT = view(at, 2 * TOK).rearrange("p (r n) -> p r n", r=2)
        cbm = view(at, 4 * TOK).rearrange("p (r g n) -> p r g n", r=2, g=2)
        seg = [view(at, TOK) for _ in range(2)]
        Ex = [view(at, TOK) for _ in range(2)]
        Mt = [view(at, TOK) for _ in range(2)]
        xdt = view(at, 2 * NT * SSD_W).rearrange("p (r t n) -> p r t n", r=2, t=NT)
        wx = view(at, 2 * NT * SSD_W).rearrange("p (r t n) -> p r t n", r=2, t=NT)
        hin = view(at, 2 * 3 * SSD_W).rearrange("p (r i n) -> p r i n", r=2, i=3)
        ytmp = view(at, SSD_W)
        ysum = view(at, SSD_W)
        at = [0]
        qlT = view(at, 3 * TOK).rearrange("p (c n) -> p c n", c=3)
        kvT = view(at, 2 * TOK).rearrange("p (c n) -> p c n", c=2)
        qtk = [view(at, MLA_H * QK) for _ in range(2)]
        krp = view(at, NT * QK).rearrange("p (t n) -> p t n", t=NT)
        rtmp = view(at, 4 * MLA_H * ROPE // 2)
        qT = view(at, MLA_H * TOK).rearrange("p (h n) -> p h n", h=MLA_H)
        kT = view(at, MLA_H * TOK).rearrange("p (h n) -> p h n", h=MLA_H)
        vt = view(at, NT * SSD_W).rearrange("p (t n) -> p t n", t=NT)
        pr = [view(at, TOK) for _ in range(2)]
        pT = [view(at, TOK) for _ in range(2)]

        with ExitStack() as dense:
            def dense_sb(name, n, dt=F32R):
                return dense.enter_context(nc.sbuf_tensor(name, [P, n], dt))

            ff_h = [dense_sb(f"ff_h_{part}", KD * TOK)[:, :].rearrange("p (c n) -> p c n", c=KD) for part in ("hi", "lo")]
            ff_w = [dense_sb(f"ff_w_{part}", W_PARTS * PART) for part in ("hi", "lo")]
            with nc.sbuf_tensor("ff_raw", [P, KD * TOK], F32) as ff_raw:
                ff_raw = ff_raw[:, :].rearrange("p (c n) -> p c n", c=KD)
            ff_act = [dense_sb(f"ff_act_{part}", KF * TOK) for part in ("hi", "lo")]
        sg = [pair[:, 0:TOK], pair[:, TOK:2 * TOK], pair2[:, 0:TOK]]
        prod = pair2[:, TOK:2 * TOK]

        me_w = [sb(f"me_w_{part}", W_SPLIT * SLOT, dt=F32R) for part in ("hi", "lo")]
        me_xe = [sb(f"me_xe_{part}", D, dt=F32R) for part in ("hi", "lo")]
        me_act = [sb(f"me_act_{part}", KE * P, dt=F32R) for part in ("hi", "lo")]
        me_ring = sb("me_ring", (ME_R - R) * SLOT)
        me_sg = [nv[:, b * P:(b + 1) * P] for b in range(3)]
        me_prod = [ns[:, b * P:(b + 1) * P] for b in range(3)]
        gather = [pair, pair2]
        lg = rstd[:, 0:384]
        scatter = sb("scatter", NE * SEQ)
        flag = sb("flag", 1, dt=mybir.dt.int32)
        with nc.sbuf_tensor("me_h", [P, KD * SEQ], F32) as me_h, nc.sbuf_tensor("weighted", [P, 2 * NE * P], F32) as weighted:
            me_h = me_h[:, :].rearrange("p (c n) -> p c n", c=KD)
        me_y = sb("me_y", NE * D)

        Xv = X[:, :].rearrange("p (c n) -> p c n", c=KD)
        htok = Xv[:, :, 0:CTX]
        Hv = H[:, :].rearrange("p (c n) -> p c n", c=KD)
        pt = ptok[:, :].rearrange("p (t n) -> p t n", t=NT)
        ident = const[:, 0:P]
        ones = const[:, P:2 * P]
        upto = const[:, 2 * P:3 * P]
        down = const[:, 3 * P:4 * P]
        sel = const[:, 4 * P:4 * P + SSD_H * P]
        rope0 = 4 * P + SSD_H * P
        first = const[:, rope0 + 64:rope0 + 64 + NE]
        fold = const[:, rope0 + 64 + NE:rope0 + 66 + NE]
        modv = mods[:, :].rearrange("p (l m c k) -> p l m c k", l=L, m=MODS, c=KD)
        amv = amod[:, :].rearrange("p (l w c k) -> p l w c k", l=L, w=2, c=KD)

        def col(l, name):
            a, n = COLS[name]
            return colp[:, l * N_COL + a:l * N_COL + a + n]

        def row(l, name):
            a, n = ROWS[name]
            return rowp[:, l * N_ROW + a:l * N_ROW + a + n]

        def wslot(n):
            return ring[:, (n % R) * SLOT:(n % R + 1) * SLOT]

        load_of = {}

        def plan(name):
            load_of[name] = len(load_of)

        for n in range(MOD_LOADS):
            plan(f"mod0.{n}")
        for l in range(L):
            for n in range(4):
                plan(f"xbc{l}.{n}")
            for n in range(len(CHUNKS)):
                plan(f"tok{l}.{n}")
            plan(f"ukv{l}")
            plan(f"uq{l}")
            for n in range(4):
                plan(f"wo{l}.{n}")
            if l == 0:
                for n in range(MOD_LOADS):
                    if n < GU_LOADS:
                        plan(f"gu.{n}")
                    plan(f"mod1.{n}")
                for n in range(DN_LOADS):
                    plan(f"dn.{n}")
            else:
                for n in range(NE * ME_LOADS):
                    plan(f"me.{n}")
        XL = [(0, 1), (2, 3), (4, 5), (6,)]

        def load_size(k):
            k %= ME_LOADS
            if k < ME_GU:
                return SLOT
            _, nf, _, nj = DN_PARTS[k - ME_GU]
            return nf * nj * P

        def part_of(q):
            if q < GU_PARTS:
                per = SLOT // PART
                return load_of["gu.0"] + 2 * (q // per), q % per * PART, PART
            n, d = divmod(q - GU_PARTS, len(DN_TILES))
            f, nf = DN_TILES[d]
            return load_of["dn.0"] + n, f * P, nf * P

        def me_slot(k):
            q = k % ME_R
            return wslot(load_of["me.0"] + q) if q < R else me_ring[:, (q - R) * SLOT:(q - R + 1) * SLOT]

        me_full = [sem(f"me_full{q}") for q in range(ME_R)]
        w_full = [sem(f"w_full{s}") for s in range(R)]
        w_begun = sem("w_begun")

        def w_wait(pe, n):
            pe.wait_ge(w_full[n % R], 16 * (n // R + 1))

        B = []
        for b in range(8):
            tile = ctx.enter_context(nc.psum_tensor(f"bank{b}", [P, 512], F32))
            B.append(Bank(tile, sem(f"bank{b}_full"), sem(f"bank{b}_free")))
        use = {}

        def uses(b, name, reads=1, fulls=1):
            B[b].add(name, reads, fulls)
            use[name] = B[b]

        for n in range(MOD_LOADS):
            uses(n % R, f"mrow0.{n}")
        uses(7, "mod0")
        tiles = [range(T0[l], NT) for l in range(L)]
        for l in range(L):
            T = tiles[l]
            both = 2 if l == 0 else 1
            uses(0 if l else 3, f"norm{2 * l}", fulls=0)
            for c in range(KX):
                uses(1 + c % 2, f"xbc{l}.{c}")
            for q in range(len(CHUNKS)):
                for i in (range(NT) if q < CTX_CHUNKS else T):
                    uses(3 + i, f"tok{l}.{q}.{i}")
            for i in range(NT):
                uses(1, f"xsT{l}.{i}")
                uses(2, f"BT{l}.{i}")
            uses(7, f"acs{l}")
            uses(3, f"rows{l}.0")
            uses(4, f"rows{l}.1")
            uses(5, f"cb{l}.0", 2)
            uses(6, f"cb{l}.1", 2)
            for r in range(2):
                for i in range(3):
                    uses(7 if r == 0 else 0, f"st{l}.{r}.{i}")
            for k in range(12):
                uses(1 + k % 2, f"bc{l}.{k}")
            for i in T:
                uses(3 + i, f"y{l}.{i}")
            for i in T:
                for r in range(2):
                    if CHAIN[r].index(i):
                        uses(1 + r, f"off{l}.{i}.{r}")
            for c in range(3):
                uses(c, f"qlT{l}.{c}")
            for c in range(2):
                uses(3 + c, f"kvT{l}.{c}")
            for h in range(MLA_H):
                uses(5 + h % 2, f"kn{l}.{h}")
            for i in range(NT):
                uses(1 + i % 2, f"v{l}.{i}")
            uses(3, f"kr{l}")
            for i in T:
                for hh in range(2):
                    uses(4 + hh, f"q{l}.{i}.{hh}")
                for hh in range(2):
                    uses(6 + hh, f"qT{l}.{i}.{hh}")
            for i in T:
                for h in range(MLA_H):
                    uses(h % 2, f"s{l}.{i}.{h}")
                    uses(2 + h % 2, f"pT{l}.{i}.{h}")
                uses(4 + i % 2, f"o{l}.{i}")
            for i in T:
                uses(6 + i % 2, f"sgu{l}.{i}", SGU_H)
            for i in T:
                uses(0, f"oT{l}.{i}.0", 2)
                uses(1, f"oT{l}.{i}.1", 3)
            for j in range(KD):
                uses(2 + j % 2, f"wo{l}.{j}", both)
            uses(0, f"norm{2 * l + 1}", fulls=0)
            if l == 0:
                for i in range(KF):
                    uses(i % 3, f"gate.{i}")
                    uses(3 + i % 3, f"up.{i}", 0)
                for n in range(MOD_LOADS):
                    uses(6, f"mrow1.{n}")
                uses(7, "mod1")
                for j in range(KD):
                    uses(6 + j % 2, f"dn.{j}", both)
            else:
                uses(0, "logits")
                for q in range(4):
                    uses(4 + q, f"htok.{q}")
                uses(1, "rank")
        uses(0, "norm4", fulls=0)

        def claim(pe, name):
            if use[name].before(name):
                pe.wait_ge(use[name].free, use[name].before(name))

        def full(eng, name):
            eng.wait_ge(use[name].full, use[name].filled(name))

        def taken(eng, name):
            eng.wait_ge(use[name].free, use[name].taken(name))

        s_par = sem("s_par")
        s_x = sem("s_x")
        s_out = sem("s_out")
        cond_ready = sem("cond_ready")
        ea_ready = sem("ea_ready")
        amod_ready = sem("amod_ready")
        sq_ready = sem("sq_ready")
        sq_used = sem("sq_used")
        ns_ready = sem("ns_ready")
        rstd_ready = sem("rstd_ready")
        tmp_ready = sem("tmp_ready")
        h_ready = sem("h_ready")
        pads_ready = sem("pads_ready")
        conv_done = sem("conv_done")
        xbc_ready = sem("xbc_ready")
        dt_a = sem("dt_a")
        dt_v = sem("dt_v")
        da_ready = sem("da_ready")
        dec_in = sem("dec_in")
        dec_ready = sem("dec_ready")
        xdt_ready = sem("xdt_ready")
        wx_ready = sem("wx_ready")
        seg_ready = sem("seg_ready")
        ex_ready = sem("ex_ready")
        m_ready = sem("m_ready")
        diag_done = sem("diag_done")
        yg_ready = sem("yg_ready")
        yss_ready = sem("yss_ready")
        gn_v = sem("gn_v")
        gn_s = sem("gn_s")
        ossd_ready = sem("ossd_ready")
        st_ready = sem("st_ready")
        sv_ready = sem("sv_ready")
        ss_ready = sem("ss_ready")
        qkn_ready = sem("qkn_ready")
        krp_ready = sem("krp_ready")
        qrope_ready = sem("qrope_ready")
        mx_ready = sem("mx_ready")
        pr_ready = sem("pr_ready")
        pv_done = sem("pv_done")
        vn_ready = sem("vn_ready")
        sg_ready = sem("sg_ready")
        act_ready = sem("act_ready")
        act_read = sem("act_read")
        top_v = sem("top_v")
        top_a = sem("top_a")
        zero_ready = sem("zero_ready")
        out_ready = sem("out_ready")
        hl_ready = sem("hl_ready")
        part_begun = sem("part_begun")
        part_hi = sem("part_hi")
        part_lo = sem("part_lo")
        dense_hi = sem("dense_hi")
        w_hi = sem("w_hi")
        w_lo = sem("w_lo")
        mask_ready = sem("mask_ready")
        flag_ready = sem("flag_ready")
        gather_ready = sem("gather_ready")
        weighted_ready = sem("weighted_ready")
        xe_full = sem("xe_full")
        xe_hi = sem("xe_hi")
        xe_lo = sem("xe_lo")
        gu_full = sem("gu_full")
        prod_ready = sem("prod_ready")
        t_full = sem("t_full")
        t_hi = sem("t_hi")
        t_lo = sem("t_lo")
        y_full = sem("y_full")
        y_taken = sem("y_taken")
        sum_full = sem("sum_full")
        added = sem("added")
        x_final = sem("x_final")
        dve_chain = sem("dve_chain")

        block = ctx.enter_context(nc.Block())

        @block.sync
        def _(sp):
            def load(name, src, n):
                i = load_of[name]
                if i >= R:
                    sp.wait_ge(w_begun, i - R + 2)
                sp.dma_start(wslot(i)[:, 0:n], src).then_inc(w_full[i % R], 16)

            sp.dma_start(condr[:, :], t["cond"]).then_inc(s_par, 16)
            sp.dma_start(const[:, :], t["const"]).then_inc(s_par, 16)
            sp.dma_start(colp[:, :], t["colp"]).then_inc(s_par, 16)
            sp.dma_start(rowp[:, :], t["rowp"].to_broadcast([P, L * N_ROW])).then_inc(s_par, 16)
            sp.dma_start(wsT[:, :], t["wsT"]).then_inc(s_par, 16)
            sp.dma_start(gfin[:, :], t["gfin"]).then_inc(s_par, 16)
            sp.dma_start(rtr[:, :], t["w_router"]).then_inc(s_par, 16)
            for n in range(R):
                load(f"mod0.{n}", t["w_mod"][n], SLOT)
            sp.dma_start(X[:, :], t["x"]).then_inc(s_x, 16)
            with sp.Fori(1, MOD_LOADS // R) as i:
                for k in range(R):
                    sp.wait_ge(B[k].full, i)
                    sp.dma_start(wslot(k), t["w_mod"][bass.ds(i * R + k, 1), :, :].rearrange("a p n -> p (a n)"))\
                      .then_inc(w_full[k], 16)
            for l in range(L):
                for n, cs in enumerate(XL):
                    load(f"xbc{l}.{n}", t["w_xbc"][l, n, :, 0:len(cs) * KD * P], len(cs) * KD * P)
                for q, (a, b) in enumerate(CHUNKS):
                    load(f"tok{l}.{q}", t["w_tok"][l, :, KD * a:KD * b], KD * (b - a))
                load(f"ukv{l}", t["w_ukv"][l], 2 * 768)
                load(f"uq{l}", t["w_uq"][l], 3 * 576)
                for n in range(4):
                    load(f"wo{l}.{n}", t["w_out"][l, n], SLOT)
                if l == 0:
                    n0 = load_of["gu.0"]
                    with sp.Fori(0, GU_LOADS // R) as i:
                        for k in range(R):
                            for src, first_row, m in ((t["w_gu"], 0, 2 * k), (t["w_mod"], MOD_LOADS, 2 * k + 1)):
                                sp.wait_ge(w_begun, i * (2 * R) + (n0 + m - R + 2))
                                sp.dma_start(wslot(n0 + m), src[bass.ds(i * R + (first_row + k), 1), :, :].rearrange("a p n -> p (a n)"))\
                                  .then_inc(w_full[(n0 + m) % R], 16)
                    for n in range(GU_LOADS - GU_LOADS % R, MOD_LOADS):
                        if n < GU_LOADS:
                            load(f"gu.{n}", t["w_gu"][n], SLOT)
                        load(f"mod1.{n}", t["w_mod"][MOD_LOADS + n], SLOT)
                    for n in range(DN_LOADS):
                        load(f"dn.{n}", t["w_dn"][n], KF // 2 * P)
                else:
                    n0 = load_of["me.0"]

                    def w_free(e, k):
                        if k >= ME_R or not isinstance(e, int):
                            sp.wait_ge(w_lo, e * ME_LOADS + (k - ME_R + 1))
                        elif k < R - 1:
                            sp.wait_ge(w_begun, n0 + k - R + 2)
                        elif k == R - 1:
                            taken(sp, f"wo{l}.{KD - 1}")

                    def expert(e, first=0):
                        for k in range(ME_GU):
                            w_free(e, k)
                            sp.dma_start(me_slot(k), t["w_egu"][bass.ds(e * KE + (k - first * KE), 1), :, :].rearrange("a p n -> p (a n)"))\
                              .then_inc(me_full[k % ME_R], 16)
                        for k, (f, nf, j, nj) in enumerate(DN_PARTS):
                            at = f * D + j * P
                            n = nf * nj * P
                            w_free(e, ME_GU + k)
                            sp.dma_start(me_slot(ME_GU + k)[:, 0:n],
                                         t["w_edn"][bass.ds(e - first if first else e, 1), :, at:at + n].rearrange("a p n -> p (a n)"))\
                              .then_inc(me_full[(ME_GU + k) % ME_R], 16)

                    expert(0)
                    with sp.Fori(1, NE) as e:
                        expert(e)
                    sp.wait_ge(flag_ready, 1)
                    with sp.If(sp.value_load(flag[0:1, 0:1], min_val=0, max_val=1)):
                        with sp.Fori(NE, 2 * NE) as e:
                            expert(e, NE)
            sp.wait_ge(out_ready, KD)
            sp.dma_start(t["out"], Xv[:, :, CTX:TOK]).then_inc(s_out, 16)
            sp.wait_ge(s_out, 16)

        @block.tensor
        def _(pe):
            def done(ins, name):
                ins.then_inc(use[name].full, 1)

            def mod_rows(bank, slot, w_value):
                pe.wait_ge(w_full[slot % R], w_value)
                for kk in range(KD):
                    g = 32 * (kk % 4)
                    ins = pe.matmul(bank.tile[g:g + 32, 0:2 * P], condp[:, kk * 32:(kk + 1) * 32],
                                    wslot(slot)[:, kk * 2 * P:(kk + 1) * 2 * P], start=(kk < 4), stop=(kk >= 4))
                    if kk == 0:
                        ins.then_inc(w_begun, 1)
                ins.then_inc(bank.full, 1)

            def mod_cols(bank, row_ready, row, out, at):
                pe.wait_ge(bank.free, row_ready)
                for c in range(2):
                    ins = pe.matmul(out[:, at + 2 * c:at + 2 * c + 2] if isinstance(at, int) else out[:, bass.ds(at + 2 * c, 2)],
                                    row[:, c * P:(c + 1) * P], fold, start=True, stop=True)
                return ins

            def modulation0():
                out = use["mod0"].tile

                def step(turn, k):
                    mod_rows(B[k], k, (turn + 1) * 16)
                    if k:
                        mod_cols(B[k - 1], turn + B[k - 1].taken(f"mrow0.{k - 1}"), mrow0[k - 1], out, turn * (4 * R) + 4 * (k - 1))
                    elif not isinstance(turn, int):
                        mod_cols(B[R - 1], turn + (B[R - 1].taken(f"mrow0.{R - 1}") - 1), mrow0[R - 1], out, turn * (4 * R) - 4)

                for k in range(R):
                    step(0, k)
                for begin, end in ((1, MOD_EARLY), (MOD_EARLY, MOD_LOADS // R)):
                    with pe.Fori(begin, end) as i:
                        for k in range(R):
                            step(i, k)
                    if begin == 1:
                        norm_sum(0, TOK)
                last = MOD_LOADS - 1
                done(mod_cols(B[R - 1], B[R - 1].taken(f"mrow0.{last}"), mrow0[R - 1], out, 4 * last), "mod0")

            def norm_sum(q, n):
                claim(pe, f"norm{q}")
                for c in range(KD):
                    pe.wait_ge(sq_ready, KD * q + c + 1)
                    pe.matmul(use[f"norm{q}"].tile[:, 0:n], ones, pair[:, (c % 2) * TOK:(c % 2) * TOK + n],
                              start=(c == 0), stop=(c == KD - 1)).then_inc(sq_used, 1)

            def in_proj(l):
                for n, cs in enumerate(XL):
                    w = load_of[f"xbc{l}.{n}"]
                    w_wait(pe, w)
                    for ci, c in enumerate(cs):
                        name = f"xbc{l}.{c}"
                        claim(pe, name)
                        for kk in range(KD):
                            if n == 0 and ci == 0:
                                pe.wait_ge(h_ready, KD * 2 * l + kk + 1)
                            ins = pe.matmul(use[name].tile[:, :], wslot(w)[:, (ci * KD + kk) * P:(ci * KD + kk + 1) * P],
                                            Hv[:, kk, :], start=(kk == 0), stop=(kk == KD - 1))
                            if ci == 0 and kk == 0:
                                ins.then_inc(w_begun, 1)
                        done(ins, name)
                for q, (a, b) in enumerate(CHUNKS):
                    w = load_of[f"tok{l}.{q}"]
                    w_wait(pe, w)
                    wv = wslot(w)[:, 0:KD * (b - a)].rearrange("p (k n) -> p k n", k=KD)
                    for i in (range(NT) if q < CTX_CHUNKS else tiles[l]):
                        name = f"tok{l}.{q}.{i}"
                        claim(pe, name)
                        for kk in range(KD):
                            ins = pe.matmul(use[name].tile[:, 0:b - a], Hv[:, kk, i * P:(i + 1) * P], wv[:, kk, :],
                                            start=(kk == 0), stop=(kk == KD - 1))
                            if kk == 0 and i == (0 if q < CTX_CHUNKS else T0[l]):
                                ins.then_inc(w_begun, 1)
                        done(ins, name)

            def ssd(l):
                T = tiles[l]
                t0 = T0[l]
                for i in range(NT):
                    claim(pe, f"xsT{l}.{i}")
                    if i == 0:
                        pe.wait_ge(xbc_ready, KX * (l + 1))
                    for c in range(3):
                        ins = pe.transpose(use[f"xsT{l}.{i}"].tile[:, c * P:(c + 1) * P], xbcT[:, c, i * P:(i + 1) * P], ident)
                    done(ins, f"xsT{l}.{i}")
                    claim(pe, f"BT{l}.{i}")
                    for c in range(2):
                        ins = pe.transpose(use[f"BT{l}.{i}"].tile[:, c * P:(c + 1) * P], xbcT[:, 3 + c, i * P:(i + 1) * P], ident)
                    done(ins, f"BT{l}.{i}")
                da = small[:, 0:48]
                claim(pe, f"acs{l}")
                pe.wait_ge(da_ready, l + 1)
                acs = use[f"acs{l}"].tile
                pe.matmul(acs[:, 0:24], upto, da[:, 0:24], start=True, stop=True)
                pe.matmul(acs[:, 24:48], down, da[:, 24:48], start=True, stop=True)
                done(pe.matmul(acs[:, 48:96], ones, da, start=True, stop=True), f"acs{l}")
                for r in range(2):
                    claim(pe, f"rows{l}.{r}")
                    for i in range(NT):
                        ins = pe.matmul(use[f"rows{l}.{r}"].tile[0:6, i * P:(i + 1) * P], da[:, r * 24 + i * 6:r * 24 + i * 6 + 6],
                                        upto if r == 0 else down, start=True, stop=True)
                    done(ins, f"rows{l}.{r}")
                for g in range(2):
                    claim(pe, f"cb{l}.{g}")
                    for i in T:
                        ins = pe.matmul(use[f"cb{l}.{g}"].tile[:, i * P:(i + 1) * P], xbcT[:, 3 + g, i * P:(i + 1) * P],
                                        xbcT[:, 5 + g, i * P:(i + 1) * P], start=True, stop=True)
                    done(ins, f"cb{l}.{g}")
                def state(i3):
                    for r in range(2):
                        i = CHAIN[r][i3]
                        name = f"st{l}.{r}.{i3}"
                        claim(pe, name)
                        if i3 == 0:
                            pe.wait_ge(wx_ready, 2 * l + r + 1)
                            taken(pe, f"BT{l}.{NT - 1}")
                        for g in range(2):
                            ins = pe.matmul(use[name].tile[:, g * 192:(g + 1) * 192], xsB[:, i, 384 + g * P:384 + (g + 1) * P],
                                            wx[:, r, i, g * 192:(g + 1) * 192], start=True, stop=True)
                        done(ins, name)

                def diag(k):
                    h, r = k // 2, k % 2
                    pe.wait_ge(m_ready, 12 * l + k + 1)
                    if k < 2:
                        pe.wait_ge(xdt_ready, 2 * l + r + 1)
                    for i in T:
                        if k == 0:
                            claim(pe, f"y{l}.{i}")
                        ins = pe.matmul(use[f"y{l}.{i}"].tile[:, h * 64:(h + 1) * 64], Mt[k % 2][:, i * P:(i + 1) * P],
                                        xdt[:, r, i, h * 64:(h + 1) * 64], start=(r == 0), stop=(r == 1))
                        if k == 11:
                            done(ins, f"y{l}.{i}")
                    if k < 11:
                        ins.then_inc(diag_done, 1)

                def rows(k):
                    h, r = k // 2, k % 2
                    name = f"bc{l}.{k}"
                    claim(pe, name)
                    if k < 2:
                        taken(pe, f"rows{l}.{r}")
                    done(pe.matmul(use[name].tile[:, t0 * P:TOK], sel[0:6, h * P:(h + 1) * P], acsT[0:6, r, t0 * P:TOK],
                                   start=True, stop=True), name)

                rows(0)
                rows(1)
                for k in range(12):
                    if k + 2 < 12:
                        rows(k + 2)
                    diag(k)
                    if k in (0, 3, 6):
                        state(k // 3)
                for i in T:
                    for r in range(2):
                        pos = CHAIN[r].index(i)
                        if pos == 0:
                            continue
                        name = f"off{l}.{i}.{r}"
                        claim(pe, name)
                        taken(pe, f"st{l}.{r}.2")
                        for g in range(2):
                            ins = pe.matmul(use[name].tile[:, g * 192:(g + 1) * 192], xbcT[:, 5 + g, i * P:(i + 1) * P],
                                            hin[:, r, pos - 1, g * 192:(g + 1) * 192], start=True, stop=True)
                        done(ins, name)

            def mla(l):
                T = tiles[l]
                pe.wait_ge(qkn_ready, l + 1)
                for c in range(3):
                    name = f"qlT{l}.{c}"
                    claim(pe, name)
                    for i in T:
                        ins = pe.transpose(use[name].tile[:, i * P:(i + 1) * P], pt[:, i, C_Q + c * P:C_Q + (c + 1) * P], ident)
                    done(ins, name)
                for c in range(2):
                    name = f"kvT{l}.{c}"
                    claim(pe, name)
                    for i in range(NT):
                        ins = pe.transpose(use[name].tile[:, i * P:(i + 1) * P], pt[:, i, C_KV + c * P:C_KV + (c + 1) * P], ident)
                    done(ins, name)
                w = load_of[f"ukv{l}"]
                w_wait(pe, w)
                ukv = wslot(w)[:, 0:2 * 768].rearrange("p (k n) -> p k n", k=2)
                for h in range(MLA_H):
                    name = f"kn{l}.{h}"
                    claim(pe, name)
                    for kk in range(2):
                        if h == 0:
                            taken(pe, f"kvT{l}.{kk}")
                        ins = pe.matmul(use[name].tile[0:NOPE, :], ukv[:, kk, h * NOPE:(h + 1) * NOPE], kvT[:, kk, :],
                                        start=(kk == 0), stop=(kk == 1))
                        if h == 0 and kk == 0:
                            ins.then_inc(w_begun, 1)
                    done(ins, name)
                for i in range(NT):
                    name = f"v{l}.{i}"
                    claim(pe, name)
                    for kk in range(2):
                        ins = pe.matmul(use[name].tile[:, 0:384], kvT[:, kk, i * P:(i + 1) * P], ukv[:, kk, 384:768],
                                        start=(kk == 0), stop=(kk == 1))
                    done(ins, name)
                name = f"kr{l}"
                claim(pe, name)
                pe.wait_ge(krp_ready, l + 1)
                for i in range(NT):
                    ins = pe.transpose(use[name].tile[0:QK, i * P:(i + 1) * P], krp[:, i, :], ident)
                done(ins, name)
                w = load_of[f"uq{l}"]
                w_wait(pe, w)
                uq = wslot(w)[:, 0:3 * 576].rearrange("p (k n) -> p k n", k=3)
                for c in range(3):
                    taken(pe, f"qlT{l}.{c}")

                def q_rows(i):
                    for hh in range(2):
                        name = f"q{l}.{i}.{hh}"
                        claim(pe, name)
                        for kk in range(3):
                            ins = pe.matmul(use[name].tile[:, 0:288], qlT[:, kk, i * P:(i + 1) * P],
                                            uq[:, kk, hh * 288:(hh + 1) * 288], start=(kk == 0), stop=(kk == 2))
                            if i == T0[l] and hh == 0 and kk == 0:
                                ins.then_inc(w_begun, 1)
                        done(ins, name)

                def q_cols(i):
                    taken(pe, f"q{l}.{i}.0")
                    taken(pe, f"q{l}.{i}.1")
                    if i >= 2:
                        pe.wait_ge(qrope_ready, 2 * l + i - 1)
                    for hh in range(2):
                        name = f"qT{l}.{i}.{hh}"
                        claim(pe, name)
                        for h in (range(0, 4) if hh == 0 else range(4, 6)):
                            ins = pe.transpose(use[name].tile[0:QK, (h % 4) * P:(h % 4 + 1) * P],
                                               qtk[i % 2][:, h * QK:(h + 1) * QK], ident)
                        done(ins, name)

                for i in T:
                    q_rows(i)
                    if i > T0[l]:
                        q_cols(i - 1)
                q_cols(NT - 1)
                units = [(i, h) for i in T for h in range(MLA_H)]

                def scores(i, h):
                    name = f"s{l}.{i}.{h}"
                    nk = 2 if i < 2 else NT
                    claim(pe, name)
                    if (i, h) == units[0]:
                        taken(pe, f"kr{l}")
                        for hh in range(MLA_H):
                            taken(pe, f"kn{l}.{hh}")
                        for ii in range(NT):
                            taken(pe, f"v{l}.{ii}")
                        for ii in T:
                            taken(pe, f"qT{l}.{ii}.0")
                            taken(pe, f"qT{l}.{ii}.1")
                    done(pe.matmul(use[name].tile[:, 0:nk * P], qT[0:QK, h, i * P:(i + 1) * P], kT[0:QK, h, 0:nk * P],
                                   start=True, stop=True), name)

                def weigh(u):
                    i, h = units[u]
                    nk = 2 if i < 2 else NT
                    taken(pe, f"pT{l}.{i}.{h}")
                    oname = f"o{l}.{i}"
                    if h == 0:
                        claim(pe, oname)
                    for k in range(nk):
                        ins = pe.matmul(use[oname].tile[:, h * 64:(h + 1) * 64], pT[u % 2][:, k * P:(k + 1) * P],
                                        vt[:, k, h * 64:(h + 1) * 64], start=(k == 0), stop=(k == nk - 1))
                    if h == MLA_H - 1:
                        done(ins, oname)
                    else:
                        ins.then_inc(pv_done, 1)

                scores(*units[0])
                scores(*units[1])
                for u, (i, h) in enumerate(units):
                    nk = 2 if i < 2 else NT
                    name = f"pT{l}.{i}.{h}"
                    claim(pe, name)
                    pe.wait_ge(pr_ready, 24 * l + u + 1)
                    for k in range(nk):
                        ins = pe.transpose(use[name].tile[:, k * P:(k + 1) * P], pr[u % 2][:, k * P:(k + 1) * P], ident)
                    done(ins, name)
                    if u + 2 < len(units):
                        scores(*units[u + 2])
                    if u:
                        weigh(u - 1)
                weigh(len(units) - 1)

            def sgu(l):
                pe.wait_ge(vn_ready, [4, 6][l])
                for i in tiles[l]:
                    name = f"sgu{l}.{i}"
                    claim(pe, name)
                    for h in range(SGU_H):
                        ins = pe.matmul(use[name].tile[:, h * 64:(h + 1) * 64], wsT[:, (l * SGU_H + h) * P:(l * SGU_H + h + 1) * P],
                                        pt[:, i, C_V + h * 64:C_V + (h + 1) * 64], start=True, stop=True)
                    done(ins, name)

            def out_proj(l):
                T = tiles[l]
                t0 = T0[l]
                pe.wait_ge(ossd_ready, l + 1)
                for i in T:
                    taken(pe, f"o{l}.{i}")
                    taken(pe, f"sgu{l}.{i}")
                    for b in range(2):
                        name = f"oT{l}.{i}.{b}"
                        claim(pe, name)
                        for c in range(4):
                            a = C_Q + (4 * b + c) * P
                            ins = pe.transpose(use[name].tile[:, c * P:(c + 1) * P], pt[:, i, a:a + P], ident)
                        done(ins, name)
                for i in T:
                    for b in range(2):
                        taken(pe, f"oT{l}.{i}.{b}")
                for n in range(4):
                    w = load_of[f"wo{l}.{n}"]
                    w_wait(pe, w)
                    for c in range(2):
                        name = f"wo{l}.{2 * n + c}"
                        claim(pe, name)
                        for kk in range(KD):
                            ins = pe.matmul(use[name].tile[:, t0 * P:TOK], wslot(w)[:, (c * KD + kk) * P:(c * KD + kk + 1) * P],
                                            Hv[:, kk, t0 * P:TOK], start=(kk == 0), stop=(kk == KD - 1))
                            if c == 0 and kk == 0:
                                ins.then_inc(w_begun, 1)
                        done(ins, name)

            def ffn():
                n0 = load_of["gu.0"]
                for kk in range(KD):
                    pe.wait_ge(hl_ready, kk + 1)
                gb = [B[b].before(f"gate.{b}") for b in range(3)]

                def split_part(q, turn, out, right, nt, first, last, load_first):
                    pe.wait_ge(part_lo, turn + (q + 1))
                    for f in range(nt):
                        a = (q % W_PARTS) * PART + f * P
                        hi, lo = (w[:, a:a + P] for w in ff_w)
                        ins = pe.matmul(out, hi, right(0, f), start=first and f == 0, stop=False)
                        if load_first and f == 0:
                            ins.then_inc(w_begun, 1)
                        ins = pe.matmul(out, lo, right(0, f), start=False, stop=False)
                        if f == 0:
                            ins.then_inc(part_begun, 1)
                        ins = pe.matmul(out, hi, right(1, f), start=False, stop=last and f == nt - 1)
                    return ins

                def hidden(k, turn, gate_free, up_read):
                    for half in range(2):
                        if half == 0:
                            pe.wait_ge(B[k].free, gate_free)
                        elif up_read is None:
                            claim(pe, f"up.{k}")
                        else:
                            pe.wait_ge(act_ready, up_read)
                        for d in range(2):
                            ins = split_part(4 * k + 2 * half + d, turn, B[3 * half + k].tile[:, :],
                                             lambda part, f: ff_h[part][:, 4 * d + f, :], 4, d == 0, d == 1, half == 0 and d == 0)
                        ins.then_inc(B[3 * half + k].full, 1)

                mrow_taken = B[6].taken("mrow1.0")
                out = use["mod1"].tile
                claim(pe, "mrow1.0")
                claim(pe, "mod1")

                def value(m):
                    return 16 * ((n0 + m) // R + 1)

                for k in range(R):
                    hidden(k, 0, gb[k], None)
                    if k:
                        mod_cols(B[6], mrow_taken + k - 1, mrow[k - 1], out, 4 * (k - 1))
                    mod_rows(B[6], n0 + 2 * k + 1, value(2 * k + 1))
                with pe.Fori(1, KF // R) as i:
                    for k in range(R):
                        hidden(k, i * (4 * R), i + gb[k], i * R + (k - 2))
                        mod_cols(B[6], i * R + (mrow_taken + k - 1), mrow[(k - 1) % R], out, i * (4 * R) + 4 * (k - 1))
                        mod_rows(B[6], n0 + 2 * k + 1, (i * 2 + ((n0 + 2 * k + 1) // R + 1)) * 16)
                for n in range(KF - KF % R, MOD_LOADS):
                    if n < KF:
                        hidden(n % R, n // R * (4 * R), gb[n % R] + n // R, n - 2)
                    mod_cols(B[6], mrow_taken + n - 1, mrow[(n - 1) % R], out, 4 * (n - 1))
                    m = load_of[f"mod1.{n}"]
                    mod_rows(B[6], m, 16 * (m // R + 1))
                n = MOD_LOADS - 1
                done(mod_cols(B[6], mrow_taken + n, mrow[n % R], out, 4 * n), "mod1")
                pe.wait_ge(act_ready, KF)
                for j in range(KD):
                    name = f"dn.{j}"
                    claim(pe, name)
                    for half in range(2):
                        for d, (f0, nf) in enumerate(DN_TILES):
                            base = (half * (KF // 2) + f0) * TOK
                            ins = split_part(GU_PARTS + (2 * j + half) * len(DN_TILES) + d, 0, use[name].tile[:, :],
                                             lambda part, f: ff_act[part][:, base + f * TOK:base + (f + 1) * TOK], nf,
                                             half == 0 and d == 0, half == 1 and d == len(DN_TILES) - 1, d == 0)
                    done(ins, name)

            def moe():
                for kk in range(KD):
                    pe.wait_ge(h_ready, 3 * KD + kk + 1)
                claim(pe, "logits")
                for i in range(2):
                    for kk in range(KD):
                        ins = pe.matmul(use["logits"].tile[:, i * NE:(i + 1) * NE], me_h[:, kk, i * P:(i + 1) * P],
                                        rtr[:, kk * NE:(kk + 1) * NE], start=(kk == 0), stop=(kk == KD - 1))
                done(ins, "logits")
                for q in range(4):
                    claim(pe, f"htok.{q}")
                    for c in range(4):
                        ins = pe.transpose(use[f"htok.{q}"].tile[:, c * P:(c + 1) * P],
                                           me_h[:, q % 2 * 4 + c, q // 2 * P:(q // 2 + 1) * P], ident)
                    done(ins, f"htok.{q}")
                claim(pe, "rank")
                rank = use["rank"].tile
                pe.wait_ge(mask_ready, 1)
                m = [lg[:, 192 + i * NE:192 + (i + 1) * NE] for i in range(2)]
                pe.matmul(rank[:, 0:NE], upto, m[0], start=True, stop=True)
                pe.matmul(rank[:, NE:2 * NE], upto, m[1], start=True, stop=False)
                pe.matmul(rank[:, NE:2 * NE], ones, m[0], start=False, stop=True)
                pe.matmul(rank[:, 2 * NE:3 * NE], ones, m[0], start=True, stop=False)
                pe.matmul(rank[:, 2 * NE:3 * NE], ones, m[1], start=False, stop=True)
                done(pe.matmul(rank[:, P:2 * P], ones, upto, start=True, stop=True), "rank")
                for q in range(4):
                    taken(pe, f"htok.{q}")
                experts(0)
                pe.wait_ge(flag_ready, 1)
                with pe.If(pe.value_load(flag[0:1, 0:1], min_val=0, max_val=1)):
                    experts(NE)

            def split_product(out, w, right, first, last):
                ins0 = pe.matmul(out, w[0], right[0], start=first, stop=False)
                pe.matmul(out, w[1], right[0], start=False, stop=False)
                return ins0, pe.matmul(out, w[0], right[1], start=False, stop=last)

            def experts(e0):
                p = e0 // NE
                y0 = 4 * (p + 1)

                def fetch(e, half):
                    for c in range(4):
                        for i in range(2):
                            d = 4 * half + c
                            at = (e - e0) * P if isinstance(e, int) else e * P - e0 * P if e0 else e * P
                            ins = pe.matmul(B[5].tile[:, c * P:(c + 1) * P], htok[:, 4 * i + d // 2, d % 2 * P:(d % 2 + 1) * P],
                                            gather[i][:, bass.ds(at, P)], start=(i == 0), stop=(i == 1))
                    ins.then_inc(xe_full, 1)

                def turn(e, i):
                    pe.wait_ge(prod_ready, e * KE + (i + 1))
                    if i >= 2:
                        pe.wait_ge(t_lo, e * KE + (i - 1))
                    pe.transpose(B[3 + i % 2].tile[:, 0:P], me_prod[i % 3], ident).then_inc(t_full, 1)

                def expert(e, last):
                    pe.wait_ge(xe_lo, e * 2 + 2)
                    for i in range(KE):
                        pe.wait_ge(w_lo, e * ME_LOADS + (i + 1))
                        if i >= 3:
                            pe.wait_ge(prod_ready, e * KE + (i - 2))
                        a = (i % W_SPLIT) * SLOT
                        wv = [w[:, a:a + SLOT].rearrange("p (h k n) -> p h k n", h=2, k=KD) for w in me_w]
                        for kk in range(KD):
                            ins0, ins = split_product(B[i % 3].tile[:, 0:2 * P].rearrange("p (h n) -> p h n", h=2),
                                                      [x[:, kk * P:(kk + 1) * P] for x in me_xe], [w[:, :, kk, :] for w in wv],
                                                      kk == 0, kk == KD - 1)
                            if kk == 0:
                                ins0.then_inc(w_begun, 1)
                        ins.then_inc(gu_full, 1)
                        if i:
                            turn(e, i - 1)
                    if not last:
                        fetch(e + 1, 0)
                    turn(e, KE - 1)
                    for k, (f0, nf, j0, nj) in enumerate(DN_PARTS):
                        pe.wait_ge(w_lo, e * ME_LOADS + (ME_GU + k + 1))
                        pe.wait_ge(t_lo, e * KE + (f0 + nf))
                        for f in range(nf):
                            for h in range(nj * P // 512):
                                half = j0 * P // 512 + h
                                if f0 + f == DN_FIRST[half]:
                                    pe.wait_ge(y_taken, e * 2 + (y0 - 1 + half))
                                a = ((ME_GU + k) % W_SPLIT) * SLOT + f * nj * P + h * 512
                                ins0, ins = split_product(B[6 + half].tile[:, :], [x[:, (f0 + f) * P:(f0 + f + 1) * P] for x in me_act],
                                                          [w[:, a:a + 512] for w in me_w], f0 + f == DN_FIRST[half],
                                                          f0 + f == DN_LAST[half])
                                if f == 0 and h == 0:
                                    ins0.then_inc(w_begun, 1)
                                if f0 + f == DN_LAST[half]:
                                    ins.then_inc(y_full, 1)
                        if k == 1 and not last:
                            pe.wait_ge(xe_lo, e * 2 + 3)
                            fetch(e + 1, 1)

                pe.wait_ge(gather_ready, p + 1)
                fetch(e0, 0)
                pe.wait_ge(xe_lo, 2 * e0 + 1)
                fetch(e0, 1)
                pe.wait_ge(weighted_ready, p + 1)
                for q in range(4):
                    if q >= 2:
                        pe.wait_ge(y_taken, 2 * e0 + 4 * p + q - 1)
                    for r in range(4):
                        e, i = 2 * q + r // 2, r % 2
                        ins = pe.transpose(B[6 + q % 2].tile[:, r * P:(r + 1) * P],
                                           weighted[:, (i * NE + e) * P:(i * NE + e + 1) * P], ident)
                    ins.then_inc(y_full, 1)
                with pe.Fori(e0, e0 + NE - 1) as e:
                    expert(e, False)
                expert(e0 + NE - 1, True)
                pe.wait_ge(y_taken, y0 + 2 * (e0 + NE))
                for j in range(KD):
                    for e in range(NE):
                        ins = pe.matmul(B[j // 2].tile[:, (j % 2) * SEQ:(j % 2 + 1) * SEQ], me_y[:, e * D + j * P:e * D + (j + 1) * P],
                                        scatter[:, e * SEQ:(e + 1) * SEQ], start=(e == 0), stop=(e == NE - 1))
                    if j % 2:
                        ins.then_inc(sum_full, 1)

            pe.wait_ge(cond_ready, 1)
            modulation0()
            for l in range(L):
                if l:
                    norm_sum(2 * l, TOK)
                in_proj(l)
                ssd(l)
                mla(l)
                sgu(l)
                out_proj(l)
                norm_sum(2 * l + 1, TOK - T0[l] * P)
                if l == 0:
                    ffn()
                else:
                    moe()
            norm_sum(4, SEQ)

        @block.scalar
        def _(ac):
            def take(name, out, in_, func=ACT.Copy, scale=1.0):
                ac.activation(out, in_, func, scale=scale).then_inc(use[name].free, 1)

            def norm(q, l, w, t0, x_ready, parts=None):
                n = TOK - t0 * P
                for c in range(KD):
                    x_ready(c)
                    if q or c >= 2:
                        ac.wait_ge(sq_used, KD * q + c - 1)
                    ac.activation(pair[:, (c % 2) * TOK:(c % 2) * TOK + n], Xv[:, c, t0 * P:TOK], ACT.Square).then_inc(sq_ready, 1)
                taken(ac, f"norm{q}")
                ac.activation(ns[:, 0:n], nv[:, 0:n], ACT.Sqrt).then_inc(ns_ready, 1)
                if w is None:
                    return
                ac.wait_ge(amod_ready, 2 * l + w + 1)
                for c in range(KD):
                    ac.wait_ge(tmp_ready, KD * q + c + 1)
                    for k in range(2):
                        a, b = k * CTX, (k + 1) * CTX
                        if a < t0 * P:
                            continue
                        for out in ([Hv[:, c, a:b]] if parts is None else [o[:, c, a - t0 * P:b - t0 * P] for o in parts]):
                            ins = ac.activation(out, pair2[:, (c % 2) * TOK + a - t0 * P:(c % 2) * TOK + b - t0 * P],
                                                ACT.Identity, bias=modv[:, l, 3 * w, c, k:k + 1], scale=amv[:, l, w, c, k:k + 1])
                    ins.then_inc(h_ready, 1)

            def in_proj(l):
                def silu(c):
                    ac.wait_ge(conv_done, KX * l + c + 1)
                    ac.activation(xbcT[:, c, :], cacc[c % 2], ACT.Silu, bias=col(l, "conv_b")[:, c:c + 1]).then_inc(xbc_ready, 1)

                for c in range(KX):
                    name = f"xbc{l}.{c}"
                    full(ac, name)
                    if c == 0:
                        ac.wait_ge(pads_ready, 2 * l + 2)
                    if c >= 2:
                        ac.wait_ge(conv_done, KX * l + c - 1)
                    take(name, xp[c % 2][:, :, 2:2 + CTX], use[name].tile[:, :].rearrange("p (s n) -> p s n", s=2))
                    if c >= 1:
                        silu(c - 1)
                silu(KX - 1)
                for q, (a, b) in enumerate(CHUNKS):
                    func = ACT.Gelu_apprx_tanh if a >= C_U else ACT.Silu if a >= C_Z else ACT.Copy
                    for i in (range(NT) if q < CTX_CHUNKS else tiles[l]):
                        name = f"tok{l}.{q}.{i}"
                        full(ac, name)
                        take(name, pt[:, i, a:b], use[name].tile[:, 0:b - a], func)
                    if q == 3:
                        ac.wait_ge(dt_v, l + 1)
                        ac.activation(small[:, 96:144], small[:, 144:192], ACT.Exp).then_inc(dt_a, 1)
                    if q == 4:
                        squares(l)
                    if q == 5:
                        ac.wait_ge(sv_ready, 2 * l + 1)
                        ac.activation(ssq[:, 0:8], sv[:, 0:8], ACT.Sqrt).then_inc(ss_ready, 1)

            def squares(l):
                T = tiles[l]
                parts = [(i, i, C_Q, Q_LORA) for i in T] + [(i, 4 + i, C_KV, KV_LORA) for i in range(NT)]
                for n, (i, to, a, w) in enumerate(parts):
                    if n:
                        ac.wait_ge(st_ready, [0, 8][l] + n)
                    ac.activation(pair[:, 0:w], pt[:, i, a:a + w], ACT.Square, accum_out=stats[:, to:to + 1]).then_inc(st_ready, 1)

            def ssd(l):
                T = tiles[l]
                t0 = T0[l]
                for i in range(NT):
                    full(ac, f"xsT{l}.{i}")
                    take(f"xsT{l}.{i}", xsB[:, i, 0:384], use[f"xsT{l}.{i}"].tile[:, 0:384])
                    full(ac, f"BT{l}.{i}")
                    take(f"BT{l}.{i}", xsB[:, i, 384:640], use[f"BT{l}.{i}"].tile[:, 0:256])
                for r in range(2):
                    full(ac, f"rows{l}.{r}")
                    take(f"rows{l}.{r}", acsT[0:6, r, :], use[f"rows{l}.{r}"].tile[0:6, :])
                ac.wait_ge(dec_in, l + 1)
                ac.activation(small[:, 432:576], small[:, 288:432], ACT.Exp).then_inc(dec_ready, 1)
                for k in range(12):
                    ac.wait_ge(seg_ready, 12 * l + k + 1)
                    if k >= 2:
                        ac.wait_ge(m_ready, 12 * l + k - 1)
                    ac.activation(Ex[k % 2][:, t0 * P:TOK], seg[k % 2][:, t0 * P:TOK], ACT.Exp).then_inc(ex_ready, 1)
                for n, i in enumerate(T):
                    ac.wait_ge(yg_ready, 4 * l + n + 1)
                    ac.activation(Mt[0][:, 0:384], pt[:, i, C_Z:C_Z + 384], ACT.Square, accum_out=sst[:, i:i + 1]).then_inc(yss_ready, 1)
                    if n + 1 < len(T):
                        ac.wait_ge(yss_ready, 4 * l + n + 1)
                ac.wait_ge(gn_v, l + 1)
                ac.activation(sst[:, 8 + t0:12], sst[:, 4 + t0:8], ACT.Sqrt).then_inc(gn_s, 1)

            def mla(l):
                T = tiles[l]
                a = T0[l] * P
                for c in range(3):
                    name = f"qlT{l}.{c}"
                    full(ac, name)
                    take(name, qlT[:, c, a:TOK], use[name].tile[:, a:TOK], scale=col(l, "g_q")[:, c:c + 1])
                for c in range(2):
                    name = f"kvT{l}.{c}"
                    full(ac, name)
                    take(name, kvT[:, c, :], use[name].tile[:, :], scale=col(l, "g_kv")[:, c:c + 1])
                ac.wait_ge(ossd_ready, l + 1)
                ac.wait_ge(sv_ready, 2 * l + 2)
                ac.activation(ssq[:, 8:12], sv[:, 8:12], ACT.Sqrt).then_inc(ss_ready, 1)
                for i in range(NT):
                    name = f"v{l}.{i}"
                    full(ac, name)
                    take(name, vt[:, i, :], use[name].tile[:, 0:384])
                name = f"kr{l}"
                full(ac, name)
                take(name, kT[NOPE:QK, :, :], use[name].tile[NOPE:QK, :].unsqueeze(1).to_broadcast([ROPE, MLA_H, TOK]))

                def q_cols(i):
                    for hh in range(2):
                        name = f"qT{l}.{i}.{hh}"
                        full(ac, name)
                        hs = slice(0, 4) if hh == 0 else slice(4, 6)
                        nh = 4 if hh == 0 else 2
                        take(name, qT[0:QK, hs, i * P:(i + 1) * P],
                             use[name].tile[0:QK, 0:nh * P].rearrange("p (h n) -> p h n", h=nh))

                for i in T:
                    for hh in range(2):
                        name = f"q{l}.{i}.{hh}"
                        full(ac, name)
                        if hh == 0 and i >= T0[l] + 2:
                            full(ac, f"qT{l}.{i - 2}.1")
                        take(name, qtk[i % 2][:, hh * 288:(hh + 1) * 288], use[name].tile[:, 0:288])
                    if i > T0[l]:
                        q_cols(i - 1)
                q_cols(NT - 1)
                units = [(i, h) for i in T for h in range(MLA_H)]
                for u, (i, h) in enumerate(units):
                    nk = 2 if i < 2 else NT
                    ac.wait_ge(mx_ready, 24 * l + u + 1)
                    if u >= 2:
                        full(ac, f"pT{l}.{units[u - 2][0]}.{units[u - 2][1]}")
                    name = f"s{l}.{i}.{h}"
                    ac.activation(pr[u % 2][:, 0:nk * P], use[name].tile[:, 0:nk * P], ACT.Exp, bias=mx[:, u % 2:u % 2 + 1],
                                  scale=SCALE, accum_out=rsum[:, i * MLA_H + h:i * MLA_H + h + 1]).then_inc(pr_ready, 1)

            def out_proj(l):
                g = col(l, "g_ssd")
                for i in tiles[l]:
                    a, b = i * P, (i + 1) * P
                    name = f"oT{l}.{i}.0"
                    full(ac, name)
                    tl = use[name].tile
                    take(name, Hv[:, 0:3, a:b], tl[:, 0:384].rearrange("p (c n) -> p c n", c=3))
                    take(name, Hv[:, 3, a:b], tl[:, 384:512], scale=g[:, 0:1])
                    name = f"oT{l}.{i}.1"
                    full(ac, name)
                    tl = use[name].tile
                    take(name, Hv[:, 4, a:b], tl[:, 0:128], scale=g[:, 1:2])
                    take(name, Hv[:, 5, a:b], tl[:, 128:256], scale=g[:, 2:3])
                    take(name, Hv[:, 6:8, a:b], tl[:, 256:512].rearrange("p (c n) -> p c n", c=2))

            def high_part(q, turn=0):
                n, at, size = part_of(q)
                if at == 0:
                    ac.wait_ge(w_full[n % R], (turn * 2 + (n // R + 1)) * 16)
                if q >= W_PARTS or not isinstance(turn, int):
                    ac.wait_ge(part_begun, turn * (4 * R) + (q - W_PARTS + 2))
                a = (q % W_PARTS) * PART
                ac.activation(ff_w[0][:, a:a + size], wslot(n)[:, at:at + size], ACT.Copy).then_inc(part_hi, 1)

            def ffn():
                gb = [B[b].filled(f"gate.{b}") for b in range(3)]

                def one(k, turn, used):
                    high_part(4 * k + 2, turn)
                    high_part(4 * k + 3, turn)
                    ac.wait_ge(B[k % 3].full, turn + (gb[k % 3] + k // 3))
                    if used is not None:
                        ac.wait_ge(act_ready, used)
                    ac.activation(sg[k % 3], B[k % 3].tile[:, :], ACT.Silu).then_inc(B[k % 3].free, 1)
                    high_part(4 * k + 4, turn)
                    high_part(4 * k + 5, turn)

                for k in range(3):
                    one(k, 0, None)
                with ac.Fori(1, KF // R) as i:
                    for k in range(3):
                        one(k, i, i * 3 + (k - 2))
                for f in range(KF - KF % R, KF):
                    one(f, 0, f - 2)
                for q in range(GU_PARTS + 2, GU_PARTS + DN_PART_N):
                    high_part(q)

            def high(e, k):
                ac.wait_ge(me_full[k % ME_R], (e * (ME_LOADS // ME_R) + (k // ME_R + 1)) * 16)
                ac.wait_ge(w_begun, e * ME_LOADS + (load_of["me.0"] + k - W_SPLIT + 2))
                size = load_size(k)
                a = (k % W_SPLIT) * SLOT
                ac.activation(me_w[0][:, a:a + size], me_slot(k)[:, 0:size], ACT.Copy).then_inc(w_hi, 1)

            def moe():
                for q in range(4):
                    full(ac, f"htok.{q}")
                    take(f"htok.{q}", htok[:, 2 * q:2 * q + 2, :], use[f"htok.{q}"].tile[:, :].rearrange("p (c n) -> p c n", c=2))
                ac.wait_ge(top_v, 1)
                ac.activation(lg[:, 32:34], lg[:, 24:26], ACT.Exp).then_inc(top_a, 1)
                experts(0)
                ac.wait_ge(flag_ready, 1)
                with ac.If(ac.value_load(flag[0:1, 0:1], min_val=0, max_val=1)):
                    ac.wait_ge(sum_full, 4)
                    for k in range(2):
                        high(NE, k)
                    experts(NE)

            def experts(e0):
                y0 = 4 * (e0 // NE + 1)

                def fetched(e, half):
                    ac.wait_ge(xe_full, e * 2 + (half + 1))
                    ac.activation(me_xe[0][:, half * 512:(half + 1) * 512], B[5].tile[:, :], ACT.Copy).then_inc(xe_hi, 1)

                def turned(e, i):
                    ac.wait_ge(t_full, e * KE + (i + 1))
                    ac.activation(me_act[0][:, i * P:(i + 1) * P], B[3 + i % 2].tile[:, 0:P], ACT.Copy).then_inc(t_hi, 1)

                def expert(e, last):
                    for k in range(ME_LOADS):
                        if k == KE:
                            if not last:
                                fetched(e + 1, 0)
                            turned(e, KE - 1)
                        if k + 2 < ME_LOADS or not last:
                            high(e, k + 2)
                        if k < KE:
                            ac.wait_ge(gu_full, e * KE + (k + 1))
                            if k >= 3:
                                ac.wait_ge(prod_ready, e * KE + (k - 2))
                            ac.activation(me_sg[k % 3], B[k % 3].tile[:, 0:P], ACT.Silu).then_inc(sg_ready, 1)
                            if k:
                                turned(e, k - 1)
                        if k == ME_GU + 1 and not last:
                            fetched(e + 1, 1)
                        if k >= ME_LOADS - 2:
                            half = k - (ME_LOADS - 2)
                            ac.wait_ge(y_full, e * 2 + (y0 + half + 1))
                            at = (e - e0) * D if isinstance(e, int) else e * D - e0 * D if e0 else e * D
                            ac.activation(me_y[:, bass.ds(at + half * 512, 512)], B[6 + half].tile[:, :], ACT.Copy).then_inc(y_taken, 1)

                fetched(e0, 0)
                fetched(e0, 1)
                for q in range(4):
                    ac.wait_ge(y_full, 2 * e0 + y0 - 4 + q + 1)
                    ac.activation(scatter[:, q * 512:(q + 1) * 512], B[6 + q % 2].tile[:, :], ACT.Copy).then_inc(y_taken, 1)
                with ac.Fori(e0, e0 + NE - 1) as e:
                    expert(e, False)
                expert(e0 + NE - 1, True)

            ac.wait_ge(s_par, 112)
            ac.wait_ge(zero_ready, 1)
            ac.activation(condp[:, :].rearrange("p (c k) -> p c k", c=KD)[:, :, 0:2], condr[:, :].rearrange("p (c k) -> p c k", c=KD),
                          ACT.Silu).then_inc(cond_ready, 1)
            for l in range(L):
                ac.activation(ea[:, l * 12:(l + 1) * 12], row(l, "a_log"), ACT.Exp).then_inc(ea_ready, 1)
            for l in range(L):
                def x_in(c):
                    if l == 0:
                        ac.wait_ge(s_x, 16)
                    else:
                        taken(ac, f"dn.{c}")

                norm(2 * l, l, 0, 0, x_in)
                in_proj(l)
                ssd(l)
                mla(l)
                out_proj(l)
                taken(ac, f"wo{l}.{KD - 1}")
                for k in range(2):
                    if l == 0:
                        high_part(k)
                    else:
                        high(0, k)
                norm(2 * l + 1, l, 1, T0[l], lambda c: taken(ac, f"wo{l}.{c}"), (me_h,) if l else (ff_raw, ff_h[0]))
                if l == 0:
                    ffn()
                else:
                    moe()
            norm(4, 1, None, 2, lambda c: ac.wait_ge(x_final, 1))

        @block.vector
        def _(ve):
            links = [0]

            def link(ins):
                links[0] += 1
                ins.then_inc(dve_chain, 1)
                ve.wait_ge(dve_chain, links[0])

            def norm_root(q, t0):
                n = TOK - t0 * P
                ve.wait_ge(sq_used, KD * (q + 1))
                ve.tensor_scalar(nv[:, 0:n], use[f"norm{q}"].tile[:, 0:n], 1.0 / D, EPS, ALU.mult, ALU.add)\
                  .then_inc(use[f"norm{q}"].free, 1)
                ve.wait_ge(ns_ready, q + 1)
                link(ve.reciprocal(rstd[:, 0:n], ns[:, 0:n]))

            def norm(q, t0, tail=None, parts=None):
                n = TOK - t0 * P
                if q:
                    norm_root(q, t0)
                if tail:
                    tail()
                    return
                for c in range(KD):
                    if q or c >= 2:
                        ve.wait_ge(h_ready, KD * q + c - 1)
                    ve.tensor_tensor(pair2[:, (c % 2) * TOK:(c % 2) * TOK + n], Xv[:, c, t0 * P:TOK], rstd[:, 0:n], ALU.mult)\
                      .then_inc(tmp_ready, 1)
                    if parts and c >= 2:
                        low_h(q, c - 2, parts)
                if parts:
                    low_h(q, KD - 2, parts)
                    low_h(q, KD - 1, parts)

            def low_h(q, c, parts):
                raw, hi, lo = parts
                ve.wait_ge(h_ready, KD * q + c + 1)
                ve.tensor_tensor(lo[:, c, :], raw[:, c, :], hi[:, c, :].bitcast(F32), ALU.subtract).then_inc(hl_ready, 1)

            def mod_row(bank, filled, out):
                ve.wait_ge(bank.full, filled)
                ve.tensor_copy(out, bank.tile[:, 0:2 * P]).then_inc(bank.free, 1)

            def modulation(l):
                name = f"mod{l}"
                full(ve, name)
                ve.tensor_tensor(modv[:, l].rearrange("p m c k -> p (m c) k"),
                                 use[name].tile[:, 0:2 * MOD_TILES].rearrange("p (j k) -> p j k", k=2),
                                 col(l, "b_mod").unsqueeze(2).to_broadcast([P, MOD_TILES, 2]), ALU.add).then_inc(use[name].free, 1)
                taken(ve, name)
                for w, g in enumerate(("g_mix", "g_ffn")):
                    ve.scalar_tensor_tensor(amv[:, l, w], modv[:, l, 3 * w + 1], 1.0,
                                            col(l, g).unsqueeze(2).to_broadcast([P, KD, 2]), ALU.add, ALU.mult)\
                      .then_inc(amod_ready, 1)

            def conv(l):
                w = col(l, "conv_w")
                for c in range(KX):
                    taken(ve, f"xbc{l}.{c}")
                    if l or c >= 2:
                        ve.wait_ge(xbc_ready, KX * l + c - 1)
                    x = xp[c % 2]
                    y = cacc[c % 2].rearrange("p (s n) -> p s n", s=2)
                    link(ve.tensor_scalar(y, x[:, :, 0:CTX], w[:, c * TAPS:c * TAPS + 1], None, ALU.mult))
                    for k in range(1, TAPS):
                        ins = ve.scalar_tensor_tensor(y, x[:, :, k:k + CTX], w[:, c * TAPS + k:c * TAPS + k + 1], y, ALU.mult, ALU.add)
                        if k < TAPS - 1:
                            link(ins)
                    ins.then_inc(conv_done, 1)

            def bc6(ap):
                return ap.unsqueeze(2).to_broadcast([P, SSD_H, SSD_HD])

            def ssd(l):
                T = tiles[l]
                t0 = T0[l]
                s = small
                da, dt = s[:, 0:48], s[:, 48:96]
                for i in range(NT):
                    taken(ve, f"tok{l}.0.{i}")
                y = s[:, 192:240]
                link(ve.tensor_tensor(y.rearrange("p (r t j) -> p r t j", r=2, t=NT),
                                      pt[:, :, C_DT:C_DT + 12].rearrange("p t (r j) -> p r t j", r=2),
                                      row(l, "dt_bias").rearrange("p (r j) -> p r j", r=2).unsqueeze(2)
                                      .to_broadcast([P, 2, NT, SSD_H]), ALU.add))
                ve.scalar_tensor_tensor(s[:, 144:192], y, -1.0, y, ALU.mult, ALU.min).then_inc(dt_v, 1)
                ve.wait_ge(dt_v, l + 1)
                link(ve.tensor_scalar(dt, y, 0.0, None, ALU.max))
                ve.wait_ge(dt_a, l + 1)
                e, w2, ww, sr = s[:, 96:144], s[:, 240:288], s[:, 288:336], s[:, 336:384]
                link(ve.tensor_scalar(w2, e, 2.0, None, ALU.add))
                link(ve.reciprocal(w2, w2))
                link(ve.tensor_tensor(w2, w2, e, ALU.mult))
                link(ve.tensor_tensor(ww, w2, w2, ALU.mult))
                link(ve.tensor_scalar(sr, ww, 1.0 / 15, None, ALU.mult))
                for n in (13, 11, 9, 7, 5, 3):
                    link(ve.scalar_tensor_tensor(sr, sr, 1.0 / n, ww, ALU.add, ALU.mult))
                link(ve.scalar_tensor_tensor(sr, sr, 1.0, w2, ALU.add, ALU.mult))
                link(ve.scalar_tensor_tensor(dt, sr, 2.0, dt, ALU.mult, ALU.add))
                ve.wait_ge(ea_ready, l + 1)
                for r in range(2):
                    ins = ve.scalar_tensor_tensor(da[:, r * 24:(r + 1) * 24].rearrange("p (t j) -> p t j", t=NT),
                                                  dt[:, r * 24:(r + 1) * 24].rearrange("p (t j) -> p t j", t=NT), -1.0,
                                                  ea[:, l * 12 + r * 6:l * 12 + r * 6 + 6].unsqueeze(1).to_broadcast([P, NT, SSD_H]),
                                                  ALU.mult, ALU.mult)
                    if r == 0:
                        link(ins)
                ins.then_inc(da_ready, 1)
                ve.wait_ge(st_ready, [8, 14][l])
                ve.tensor_scalar(sv[:, t0:4], stats[:, t0:4], 1.0 / Q_LORA, EPS, ALU.mult, ALU.add)
                ve.tensor_scalar(sv[:, 4:8], stats[:, 4:8], 1.0 / KV_LORA, EPS, ALU.mult, ALU.add).then_inc(sv_ready, 1)
                ve.wait_ge(ss_ready, 2 * l + 1)
                link(ve.reciprocal(rs[:, 0:8], ssq[:, 0:8]))
                for i in T:
                    ins = ve.tensor_scalar(pt[:, i, C_Q:C_Q + 384], pt[:, i, C_Q:C_Q + 384], rs[:, i:i + 1], None, ALU.mult)
                for i in range(NT):
                    ins = ve.tensor_scalar(pt[:, i, C_KV:C_KV + 256], pt[:, i, C_KV:C_KV + 256], rs[:, 4 + i:5 + i], None, ALU.mult)
                ins.then_inc(qkn_ready, 1)
                taken(ve, f"xsT{l}.{NT - 1}")
                for r in range(2):
                    ve.tensor_tensor(xdt[:, r].rearrange("p t (j n) -> p t j n", j=SSD_H),
                                     xsB[:, :, 0:384].rearrange("p t (j n) -> p t j n", j=SSD_H),
                                     dt[:, r * 24:(r + 1) * 24].rearrange("p (t j) -> p t j", t=NT).unsqueeze(3)
                                     .to_broadcast([P, NT, SSD_H, SSD_HD]), ALU.mult).then_inc(xdt_ready, 1)
                name = f"acs{l}"
                full(ve, name)
                acs = acs_s[:, :]
                ve.tensor_copy(acs, use[name].tile[:, 0:96]).then_inc(use[name].free, 1)
                taken(ve, name)
                ve.tensor_tensor(s[:, 288:336], acs[:, 48:96], acs[:, 0:48], ALU.subtract)
                ve.tensor_copy(s[:, 336:432], acs[:, 0:96]).then_inc(dec_in, 1)
                for g in range(2):
                    name = f"cb{l}.{g}"
                    full(ve, name)
                    for r in range(2):
                        m = upto if r == 0 else down
                        n = NT - t0
                        ve.tensor_tensor(cbm[:, r, g, t0 * P:TOK].rearrange("p (t n) -> p t n", t=n),
                                         use[name].tile[:, t0 * P:TOK].rearrange("p (t n) -> p t n", t=n),
                                         m.unsqueeze(1).to_broadcast([P, n, P]), ALU.mult).then_inc(use[name].free, 1)

                def segs(k):
                    h, r = k // 2, k % 2
                    name = f"bc{l}.{k}"
                    full(ve, name)
                    if k >= 2:
                        ve.wait_ge(ex_ready, 12 * l + k - 1)
                    n = NT - t0
                    a = acs[:, r * 24 + h:r * 24 + 24:6][:, t0:NT].unsqueeze(2).to_broadcast([P, n, P])
                    sv_ = seg[k % 2][:, t0 * P:TOK].rearrange("p (t n) -> p t n", t=n)
                    ve.tensor_tensor(sv_, use[name].tile[:, t0 * P:TOK].rearrange("p (t n) -> p t n", t=n), a, ALU.min)\
                      .then_inc(use[name].free, 1)
                    taken(ve, name)
                    ve.tensor_tensor(sv_, sv_, a, ALU.subtract).then_inc(seg_ready, 1)

                def mm(k):
                    h, r = k // 2, k % 2
                    ve.wait_ge(ex_ready, 12 * l + k + 1)
                    if k == 0:
                        taken(ve, f"cb{l}.1")
                    if k >= 2:
                        ve.wait_ge(diag_done, 11 * l + k - 1)
                    ve.tensor_tensor(Mt[k % 2][:, t0 * P:TOK], Ex[k % 2][:, t0 * P:TOK], cbm[:, r, h // HPG, t0 * P:TOK], ALU.mult)\
                      .then_inc(m_ready, 1)

                dec = s[:, 432:576]

                def state(i3):
                    if i3 == 0:
                        ve.wait_ge(dec_ready, l + 1)
                    for r in range(2):
                        name = f"st{l}.{r}.{i3}"
                        full(ve, name)
                        if i3 == 0:
                            ve.tensor_copy(hin[:, r, 0], use[name].tile[:, 0:384]).then_inc(use[name].free, 1)
                        else:
                            i = CHAIN[r][i3]
                            cd = dec[:, 96 + r * 24 + i * 6:96 + r * 24 + i * 6 + 6]
                            link(ve.tensor_tensor(hin[:, r, i3].rearrange("p (j n) -> p j n", j=SSD_H),
                                                  hin[:, r, i3 - 1].rearrange("p (j n) -> p j n", j=SSD_H), bc6(cd), ALU.mult))
                            ve.tensor_tensor(hin[:, r, i3], hin[:, r, i3], use[name].tile[:, 0:384], ALU.add)\
                              .then_inc(use[name].free, 1)
                        taken(ve, name)

                for k in range(12):
                    segs(k)
                    if k >= 1:
                        mm(k - 1)
                    if k in (3, 6, 9):
                        state(k // 3 - 1)
                mm(11)
                for n, i in enumerate(T):
                    skip = row(l, "d_skip")
                    v6 = ysum.rearrange("p (j n) -> p j n", j=SSD_H)
                    t6 = ytmp.rearrange("p (j n) -> p j n", j=SSD_H)
                    link(ve.tensor_tensor(v6, xsB[:, i, 0:384].rearrange("p (j n) -> p j n", j=SSD_H), bc6(skip), ALU.mult))
                    name = f"y{l}.{i}"
                    full(ve, name)
                    ve.tensor_tensor(ysum, ysum, use[name].tile[:, 0:384], ALU.add).then_inc(use[name].free, 1)
                    taken(ve, name)
                    for r in range(2):
                        if CHAIN[r].index(i) == 0:
                            continue
                        name = f"off{l}.{i}.{r}"
                        full(ve, name)
                        ex = dec[:, 48 + r * 24 + i * 6:48 + r * 24 + i * 6 + 6]
                        ve.tensor_tensor(t6, use[name].tile[:, 0:384].rearrange("p (j n) -> p j n", j=SSD_H), bc6(ex), ALU.mult)\
                          .then_inc(use[name].free, 1)
                        taken(ve, name)
                        link(ve.tensor_tensor(ysum, ysum, ytmp, ALU.add))
                    taken(ve, f"tok{l}.5.{i}")
                    ve.tensor_tensor(pt[:, i, C_Z:C_Z + 384], ysum, pt[:, i, C_Z:C_Z + 384], ALU.mult).then_inc(yg_ready, 1)
                    ve.wait_ge(yg_ready, 4 * l + n + 1)
                ve.wait_ge(yss_ready, 4 * l + len(T))
                ve.tensor_scalar(sst[:, 4 + t0:8], sst[:, t0:4], 1.0 / SSD_W, EPS, ALU.mult, ALU.add).then_inc(gn_v, 1)
                ve.wait_ge(gn_s, l + 1)
                link(ve.reciprocal(sst[:, 12 + t0:16], sst[:, 8 + t0:12]))
                for n, i in enumerate(T):
                    ins = ve.tensor_scalar(pt[:, i, C_Z:C_Z + 384], pt[:, i, C_Z:C_Z + 384], sst[:, 12 + i:13 + i], None, ALU.mult)
                ins.then_inc(ossd_ready, 1)

            def mla(l):
                T = tiles[l]
                t0 = T0[l]
                taken(ve, f"tok{l}.7.{NT - 1}")
                for i in T:
                    link(ve.bn_stats(bn[:, i * 8:i * 8 + 6], pt[:, i, C_V:C_V + 256]))
                    link(ve.bn_aggr(bn[:, i * 8 + 6:i * 8 + 8], bn[:, i * 8:i * 8 + 6]))
                bv = bn[:, :].rearrange("p (t n) -> p t n", t=NT)
                ve.tensor_scalar(sv[:, 8 + t0:12], bv[:, t0:NT, 7], EPS, None, ALU.add).then_inc(sv_ready, 1)

                def rotate(src, dst, i, nh, width):
                    cs = const[:, rope0 + (i - 2) * 32:rope0 + (i - 1) * 32].rearrange("p (s a f) -> p s a f", s=2, a=2)
                    c = cs[:, 0].unsqueeze(1).to_broadcast([P, nh, 2, 8])
                    s = cs[:, 1].unsqueeze(1).to_broadcast([P, nh, 2, 8])
                    tm = [rtmp[:, k * 96:k * 96 + nh * 16].rearrange("p (h a f) -> p h a f", h=nh, a=2) for k in range(4)]
                    t1 = src.rearrange("p h (a m f) -> p h a m f", a=2, m=2)[:, :, :, 0, :]
                    t2 = src.rearrange("p h (a m f) -> p h a m f", a=2, m=2)[:, :, :, 1, :]
                    d1 = dst.rearrange("p h (a m f) -> p h a m f", a=2, m=2)[:, :, :, 0, :]
                    d2 = dst.rearrange("p h (a m f) -> p h a m f", a=2, m=2)[:, :, :, 1, :]
                    ve.tensor_tensor(tm[0], t1, c, ALU.mult)
                    ve.tensor_tensor(tm[1], t2, s, ALU.mult)
                    ve.tensor_tensor(tm[2], t1, s, ALU.mult)
                    link(ve.tensor_tensor(tm[3], t2, c, ALU.mult))
                    link(ve.tensor_tensor(d1, tm[0], tm[1], ALU.subtract))
                    return ve.tensor_tensor(d2, tm[2], tm[3], ALU.add)

                link(ve.memset(krp[:, :, 0:NOPE], 0.0))
                for i in range(2):
                    link(ve.tensor_copy(krp[:, i, NOPE:QK], pt[:, i, C_KR:C_KR + ROPE]))
                link(rotate(pt[:, 2, C_KR:C_KR + ROPE].unsqueeze(1), krp[:, 2, NOPE:QK].unsqueeze(1), 2, 1, ROPE))
                rotate(pt[:, 3, C_KR:C_KR + ROPE].unsqueeze(1), krp[:, 3, NOPE:QK].unsqueeze(1), 3, 1, ROPE).then_inc(krp_ready, 1)
                for h in range(MLA_H):
                    name = f"kn{l}.{h}"
                    full(ve, name)
                    ve.tensor_copy(kT[0:NOPE, h, :], use[name].tile[0:NOPE, :]).then_inc(use[name].free, 1)
                for i in T:
                    taken(ve, f"q{l}.{i}.0")
                    taken(ve, f"q{l}.{i}.1")
                    if i >= 2:
                        if i == 2:
                            ve.wait_ge(krp_ready, l + 1)
                        else:
                            ve.wait_ge(qrope_ready, 2 * l + 1)
                        q = qtk[i % 2].rearrange("p (h n) -> p h n", h=MLA_H)[:, :, NOPE:QK]
                        rotate(q, q, i, MLA_H, QK).then_inc(qrope_ready, 1)
                ve.wait_ge(ss_ready, 2 * l + 2)
                link(ve.reciprocal(rs[:, 8:12], ssq[:, 8:12]))
                bn2 = bn[:, :].rearrange("p (t n) -> p t n", t=NT)
                for i in T:
                    v = pt[:, i, C_V:C_V + 256]
                    link(ve.tensor_scalar(v, v, bn2[:, i, 6:7], rs[:, 8 + i:9 + i], ALU.subtract, ALU.mult))
                    link(ve.tensor_tensor(v, v, row(l, "g_sgu"), ALU.mult))
                    ve.tensor_tensor(v, v, row(l, "beta_sgu"), ALU.add).then_inc(vn_ready, 1)
                units = [(i, h) for i in T for h in range(MLA_H)]

                def top(u):
                    i, h = units[u]
                    nk = 2 if i < 2 else NT
                    name = f"s{l}.{i}.{h}"
                    full(ve, name)
                    if u >= 2:
                        ve.wait_ge(pr_ready, 24 * l + u - 1)
                    ve.tensor_reduce(mx[:, 2 + u % 2:3 + u % 2], use[name].tile[:, 0:nk * P], AX.X, ALU.max)\
                      .then_inc(use[name].free, 1)
                    taken(ve, name)
                    ve.tensor_scalar(mx[:, u % 2:u % 2 + 1], mx[:, 2 + u % 2:3 + u % 2], -SCALE, None, ALU.mult).then_inc(mx_ready, 1)

                def divide(i):
                    name = f"o{l}.{i}"
                    a = i * MLA_H
                    link(ve.reciprocal(rinv[:, a:a + MLA_H], rsum[:, a:a + MLA_H]))
                    full(ve, name)
                    ve.tensor_tensor(pt[:, i, C_Q:C_Q + 384].rearrange("p (j n) -> p j n", j=MLA_H),
                                     use[name].tile[:, 0:384].rearrange("p (j n) -> p j n", j=MLA_H),
                                     bc6(rinv[:, a:a + MLA_H]), ALU.mult).then_inc(use[name].free, 1)

                top(0)
                top(1)
                for u, (i, h) in enumerate(units):
                    nk = 2 if i < 2 else NT
                    name = f"pT{l}.{i}.{h}"
                    full(ve, name)
                    if u >= 2:
                        if units[u - 2][1] == MLA_H - 1:
                            full(ve, f"o{l}.{units[u - 2][0]}")
                        else:
                            ve.wait_ge(pv_done, 20 * l + (u - 2) - (u - 2) // MLA_H + 1)
                    ve.tensor_copy(pT[u % 2][:, 0:nk * P], use[name].tile[:, 0:nk * P]).then_inc(use[name].free, 1)
                    if u + 2 < len(units):
                        top(u + 2)
                    if h == 0 and u:
                        divide(i - 1)
                divide(NT - 1)

            def sgu(l):
                for i in tiles[l]:
                    name = f"sgu{l}.{i}"
                    full(ve, name)
                    for h in range(SGU_H):
                        u = pt[:, i, C_U + h * 64:C_U + (h + 1) * 64]
                        ve.scalar_tensor_tensor(u, use[name].tile[:, h * 64:(h + 1) * 64], col(l, "b_sgu")[:, h:h + 1], u,
                                                ALU.add, ALU.mult).then_inc(use[name].free, 1)

            def residual(l, m, name, j, t0=None):
                full(ve, name)
                for k in range(2):
                    if k * CTX < T0[l] * P:
                        continue
                    ve.scalar_tensor_tensor(Xv[:, j, k * CTX:(k + 1) * CTX], use[name].tile[:, k * CTX:(k + 1) * CTX],
                                            modv[:, l, m, j, k:k + 1], Xv[:, j, k * CTX:(k + 1) * CTX], ALU.mult, ALU.add)\
                      .then_inc(use[name].free, 1)

            def low_part(q, turn=0):
                n, at, size = part_of(q)
                ve.wait_ge(part_hi, turn * (4 * R) + (q + 1))
                a = (q % W_PARTS) * PART
                ve.tensor_tensor(ff_w[1][:, a:a + size], wslot(n)[:, at:at + size], ff_w[0][:, a:a + size].bitcast(F32),
                                 ALU.subtract).then_inc(part_lo, 1)

            def ffn():
                gb = [B[b].taken(f"gate.{b}") for b in range(3)]
                ub = [B[3 + b].filled(f"up.{b}") for b in range(3)]

                mb = B[6].filled("mrow1.0")

                def one(k, turn):
                    for q in range(4 * k + 2, min(4 * k + 6, GU_PARTS)):
                        low_part(q, turn)
                    b = k % R
                    ve.wait_ge(B[b].free, turn + (gb[b] + k // R))
                    ve.wait_ge(B[3 + b].full, turn + (ub[b] + k // R))
                    if k or not isinstance(turn, int):
                        ve.wait_ge(act_ready, turn * R + k)
                    ve.tensor_tensor(prod, sg[b], B[3 + b].tile[:, :], ALU.mult)
                    hi, lo = (a[:, bass.ds(turn * (R * TOK) + k * TOK, TOK)] for a in ff_act)
                    ve.tensor_tensor(hi, sg[b], B[3 + b].tile[:, :], ALU.mult).then_inc(dense_hi, 1)
                    ve.wait_ge(dense_hi, turn * R + (k + 1))
                    ve.tensor_tensor(lo, prod, hi.bitcast(F32), ALU.subtract).then_inc(act_ready, 1)
                    mod_row(B[6], turn * R + (mb + k), mrow[b])

                for k in range(R):
                    one(k, 0)
                with ve.Fori(1, KF // R) as i:
                    for k in range(R):
                        one(k, i)
                for f in range(KF - KF % R, KF):
                    one(f, 0)
                for f in range(KF, MOD_LOADS):
                    mod_row(B[6], mb + f, mrow[f % R])
                for q in range(2):
                    low_part(GU_PARTS + q)
                modulation(1)
                per = 2 * len(DN_TILES)
                for j in range(KD):
                    for q in range(GU_PARTS + per * j + 2, GU_PARTS + min(per * (j + 1) + 2, DN_PART_N)):
                        low_part(q)
                    residual(0, 5, f"dn.{j}", j)

            def route():
                full(ve, "logits")
                v = [lg[:, 40 + 16 * k:56 + 16 * k].rearrange("p (t e) -> p t e", t=2) for k in range(9)]
                lo, eq, key, oh1, l2, oh2, ga, gb_, tm = v
                mask, rank = (lg[:, a:a + 16].rearrange("p (t e) -> p t e", t=2) for a in (192, 208))
                m1, m2, dd = lg[:, 0:2], lg[:, 8:10], lg[:, 24:26]
                kx = lg[:, 16:18]
                fb = first.unsqueeze(1).to_broadcast([P, 2, NE])

                def b8(a):
                    return a.unsqueeze(2).to_broadcast([P, 2, NE])

                ve.tensor_copy(lo, use["logits"].tile[:, 0:16].rearrange("p (t e) -> p t e", t=2)).then_inc(use["logits"].free, 1)
                taken(ve, "logits")

                def best(src, m, oh):
                    link(ve.tensor_reduce(m, src, AX.X, ALU.max))
                    link(ve.tensor_tensor(eq, src, b8(m), ALU.is_equal))
                    link(ve.tensor_tensor(key, eq, fb, ALU.mult))
                    link(ve.tensor_reduce(kx, key, AX.X, ALU.max))
                    link(ve.tensor_tensor(oh, key, b8(kx), ALU.is_equal))

                best(lo, m1, oh1)
                link(ve.scalar_tensor_tensor(l2, oh1, -3.0e38, lo, ALU.mult, ALU.add))
                best(l2, m2, oh2)
                ve.tensor_tensor(mask, oh1, oh2, ALU.add).then_inc(mask_ready, 1)
                ve.tensor_tensor(dd, m2, m1, ALU.subtract).then_inc(top_v, 1)
                ve.wait_ge(top_a, 1)
                ex, w1, w2 = lg[:, 32:34], lg[:, 4:6], lg[:, 12:14]
                link(ve.tensor_scalar(w2, ex, 1.0, None, ALU.add))
                link(ve.reciprocal(w1, w2))
                link(ve.tensor_tensor(w2, ex, w1, ALU.mult))
                link(ve.tensor_tensor(ga, oh1, b8(w1), ALU.mult))
                link(ve.tensor_tensor(gb_, oh2, b8(w2), ALU.mult))
                link(ve.tensor_tensor(ga, ga, gb_, ALU.add))
                full(ve, "rank")
                tl = use["rank"].tile
                ve.wait_ge(mask_ready, 1)
                ve.tensor_tensor(rank, tl[:, 0:2 * NE].rearrange("p (t e) -> p t e", t=2), mask, ALU.mult)
                ve.tensor_copy(lg[:, 256:384], tl[:, P:2 * P]).then_inc(use["rank"].free, 1)
                link(ve.tensor_reduce(lg[:, 224:225], tl[:, 2 * NE:3 * NE], AX.X, ALU.max))
                ve.tensor_scalar(flag[:, :], lg[:, 224:225], float(P), None, ALU.is_gt).then_inc(flag_ready, 1)
                slots(0)

            def slots(e0):
                rank, ga = (lg[:, a:a + 16].rearrange("p (t e) -> p t e", t=2) for a in (208, 136))
                if e0:
                    ve.tensor_scalar(rank, rank, -float(P), None, ALU.add).then_inc(mask_ready, 1)
                    ve.wait_ge(mask_ready, 2)
                gv = [a[:, :].rearrange("p (e n) -> p e n", e=NE) for a in gather]
                wv = weighted[:, :].rearrange("p (t e n) -> p t e n", t=2, e=NE)
                number = lg[:, 256:384].unsqueeze(1).to_broadcast([P, NE, P])
                for i in range(2):
                    ins = ve.tensor_tensor(gv[i], number, rank[:, i].unsqueeze(2).to_broadcast([P, NE, P]), ALU.is_equal)
                ins.then_inc(gather_ready, 1)
                ve.wait_ge(gather_ready, e0 // NE + 1)
                for i in range(2):
                    ins = ve.tensor_tensor(wv[:, i], gv[i], ga[:, i].unsqueeze(2).to_broadcast([P, NE, P]), ALU.mult)
                ins.then_inc(weighted_ready, 1)

            def low(e, k):
                ve.wait_ge(w_hi, e * ME_LOADS + (k + 1))
                size = load_size(k)
                a = (k % W_SPLIT) * SLOT
                ve.tensor_tensor(me_w[1][:, a:a + size], me_slot(k)[:, 0:size], me_w[0][:, a:a + size].bitcast(F32),
                                 ALU.subtract).then_inc(w_lo, 1)

            def moe():
                route()
                experts(0)
                ve.wait_ge(flag_ready, 1)
                with ve.If(ve.value_load(flag[0:1, 0:1], min_val=0, max_val=1)):
                    for k in range(2):
                        low(NE, k)
                    slots(NE)
                    experts(NE)
                ve.memset(lg[:, 225:226], 0.0).then_inc(x_final, 1)

            def experts(e0):
                def fetched(e, half):
                    ve.wait_ge(xe_hi, e * 2 + (half + 1))
                    hi, lo = (x[:, half * 512:(half + 1) * 512] for x in me_xe)
                    ve.tensor_tensor(lo, B[5].tile[:, :], hi.bitcast(F32), ALU.subtract).then_inc(xe_lo, 1)

                def turned(e, i):
                    ve.wait_ge(t_hi, e * KE + (i + 1))
                    hi, lo = (a[:, i * P:(i + 1) * P] for a in me_act)
                    ve.tensor_tensor(lo, B[3 + i % 2].tile[:, 0:P], hi.bitcast(F32), ALU.subtract).then_inc(t_lo, 1)

                def expert(e, last):
                    for k in range(ME_LOADS):
                        if k == KE:
                            if not last:
                                fetched(e + 1, 0)
                            turned(e, KE - 1)
                        if k + 2 < ME_LOADS or not last:
                            low(e, k + 2)
                        if k < KE:
                            b = k % 3
                            ve.wait_ge(sg_ready, e * KE + (k + 1))
                            if k >= 3:
                                ve.wait_ge(t_full, e * KE + (k - 2))
                            ve.tensor_tensor(me_prod[b], B[b].tile[:, P:2 * P], me_sg[b], ALU.mult).then_inc(prod_ready, 1)
                            if k:
                                turned(e, k - 1)
                        if k == ME_GU + 1 and not last:
                            fetched(e + 1, 1)

                fetched(e0, 0)
                fetched(e0, 1)
                with ve.Fori(e0, e0 + NE - 1) as e:
                    expert(e, False)
                expert(e0 + NE - 1, True)
                for j in range(KD):
                    ve.wait_ge(sum_full, 4 * (e0 // NE) + j // 2 + 1)
                    ve.scalar_tensor_tensor(Xv[:, j, CTX:TOK], B[j // 2].tile[:, (j % 2) * SEQ:(j % 2 + 1) * SEQ],
                                            modv[:, 1, 5, j, 1:2], Xv[:, j, CTX:TOK], ALU.mult, ALU.add).then_inc(added, 1)
                ve.wait_ge(added, e0 + NE)

            def final():
                for c in range(KD):
                    ve.scalar_tensor_tensor(Xv[:, c, CTX:TOK], Xv[:, c, CTX:TOK], gfin[:, c:c + 1], rstd[:, 0:SEQ],
                                            ALU.mult, ALU.mult).then_inc(out_ready, 1)

            ve.memset(condp[:, :], 0.0).then_inc(zero_ready, 1)
            ve.wait_ge(s_par, 112)
            ve.memset(sv[:, :], 1.0)
            ve.memset(sst[:, :], 1.0)
            ve.memset(stats[:, :], 1.0)
            for l in range(L):
                if l == 0:
                    for begin, end in ((0, MOD_EARLY), (MOD_EARLY, MOD_LOADS // R)):
                        with ve.Fori(begin, end) as i:
                            for k in range(R):
                                mod_row(B[k], i + B[k].filled(f"mrow0.{k}"), mrow0[k])
                        if begin == 0:
                            norm_root(0, 0)
                    modulation(0)
                    ve.wait_ge(s_x, 16)
                else:
                    for c in range(KD):
                        taken(ve, f"dn.{c}")
                norm(2 * l, 0)
                for x in xp:
                    ve.memset(x[:, :, 0:2], 0.0)
                    ve.memset(x[:, :, CTX + 2:CTX + 4], 0.0).then_inc(pads_ready, 1)
                conv(l)
                ssd(l)
                mla(l)
                sgu(l)
                for j in range(KD):
                    residual(l, 2, f"wo{l}.{j}", j)
                taken(ve, f"wo{l}.{KD - 1}")
                for k in range(2):
                    if l == 0:
                        low_part(k)
                    else:
                        low(0, k)
                norm(2 * l + 1, T0[l], parts=None if l else (ff_raw, *ff_h))
                if l == 0:
                    ffn()
                else:
                    moe()
            norm(4, 2, final)

        @block.gpsimd
        def _(po):
            for l in range(L):
                po.wait_ge(dec_ready, l + 1)
                for r in range(2):
                    po.wait_ge(xdt_ready, 2 * l + r + 1)
                    te = small[:, 432 + r * 24:432 + (r + 1) * 24].rearrange("p (t j) -> p t j", t=NT)
                    po.tensor_tensor(wx[:, r].rearrange("p t (j n) -> p t j n", j=SSD_H),
                                     xdt[:, r].rearrange("p t (j n) -> p t j n", j=SSD_H),
                                     te.unsqueeze(3).to_broadcast([P, NT, SSD_H, SSD_HD]), ALU.mult).then_inc(wx_ready, 1)


def small_params(v):
    def cols(a, n):
        return np.asarray(a).reshape(L, n, P).transpose(2, 0, 1)

    conv_w = np.asarray(v["conv_w"]).reshape(L, TAPS, KX, P).transpose(3, 0, 2, 1).reshape(P, L, KX * TAPS)
    b_sgu = np.asarray(v["b_sgu"]).transpose(2, 0, 1)
    col = np.concatenate([conv_w, cols(v["conv_b"], KX), cols(v["b_mod"], MOD_TILES), cols(v["g_mix"], KD), cols(v["g_ffn"], KD), b_sgu,
                          cols(v["g_ssd"], 3), cols(v["g_q"], 3), cols(v["g_kv"], 2)], axis=2)
    rows = np.concatenate([np.asarray(v[n]).reshape(L, -1) for n in ("dt_bias", "a_log", "d_skip", "g_sgu", "beta_sgu")], axis=1)
    return col.reshape(P, -1), rows.reshape(1, -1)


def tiles_of(w, k, per):
    lead = w.shape[:-2]
    n = w.shape[-1] // (per * P)
    a = w.reshape(*lead, k, P, n, per, P)
    m = len(lead)
    return a.transpose(*range(m), m + 2, m + 1, m + 3, m, m + 4).reshape(*lead, n, P, per * k * P)


def kernel(**inputs):
    import concourse.bacc as bacc
    from concourse.bass_utils import run_bass_kernel_spmd

    v = {k: np.asarray(a) for k, a in inputs.items()}
    s = IN_SGU
    z0, x0 = s, s + SSD_W
    dt0 = x0 + XBC
    q0 = dt0 + 12
    kv0 = q0 + Q_LORA
    kr0 = kv0 + KV_LORA
    w_in = v["w_in"]
    xbc = np.concatenate([w_in[:, :, x0:dt0], np.zeros((L, D, P), np.float32)], axis=2)
    tok = np.concatenate([w_in[:, :, dt0:q0], w_in[:, :, kr0:], w_in[:, :, kv0:kr0], w_in[:, :, q0:kv0], w_in[:, :, z0:x0],
                          w_in[:, :, 0:s]], axis=2).reshape(L, KD, P, C_END).transpose(0, 2, 1, 3)
    tok = np.concatenate([tok[..., a:b].reshape(L, P, -1) for a, b in CHUNKS], axis=2)
    ukv = v["w_ukv"].reshape(L, 2, P, MLA_H, 2, 64).transpose(0, 2, 1, 4, 3, 5).reshape(L, P, 2 * 768)
    uq = v["w_uq"].reshape(L, 3, P, 576).transpose(0, 2, 1, 3).reshape(L, P, 3 * 576)
    wo = v["w_out"]
    wo = np.concatenate([wo[:, SGU_W + SSD_W:], wo[:, SGU_W:SGU_W + SSD_W], wo[:, :SGU_W]], axis=1)
    gu = np.concatenate([tiles_of(v["w_gate"][0], KD, 1), tiles_of(v["w_up"][0], KD, 1)], axis=2)
    dn = v["w_down"][0].reshape(2, KF // 2, P, KD, P).transpose(3, 0, 2, 1, 4).reshape(DN_LOADS, P, -1)
    egu = np.concatenate([tiles_of(v["w_gate_e"][0], KD, 1), tiles_of(v["w_up_e"][0], KD, 1)], axis=3).reshape(NE * KE, P, SLOT)
    edn = v["w_down_e"][0].reshape(NE, KE, P, D).transpose(0, 2, 1, 3).reshape(NE, P, KE * D)
    x = np.concatenate([v["ctx"][0], v["x"][0]], axis=0).reshape(TOK, KD, P).transpose(2, 1, 0).reshape(P, -1)
    cond = np.stack([v["c_ctx"].reshape(KD, P), v["c"].reshape(KD, P)], axis=2).transpose(1, 0, 2).reshape(P, -1)
    colp, rowp = small_params(v)
    arrays = {
        "x": x, "cond": cond, "const": const_array(), "colp": colp, "rowp": rowp,
        "wsT": v["w_sgu"].transpose(3, 0, 1, 2).reshape(P, -1),
        "gfin": v["g_final"].reshape(KD, P).T,
        "w_router": v["w_router"][0].reshape(KD, P, NE).transpose(1, 0, 2).reshape(P, -1),
        "w_mod": v["w_mod"].reshape(L, KD, P, MOD_LOADS, 2 * P).transpose(0, 3, 2, 1, 4).reshape(L * MOD_LOADS, P, SLOT),
        "w_xbc": tiles_of(xbc, KD, 2), "w_tok": tok, "w_ukv": ukv, "w_uq": uq, "w_out": tiles_of(wo, KD, 2),
        "w_gu": gu, "w_dn": dn, "w_egu": egu, "w_edn": edn,
    }
    nc = bacc.Bacc("TRN2", target_bir_lowering=False, num_devices=1)
    t, feed = {}, {}
    for name, a in arrays.items():
        feed[f"in_{name}"] = np.ascontiguousarray(a)
        t[name] = nc.dram_tensor(f"in_{name}", a.shape, F32, kind="ExternalInput").ap()
    t["out"] = nc.dram_tensor("out", (P, KD, SEQ), F32, kind="ExternalOutput").ap()
    program(nc, t)
    r = run_bass_kernel_spmd(nc, [feed], core_ids=[0])
    return r.results[0]["out"].transpose(2, 1, 0).reshape(1, SEQ, D)
```
